# Optimizing a Trainium2 kernel written in Bass

```python
import math
import jax, jax.numpy as jnp
from jax import lax
import numpy as np

D_MODEL = 1024
BATCH = 1
SEQ = 256
DEPTH = 1
DEC_BATCH = 8
DEC_SEQ = 1
PAST_LEN = 2048
PAGE_SIZE = 128

N_META = 16
N_HEADS = 8
Q_RANK = 256
KV_RANK = 256
NOPE_DIM = 64
ROPE_DIM = 32
QK_DIM = NOPE_DIM + ROPE_DIM
V_DIM = D_MODEL // N_HEADS
ROPE_BASE = 10000.0
ATTN_SCALE = 1.0 / math.sqrt(QK_DIM)
POOL_WIDTH = D_MODEL // 2
POOL_WINDOWS = (2, 4, 8, 16)
N_POOL_GROUPS = len(POOL_WINDOWS)
POOL_GROUP = POOL_WIDTH // N_POOL_GROUPS
POOL_OUT_GROUP = D_MODEL // N_POOL_GROUPS
POOL_HIST = max(POOL_WINDOWS) - 1
N_EXPERTS = 32
TOP_K = 4
D_FF = D_MODEL
SWIGLU_LIMIT = 7.0
SWIGLU_ALPHA = 1.702
MOE_BLOCK = 128
Q_BLOCK = 128
EPS = 1e-6
IN_COLS = Q_RANK + KV_RANK + ROPE_DIM + POOL_WIDTH + 2 * D_MODEL

kernel_name = 'mla_pool_moe_hybrid_step'

def rmsnorm(x, g):
    xf = x.astype(jnp.float32)
    y = xf * lax.rsqrt(jnp.mean(xf * xf, axis=-1, keepdims=True) + EPS)
    return (y * g.astype(jnp.float32)).astype(x.dtype)

def rope(x, pos):
    half = ROPE_DIM // 2
    inv = ROPE_BASE ** (-jnp.arange(half, dtype=jnp.float32) / half)
    ang = pos.astype(jnp.float32)[:, None] * inv[None, :]
    shape = (1, ang.shape[0]) + (1,) * (x.ndim - 3) + (half,)
    cos = jnp.cos(ang).reshape(shape)
    sin = jnp.sin(ang).reshape(shape)
    xf = x.astype(jnp.float32)
    x1, x2 = xf[..., :half], xf[..., half:]
    return jnp.concatenate([x1 * cos - x2 * sin, x1 * sin + x2 * cos], axis=-1).astype(x.dtype)

def split_in(z):
    i0 = Q_RANK
    i1 = i0 + KV_RANK
    i2 = i1 + ROPE_DIM
    i3 = i2 + POOL_WIDTH
    i4 = i3 + D_MODEL
    return z[..., :i0], z[..., i0:i1], z[..., i1:i2], z[..., i2:i3], z[..., i3:i4], z[..., i4:]

def mla_attend_prompt(q_lat, q_rope, ckv, kr):
    B, L = q_lat.shape[0], q_lat.shape[1]
    n_blk = -(-L // Q_BLOCK)
    Lp = n_blk * Q_BLOCK
    pad = Lp - L
    q_lat = jnp.pad(q_lat, ((0, 0), (0, pad), (0, 0), (0, 0)))
    q_rope = jnp.pad(q_rope, ((0, 0), (0, pad), (0, 0), (0, 0)))
    ckv = jnp.pad(ckv, ((0, 0), (0, pad), (0, 0)))
    kr = jnp.pad(kr, ((0, 0), (0, pad), (0, 0)))
    qb = jnp.moveaxis(q_lat.reshape(B, n_blk, Q_BLOCK, N_HEADS, KV_RANK), 1, 0)
    rb = jnp.moveaxis(q_rope.reshape(B, n_blk, Q_BLOCK, N_HEADS, ROPE_DIM), 1, 0)
    kpos = jnp.arange(Lp)

    def block(args):
        ql, qr, i = args
        qpos = i * Q_BLOCK + jnp.arange(Q_BLOCK)
        s = (jnp.einsum('bqhc,bkc->bhqk', ql, ckv, preferred_element_type=jnp.float32)
             + jnp.einsum('bqhr,bkr->bhqk', qr, kr, preferred_element_type=jnp.float32)) * ATTN_SCALE
        s = jnp.where(kpos[None, None, None, :] <= qpos[None, None, :, None], s, -jnp.inf)
        p = jax.nn.softmax(s, axis=-1).astype(ckv.dtype)
        return jnp.einsum('bhqk,bkc->bqhc', p, ckv)

    o = lax.map(block, (qb, rb, jnp.arange(n_blk)))
    return jnp.moveaxis(o, 0, 1).reshape(B, Lp, N_HEADS, KV_RANK)[:, :L]

def mla_attend_sample(q_lat, q_rope, ckv_new, kr_new, ckv_past, kr_past):
    S = q_lat.shape[1]
    P = ckv_past.shape[1]
    s_past = (jnp.einsum('bqhc,bkc->bhqk', q_lat, ckv_past, preferred_element_type=jnp.float32)
              + jnp.einsum('bqhr,bkr->bhqk', q_rope, kr_past, preferred_element_type=jnp.float32))
    s_new = (jnp.einsum('bqhc,bkc->bhqk', q_lat, ckv_new, preferred_element_type=jnp.float32)
             + jnp.einsum('bqhr,bkr->bhqk', q_rope, kr_new, preferred_element_type=jnp.float32))
    causal = jnp.arange(S)[None, :] <= jnp.arange(S)[:, None]
    s_new = jnp.where(causal[None, None], s_new, -jnp.inf)
    s = jnp.concatenate([s_past, s_new], axis=-1) * ATTN_SCALE
    p = jax.nn.softmax(s, axis=-1).astype(ckv_new.dtype)
    return (jnp.einsum('bhqk,bkc->bqhc', p[..., :P], ckv_past)
            + jnp.einsum('bhqk,bkc->bqhc', p[..., P:], ckv_new))

def pool_mix(p_ext, pos, w_pool, pool_scale):
    B = p_ext.shape[0]
    L = p_ext.shape[1] - POOL_HIST
    pf = p_ext.astype(jnp.float32)
    cs = jnp.cumsum(pf, axis=1)
    cs = jnp.concatenate([jnp.zeros_like(cs[:, :1]), cs], axis=1)
    outs = []
    for g, w in enumerate(POOL_WINDOWS):
        lo, hi = g * POOL_GROUP, (g + 1) * POOL_GROUP
        s = cs[:, POOL_HIST + 1:POOL_HIST + 1 + L, lo:hi] - cs[:, POOL_HIST + 1 - w:POOL_HIST + 1 - w + L, lo:hi]
        cnt = jnp.minimum(w, pos + 1).astype(jnp.float32)
        outs.append(s / cnt[None, :, None])
    pooled = jnp.concatenate(outs, axis=-1) - pf[:, POOL_HIST:]
    grouped = pooled.reshape(B, L, N_POOL_GROUPS, POOL_GROUP)
    y = jnp.einsum('blgc,gco->blgo', grouped, w_pool.astype(jnp.float32)).reshape(B, L, D_MODEL)
    return (y * pool_scale.astype(jnp.float32)).astype(p_ext.dtype)

def moe(h, w_router, b_router, w_gate_up, b_gate_up, w_down, b_down):
    B, L, D = h.shape
    t = h.reshape(-1, D)
    T = t.shape[0]
    logits = (t @ w_router + b_router).astype(jnp.float32)
    top_v, top_i = lax.top_k(logits, TOP_K)
    gates = jax.nn.softmax(top_v, axis=-1)
    n_asg = T * TOP_K
    e = top_i.reshape(-1)
    tok = jnp.repeat(jnp.arange(T), TOP_K)
    g = gates.reshape(-1)
    order = jnp.argsort(e)
    e_s, tok_s, g_s = e[order], tok[order], g[order]
    counts = jnp.bincount(e, length=N_EXPERTS)
    padded = (counts + MOE_BLOCK - 1) // MOE_BLOCK * MOE_BLOCK
    start = jnp.cumsum(counts) - counts
    pend = jnp.cumsum(padded)
    pstart = pend - padded
    dest = pstart[e_s] + jnp.arange(n_asg) - start[e_s]
    n_blocks = -(-n_asg // MOE_BLOCK) + N_EXPERTS
    cap = n_blocks * MOE_BLOCK
    xp = jnp.zeros((cap, D), t.dtype).at[dest].set(t[tok_s])
    blk_e = jnp.minimum(jnp.searchsorted(pend, jnp.arange(n_blocks) * MOE_BLOCK, side='right'), N_EXPERTS - 1)

    def expert_block(args):
        xb, ei = args
        gu = xb @ w_gate_up[ei] + b_gate_up[ei]
        gate = jnp.minimum(gu[:, :D_FF], SWIGLU_LIMIT)
        up = jnp.clip(gu[:, D_FF:], -SWIGLU_LIMIT, SWIGLU_LIMIT)
        act = gate * jax.nn.sigmoid(gate * SWIGLU_ALPHA)
        return ((up + 1.0) * act) @ w_down[ei] + b_down[ei]

    yp = lax.map(expert_block, (xp.reshape(n_blocks, MOE_BLOCK, D), blk_e)).reshape(cap, D)
    y = jax.ops.segment_sum(yp[dest] * g_s[:, None].astype(yp.dtype), tok_s, num_segments=T)
    return y.reshape(B, L, D)

def decoder_layer(x, pos, pool_hist, past, norm1_g, w_in, q_norm_g, w_uq, kv_norm_g, w_uk, w_uv,
                  w_pool, pool_scale, w_out, norm2_g, w_router, b_router, w_gate_up, b_gate_up,
                  w_down, b_down):
    B, L, _ = x.shape
    h = rmsnorm(x, norm1_g)
    cq, ckv, kr, p, ga, gb = split_in(h @ w_in)
    q = (rmsnorm(cq, q_norm_g) @ w_uq).reshape(B, L, N_HEADS, QK_DIM)
    q_rope = rope(q[..., NOPE_DIM:], pos)
    q_lat = jnp.einsum('blhn,hnc->blhc', q[..., :NOPE_DIM], w_uk)
    ckv = rmsnorm(ckv, kv_norm_g)
    kr = rope(kr, pos)
    if past is None:
        o_lat = mla_attend_prompt(q_lat, q_rope, ckv, kr)
    else:
        o_lat = mla_attend_sample(q_lat, q_rope, ckv, kr, past[0], past[1])
    a = jnp.einsum('blhc,hcv->blhv', o_lat, w_uv).reshape(B, L, D_MODEL)
    p_ext = jnp.concatenate([pool_hist.astype(p.dtype), p], axis=1)
    b = pool_mix(p_ext, pos, w_pool, pool_scale)
    merged = jax.nn.sigmoid(ga) * a + jax.nn.sigmoid(gb) * b
    x = x + merged @ w_out
    x = x + moe(rmsnorm(x, norm2_g), w_router, b_router, w_gate_up, b_gate_up, w_down, b_down)
    return x, ckv, kr, p_ext[:, -POOL_HIST:]

def setup_inputs(seed: int = 0) -> dict:
    key = jax.random.key(seed)
    ks = jax.random.split(key, 32)
    f32 = jnp.float32
    n_pages = PAST_LEN // PAGE_SIZE
    n_phys = (DEC_BATCH * n_pages * 5) // 4

    def nrm(k, shape, scale):
        return jax.random.normal(k, shape, f32) * scale

    def gain(k, shape):
        return 1.0 + 0.05 * jax.random.normal(k, shape, f32)

    page_table = jax.random.permutation(ks[5], n_phys)[:DEC_BATCH * n_pages].reshape(DEC_BATCH, n_pages).astype(jnp.int32)
    return {
        'x_prompt': nrm(ks[0], (BATCH, SEQ, D_MODEL), 1.0),
        'x_sample': nrm(ks[1], (DEC_BATCH, DEC_SEQ, D_MODEL), 1.0),
        'cache_ckv': nrm(ks[2], (DEPTH, n_phys, PAGE_SIZE, KV_RANK), 1.0),
        'cache_krope': nrm(ks[3], (DEPTH, n_phys, PAGE_SIZE, ROPE_DIM), 1.0),
        'state_pool': nrm(ks[4], (DEPTH, DEC_BATCH, POOL_HIST, POOL_WIDTH), 1.0),
        'page_table': page_table,
        'meta_tokens': nrm(ks[6], (N_META, D_MODEL), 1.0),
        'norm1_g': gain(ks[7], (DEPTH, D_MODEL)),
        'w_in': nrm(ks[8], (DEPTH, D_MODEL, IN_COLS), D_MODEL ** -0.5),
        'q_norm_g': gain(ks[9], (DEPTH, Q_RANK)),
        'w_uq': nrm(ks[10], (DEPTH, Q_RANK, N_HEADS * QK_DIM), Q_RANK ** -0.5),
        'kv_norm_g': gain(ks[11], (DEPTH, KV_RANK)),
        'w_uk': nrm(ks[12], (DEPTH, N_HEADS, NOPE_DIM, KV_RANK), KV_RANK ** -0.5),
        'w_uv': nrm(ks[13], (DEPTH, N_HEADS, KV_RANK, V_DIM), KV_RANK ** -0.5),
        'w_pool': nrm(ks[14], (DEPTH, N_POOL_GROUPS, POOL_GROUP, POOL_OUT_GROUP), POOL_GROUP ** -0.5),
        'pool_scale': gain(ks[15], (DEPTH, D_MODEL)),
        'w_out': nrm(ks[16], (DEPTH, D_MODEL, D_MODEL), D_MODEL ** -0.5),
        'norm2_g': gain(ks[17], (DEPTH, D_MODEL)),
        'w_router': nrm(ks[18], (DEPTH, D_MODEL, N_EXPERTS), D_MODEL ** -0.5),
        'b_router': nrm(ks[19], (DEPTH, N_EXPERTS), 0.01),
        'w_gate_up': nrm(ks[20], (DEPTH, N_EXPERTS, D_MODEL, 2 * D_FF), D_MODEL ** -0.5),
        'b_gate_up': nrm(ks[21], (DEPTH, N_EXPERTS, 2 * D_FF), 0.01),
        'w_down': nrm(ks[22], (DEPTH, N_EXPERTS, D_FF, D_MODEL), D_FF ** -0.5),
        'b_down': nrm(ks[23], (DEPTH, N_EXPERTS, D_MODEL), 0.01),
        'final_norm_g': gain(ks[24], (D_MODEL,)),
    }

def reference(x_prompt, x_sample, cache_ckv, cache_krope, state_pool, page_table, meta_tokens,
              norm1_g, w_in, q_norm_g, w_uq, kv_norm_g, w_uk, w_uv, w_pool, pool_scale, w_out,
              norm2_g, w_router, b_router, w_gate_up, b_gate_up, w_down, b_down, final_norm_g):
    B = x_prompt.shape[0]
    Bd = x_sample.shape[0]
    n_pages = PAST_LEN // PAGE_SIZE
    xp = jnp.concatenate([jnp.broadcast_to(meta_tokens.astype(x_prompt.dtype)[None], (B, N_META, D_MODEL)), x_prompt], axis=1)
    pos_p = jnp.arange(xp.shape[1])
    pos_s = PAST_LEN + jnp.arange(x_sample.shape[1])
    xs = x_sample
    ckv_p_l, kr_p_l, pool_p_l, ckv_s_l, kr_s_l, pool_s_l = [], [], [], [], [], []
    for l in range(DEPTH):
        lw = (norm1_g[l], w_in[l], q_norm_g[l], w_uq[l], kv_norm_g[l], w_uk[l], w_uv[l], w_pool[l],
              pool_scale[l], w_out[l], norm2_g[l], w_router[l], b_router[l], w_gate_up[l],
              b_gate_up[l], w_down[l], b_down[l])
        hist0 = jnp.zeros((B, POOL_HIST, POOL_WIDTH), xp.dtype)
        xp, ckv_p, kr_p, pool_p = decoder_layer(xp, pos_p, hist0, None, *lw)
        past = (cache_ckv[l][page_table].reshape(Bd, n_pages * PAGE_SIZE, KV_RANK),
                cache_krope[l][page_table].reshape(Bd, n_pages * PAGE_SIZE, ROPE_DIM))
        xs, ckv_s, kr_s, pool_s = decoder_layer(xs, pos_s, state_pool[l], past, *lw)
        ckv_p_l.append(ckv_p); kr_p_l.append(kr_p); pool_p_l.append(pool_p)
        ckv_s_l.append(ckv_s); kr_s_l.append(kr_s); pool_s_l.append(pool_s)
    y_prompt = rmsnorm(xp, final_norm_g)[:, N_META:]
    y_sample = rmsnorm(xs, final_norm_g)
    new_ckv_prompt = jnp.stack(ckv_p_l)
    new_krope_prompt = jnp.stack(kr_p_l)
    new_pool_prompt = jnp.stack(pool_p_l)
    new_ckv_sample = jnp.stack(ckv_s_l)
    new_krope_sample = jnp.stack(kr_s_l)
    new_pool_sample = jnp.stack(pool_s_l)
    return (y_prompt, y_sample, new_ckv_prompt, new_krope_prompt, new_pool_prompt, new_ckv_sample, new_krope_sample, new_pool_sample)


_drawn_inputs = setup_inputs


def setup_inputs(seed=0):
    import zlib

    import numpy as np

    out = dict(_drawn_inputs(seed))
    spreads = {}
    factors = {'cache_ckv': 2.883, 'cache_krope': 5.172, 'q_norm_g': 8.0, 'b_gate_up': 8.0, 'b_down': 8.0}
    for name, (base, spread) in spreads.items():
        noise = np.random.default_rng([zlib.crc32(name.encode()), seed]).standard_normal(out[name].shape)
        drawn = base * np.exp(spread * noise) if base else spread * noise
        out[name] = __import__('jax').numpy.asarray(drawn.astype(out[name].dtype))
    for name, factor in factors.items():
        out[name] = (out[name] * factor).astype(out[name].dtype)
    return out
```

```python
from contextlib import ExitStack

import concourse.bass as bass
from concourse import mybir

F32 = mybir.dt.float32
I32 = mybir.dt.int32
U32 = mybir.dt.uint32
ALU = mybir.AluOpType
ACT = mybir.ActivationFunctionType
AX = mybir.AxisListType

P = 128
D = 1024
KD = D // P
SEQ, META, NB = 256, 16, 8
LP = META + SEQ
T = LP + NB
ROWS = (P, P, T - 2 * P)
NT = len(ROWS)
LAST = LP - 2 * P
H = 8
C = 256
CT = C // P
R = 32
NO = 64
QK = NO + R
PW = 512
G = 4
HIST = 15
PAGES, PAGE, PAST = 16, 128, 2048
NE = 32
SL = 64
PASSES = -(-T // SL)
SCALE = (NO + R) ** -0.5
EPS = 1e-6
LIMIT, ALPHA = 7.0, 1.702
QKV = 2 * C + R
SLOT = 4096
NSLOT = 6
NEG = -1.0e30

CONST = {}
_at = 0
for _name, _n in (("ident", P), ("rope", T), ("rope0", T), ("fold", P), ("fold_hi", R), ("half", P),
                  ("before", P), ("iota", PASSES * SL), ("mask1", 2 * P), ("mask2", LP), ("headsel", H),
                  ("diag", NB * H), ("invcnt", G * 16), ("valid", NT), ("mod32", 1)):
    CONST[_name] = (_at, _n)
    _at += _n
NCONST = _at
VECS = 2 * KD + 2 * CT


def build(nc, a, o):
    with ExitStack() as ctx:
        def sem(name):
            return ctx.enter_context(nc.semaphore(name))

        arena = ctx.enter_context(nc.sbuf_tensor("arena", [P, 53200], F32))
        ps = ctx.enter_context(nc.psum_tensor("ps", [P, 8, 512], F32))
        top = [0]

        def at(start, n):
            return arena[:, start:start + n]

        def take(n):
            start = top[0]
            top[0] += n
            assert top[0] <= 53200, top[0]
            return start

        ring0 = take(NSLOT * SLOT)
        slot = [at(ring0 + SLOT * c, SLOT) for c in range(NSLOT)]
        w_uk = at(ring0, H * C)[0:NO, :].rearrange("p (h c) -> p h c", h=H)
        p_ext = at(ring0 + 2048, G * (16 + LP)).rearrange("p (g t) -> p g t", g=G)
        s_ext = at(ring0 + 2048 + G * (16 + LP), G * NB * 16).rearrange("p (g b t) -> p g b t", g=G, b=NB)
        sample0 = ring0 + SLOT
        keysT = at(sample0, 3 * PAST).rearrange("p (t k) -> p t k", t=3)
        w_qkv = at(sample0, KD * QKV).rearrange("p (k n) -> p k n", k=KD)
        w_kr = at(sample0 + KD * QKV, KD * 2 * R).rearrange("p (k n) -> p k n", k=KD)
        cache_c, cache_r = [], []
        for u in range(2):
            base = sample0 + 3 * PAST + u * (PAGES * (C + R))
            cache_c.append(at(base, PAGES * C))
            cache_r.append(at(base + PAGES * C, PAGES * R))
        base = sample0 + 3 * PAST + PAGES * (C + R)
        w_uq = at(base, CT * H * QK).rearrange("p (k h n) -> p k h n", k=CT, h=H)
        w_uqx = at(base + CT * H * QK, CT * H * P).rearrange("p (k h n) -> p k h n", k=CT, h=H)
        o_part = at(ring0 + 5 * SLOT, NB * C).rearrange("p (b c) -> p b c", b=NB)
        w_p = slot[5].rearrange("p (k n) -> p k n", k=KD)

        x = at(take(NT * D), NT * D).rearrange("p (t d) -> p t d", t=NT)
        start = take(NT * D)
        xn = at(start, NT * D).rearrange("p (t d) -> p t d", t=NT)
        vals = xn
        h2 = xn
        hT = at(take(KD * T), KD * T).rearrange("p (k t) -> p k t", k=KD)
        start = take(KD * T)
        zT = at(start, 4 * T).rearrange("p (k t) -> p k t", k=4)
        zsq0 = start + 4 * T
        zsq = at(zsq0, 4 * T).rearrange("p (k t) -> p k t", k=4)
        mT = at(start, KD * T).rearrange("p (k t) -> p k t", k=KD)
        start = take(CT * H * NO)
        norm2_g = at(start, D)
        w_ukT = at(start, CT * H * NO).rearrange("p (k n) -> p k n", k=CT)
        start = take(CT * H * P)
        w_uv = at(start, CT * H * P).rearrange("p (h k v) -> p h k v", h=H, k=CT)
        w_rt = at(start, KD * NE).rearrange("p (k e) -> p k e", k=KD)
        b_rt = at(start + KD * NE, NE)
        final_g = at(start + 512, D)
        w_pool = at(take(G * 256), G * 256).rearrange("p (g n) -> p g n", g=G)
        start = take(3 * T)
        r_bc = at(start, 2 * T).rearrange("p (k t) -> p k t", k=2)
        rope_q = at(start + 2 * T, T)
        probs2T = at(start, 2 * 3 * P).rearrange("p (g k q) -> p g k q", g=2, k=3)
        con0 = take(NCONST)
        const = {k: at(con0 + s, n) for k, (s, n) in CONST.items()}
        ones = at(take(P), P)
        vrow = at(take(P), P)[0:VECS, :]
        vecT = at(take(VECS), VECS)
        small = at(take(64), 64)
        small2 = at(take(64), 64)
        idx = at(take(NB * 4), NB * 4).bitcast(U32)
        pool_cell = at(take(2), 2)
        idx_now = at(take(8), 8).bitcast(U32)
        pt = at(take(NB * PAGES), NB * PAGES).bitcast(I32)
        stats = at(take(2 * NB), 2 * NB).rearrange("p (k b) -> p k b", k=2)
        aS = at(take(H * NB), H * NB).rearrange("p (h b) -> p h b", h=H)
        sga_last = at(take(H * LAST), H * LAST).rearrange("p (h t) -> p h t", h=H)
        overlay = top[0]
        TQ = T + 8
        qT = at(take(H * TQ), H * TQ).rearrange("p (h t) -> p h t", h=H)
        kT = at(take(2 * LP), 2 * LP).rearrange("p (u t) -> p u t", u=2)
        krT = at(take(T), T)
        kr_cs = at(take(T), T)
        cT = at(take(CT * T), CT * T).rearrange("p (k t) -> p k t", k=CT)
        c_out = at(take(NT * (C + R)), NT * (C + R)).rearrange("p (t c) -> p t c", t=NT)
        start = take(G * T)
        pooled = at(start, G * T).rearrange("p (g t) -> p g t", g=G)
        qL = at(take(CT * NB * 32), CT * NB * 32).rearrange("p (k b h) -> p k b h", k=CT, b=NB)
        qR = at(take(NB * 32), NB * 32).rearrange("p (b h) -> p b h", b=NB)
        qLb = at(take(2 * CT * 32), 2 * CT * 32).rearrange("p (u k h) -> p u k h", u=2, k=CT)
        qRb = at(take(2 * 32), 2 * 32).rearrange("p (u h) -> p u h", u=2)
        probs0 = take(2 * 512)
        probs = at(probs0, 2 * 512).rearrange("p (u k) -> p u k", u=2)
        probsT0 = take(2 * 512)
        probsT = at(probsT0, 2 * 512).rearrange("p (u k) -> p u k", u=2)
        sig0 = take(2 * T + 16)
        sig = at(sig0, 2 * T).rearrange("p (k t) -> p k t", k=2)
        pool_a = at(probs0, LP)
        pool_b = at(probs0 + 512, LP)
        sp_rows = at(probsT0, PW)[0:NB * HIST, :]
        p_rows = at(zsq0, PW)[0:HIST, :]
        s_rows = at(zsq0 + PW, PW)[0:NB, :]
        probs_last = kr_cs[:, 0:LP]
        merge0 = probs0
        top_front = top[0]
        top[0] = overlay
        lg = at(take(NT * NE), NT * NE).rearrange("p (t e) -> p t e", t=NT)
        top8 = at(take(NT * 8), NT * 8).rearrange("p (t e) -> p t e", t=NT)
        rt = at(take(4 * NT * NE), 4 * NT * NE).rearrange("p (n t e) -> p n t e", n=4, t=NT)
        sel = at(take(NT * NE), NT * NE).rearrange("p (t e) -> p t e", t=NT)
        rank = at(take(NT * (NE + 1)), NT * (NE + 1)).rearrange("p (t e) -> p t e", t=NT)
        gates = at(take(NT * (NE + 1)), NT * (NE + 1)).rearrange("p (t e) -> p t e", t=NT)
        most = at(take(2), 2)
        most_i = at(take(2), 2).bitcast(I32)
        pick = at(take(NT * SL), NT * SL).rearrange("p (t s) -> p t s", t=NT)
        pickg = at(take(NT * 2 * SL), NT * 2 * SL).rearrange("p (t u s) -> p t u s", t=NT, u=2)
        pickT = at(take(NT * P), NT * P).rearrange("p (t n) -> p t n", t=NT)
        xg = at(take(KD * SL), KD * SL).rearrange("p (k s) -> p k s", k=KD)
        gate = at(take(512), 512)
        sgm = at(take(512), 512)
        up = at(take(512), 512)
        upg = at(take(512), 512)
        hid = at(take(512), 512)
        hidT = at(take(512), 512).rearrange("p (j n) -> p j n", j=4)
        ye = at(take(512), 512)
        bias = at(take(3 * 512), 3 * 512)[0:2, :].rearrange("p (g n) -> p g n", g=3)
        top[0] = max(top[0], top_front)

        ident = const["ident"]
        half = const["half"][0:2, :]

        in_x, in_const, in_vec, in_g2 = sem("in_x"), sem("in_const"), sem("in_vec"), sem("in_g2")
        in_qkv = [sem("in_qkv_a"), sem("in_qkv_b")]
        in_uq, in_uk, in_uv, in_pool, in_p, in_hist, in_pt = (
            sem(n) for n in ("in_uq", "in_uk", "in_uv", "in_pool", "in_p", "in_hist", "in_pt"))
        in_gab = [sem(f"in_gab{j}") for j in range(4)]
        in_wo = [sem("in_wo0"), sem("in_wo1")]
        in_router, in_final = sem("in_router"), sem("in_final")
        in_cache = [sem("in_cache0"), sem("in_cache1")]
        in_chunk = [sem(f"in_chunk{c}") for c in range(NSLOT)]
        in_bias = sem("in_bias")
        out_small, out_y = sem("out_small"), sem("out_y")
        ones_ready, kr_weights, uq_weights, zeros_ready, idx_ready = (
            sem(n) for n in ("ones_ready", "kr_weights", "uq_weights", "zeros_ready", "idx_ready"))
        idx_copied = sem("idx_copied")
        dve_step, act_step, pool_step = sem("dve_step"), sem("act_step"), sem("pool_step")
        sumsq, meansq, root, xn_ready = sem("sumsq"), sem("meansq"), sem("root"), sem("xn_ready")
        pe_vec, vec_ready, pe_hT, hT_act, hT_dve = (
            sem(n) for n in ("pe_vec", "vec_ready", "pe_hT", "hT_act", "hT_dve"))
        pe_z, zsq_ready, z_copied, kr_rot = (sem(n) for n in ("pe_z", "zsq_ready", "z_copied", "kr_rot"))
        pe_stat, r_ready, c_ready = sem("pe_stat"), sem("r_ready"), sem("c_ready")
        pe_ukT, ukT_ready, pe_hist, hist_ready = (
            sem(n) for n in ("pe_ukT", "ukT_ready", "pe_hist", "hist_ready"))
        pe_p, p_prompt, p_sample, pooled_ready = (
            sem(n) for n in ("pe_p", "p_prompt", "p_sample", "pooled_ready"))
        pe_kr, kr_ready, kT_rope = sem("pe_kr"), sem("kr_ready"), sem("kT_rope")
        pe_q, q_ready, pe_v, v_ready = sem("pe_q"), sem("q_ready"), sem("pe_v"), sem("v_ready")
        pe_cout, cout_ready, pe_prow, prow_ready = (
            sem(n) for n in ("pe_cout", "cout_ready", "pe_prow", "prow_ready"))
        pe_ql, ql_ready = sem("pe_ql"), sem("ql_ready")
        pe_kt, kt_act, kt_dve, q_batch, s_done, s_max, e_ready = (
            sem(n) for n in ("pe_kt", "kt_act", "kt_dve", "q_batch", "s_done", "s_max", "e_ready"))
        pe_pt, pt_ready, pv_done, o_ready = (sem(n) for n in ("pe_pt", "pt_ready", "pv_done", "o_ready"))
        merge_in, pe_merge, merge_act = sem("merge_in"), sem("pe_merge"), sem("merge_act")
        pe_k, k_ready, pe_s, s_masked, p_exp, p_norm = (
            sem(n) for n in ("pe_k", "k_ready", "pe_s", "s_masked", "p_exp", "p_norm"))
        pe_pT, pT_ready, pe_a, a_merged = (sem(n) for n in ("pe_pT", "pT_ready", "pe_a", "a_merged"))
        pe_gab, gab_exp, sig_ready, pe_y, y_merged = (
            sem(n) for n in ("pe_gab", "gab_exp", "sig_ready", "pe_y", "y_merged"))
        s2_masked, p2_exp, p2_norm, pe_p2T, p2T_ready, pe_a2, a2_merged = (
            sem(n) for n in ("s2_masked", "p2_exp", "p2_norm", "pe_p2T", "p2T_ready", "pe_a2", "a2_merged"))
        pe_wo, x_mid = sem("pe_wo"), sem("x_mid")
        h2_ready, pe_h2T, h2T_act, h2T_dve = (sem(n) for n in ("h2_ready", "pe_h2T", "h2T_act", "h2T_dve"))
        pe_logit, top_ready, e_top, sel_ready, pe_rank, rank_ready, most_ready = (
            sem(n) for n in ("pe_logit", "top_ready", "e_top", "sel_ready", "pe_rank", "rank_ready", "most_ready"))
        slot_free = [sem(f"slot_free{c}") for c in range(NSLOT)]
        x_zero, out_pool, sum_kept = sem("x_zero"), sem("out_pool"), sem("sum_kept")
        pick_ready, pickg_ready, pe_gather, xg_ready = (
            sem(n) for n in ("pick_ready", "pickg_ready", "pe_gather", "xg_ready"))
        pe_gu, gate_ready, up_ready, upg_ready, sgm_ready, hid_ready = (
            sem(n) for n in ("pe_gu", "gate_ready", "up_ready", "upg_ready", "sgm_ready", "hid_ready"))
        pe_pick, pickT_ready, pe_hidT, hidT_ready, pe_down, ye_ready = (
            sem(n) for n in ("pe_pick", "pickT_ready", "pe_hidT", "hidT_ready", "pe_down", "ye_ready"))
        pe_comb, y_added, y_final = sem("pe_comb"), sem("y_added"), sem("y_final")

        block = ctx.enter_context(nc.Block())

        win = a["w_in"].rearrange("l (k p) n -> p (l k) n", p=P)
        cache_c_rows = a["cache_ckv"].rearrange("l n (q i) c -> (l n q) (i c)", i=4)
        cache_r_rows = a["cache_krope"].rearrange("l n (q i) c -> (l n q) (i c)", i=4)
        gu_rows = a["w_gate_up"].rearrange("l e (k p) n -> p (l e k) n", p=P)
        dn_rows = a["w_down"].rearrange("l e (k p) n -> p (l e k) n", p=P)
        bgu_rows = a["b_gate_up"].rearrange("l e (g u n) -> u (l e) g n", g=2, u=2)
        bdn_rows = a["b_down"].rearrange("l e (u n) -> u (l e) n", u=2)

        @block.sync
        def _(sp):
            sp.dma_start(x[0:META, 0, :], a["meta_tokens"]).then_inc(in_x, 16)
            sp.dma_start(x[META:P, 0, :], a["x_prompt"][0, 0:P - META, :]).then_inc(in_x, 16)
            sp.dma_start(x[:, 1, :], a["x_prompt"][0, P - META:2 * P - META, :]).then_inc(in_x, 16)
            sp.wait_ge(x_zero, 1)
            sp.dma_start(x[0:LAST, 2, :], a["x_prompt"][0, 2 * P - META:SEQ, :]).then_inc(in_x, 16)
            sp.dma_start(x[LAST:LAST + NB, 2, :], a["x_sample"][:, 0, :]).then_inc(in_x, 16)
            sp.dma_start(at(con0, NCONST), a["consts"]).then_inc(in_const, 16)
            for j in range(2):
                sp.dma_start(w_qkv[:, 4 * j:4 * j + 4, :], win[:, 4 * j:4 * j + 4, 0:QKV]).then_inc(in_qkv[j], 16)
            sp.dma_start(w_uk, a["w_uk"][0].rearrange("h n c -> n h c")).then_inc(in_uk, 16)
            sp.dma_start(w_uq, a["w_uq"][0].rearrange("(k p) (h n) -> p k h n", p=P, h=H)).then_inc(in_uq, 16)
            sp.dma_start(w_p, win[:, :, QKV:QKV + PW]).then_inc(in_p, 16)
            sp.dma_start(sp_rows, a["state_pool"][0].rearrange("b t c -> (b t) c")).then_inc(in_hist, 16)
            sp.dma_start(w_uv, a["w_uv"][0].rearrange("h (k p) v -> p h k v", p=P)).then_inc(in_uv, 16)
            sp.dma_start(w_pool, a["w_pool"][0].rearrange("g p n -> p g n")).then_inc(in_pool, 16)
            sp.dma_start(o["pool_s"][0, :, 0:HIST - 1, :], a["state_pool"][0, :, 1:HIST, :]).then_inc(out_small, 16)
            for j in range(4):
                if j == 0:
                    sp.wait_ge(pe_ql, 1)
                    sp.wait_ge(pe_prow, 1)
                    sp.wait_ge(pooled_ready, G)
                    sp.wait_ge(p_sample, G + 1)
                else:
                    sp.wait_ge(pv_done, NB)
                dst = slot[j].rearrange("p (k u n) -> p k u n", k=KD, u=2)
                for u in range(2):
                    col = QKV + PW + u * D + j * 256
                    sp.dma_start(dst[:, :, u, :], win[:, :, col:col + 256]).then_inc(in_gab[j], 16)
            for n in range(2):
                if n == 1:
                    sp.wait_ge(pe_merge, 3)
                sp.dma_start(slot[4 + n].rearrange("p (k n) -> p k n", k=KD),
                             a["w_out"][0].rearrange("(k p) n -> p k n", p=P)[:, :, 512 * n:512 * n + 512]
                             ).then_inc(in_wo[n], 16)
            sp.wait_ge(pe_merge, 4)
            sp.dma_start(w_rt, a["w_router"][0].rearrange("(k p) e -> p k e", p=P)).then_inc(in_router, 16)
            sp.dma_start(b_rt, a["b_router"].to_broadcast([P, NE])).then_inc(in_router, 16)
            sp.dma_start(final_g, a["final_norm_g"].rearrange("(a n) -> a n", a=1).to_broadcast([P, D])
                         ).then_inc(in_final, 16)

            def expert_weights(e, n):
                for c in range(4):
                    sp.wait_ge(slot_free[c], n + 1)
                    sp.dma_start(slot[c].rearrange("p (k n) -> p k n", k=2),
                                 gu_rows[:, bass.ds(e * KD + 2 * c, 2), :]).then_inc(in_chunk[c], 16)
                sp.wait_ge(h2_ready, 1)
                sp.wait_ge(out_small, 144)
                sp.wait_ge(pe_down, n)
                sp.dma_start(bias[:, 0:2, :], bgu_rows[:, bass.ds(e, 1), :, :].rearrange("u e g n -> u (e g) n")
                             ).then_inc(in_bias, 16)
                sp.dma_start(bias[:, 2, :], bdn_rows[:, bass.ds(e, 1), :].rearrange("u e n -> u (e n)")
                             ).then_inc(in_bias, 16)
                for c in range(2):
                    sp.wait_ge(slot_free[4 + c], n + 1)
                    sp.dma_start(slot[4 + c].rearrange("p (k n) -> p k n", k=4),
                                 dn_rows[:, bass.ds(e * KD + 4 * c, 4), :]).then_inc(in_chunk[4 + c], 16)

            with sp.Fori(0, NE) as e:
                expert_weights(e, e)
            sp.wait_ge(most_ready, 1)
            count = sp.value_load(most_i[0:1, 0:1], min_val=0, max_val=T)
            with sp.If(count > SL):
                with sp.Fori(0, PASSES - 1) as j:
                    with sp.Fori(0, NE) as e:
                        expert_weights(e, j * NE + e + NE)
            sp.wait_ge(y_final, 1 + NT)
            sp.dma_start(o["y_p"][0, 0:P - META, :], h2[META:P, 0, :]).then_inc(out_y, 16)
            sp.dma_start(o["y_p"][0, P - META:2 * P - META, :], h2[:, 1, :]).then_inc(out_y, 16)
            sp.dma_start(o["y_p"][0, 2 * P - META:SEQ, :], h2[0:LAST, 2, :]).then_inc(out_y, 16)
            sp.dma_start(o["y_s"][:, 0, :], h2[LAST:LAST + NB, 2, :]).then_inc(out_y, 16)
            sp.wait_ge(out_y, 64)

        @block.gpsimd
        def _(pool):
            made = [0]

            def link(ins):
                made[0] += 1
                ins.then_inc(pool_step, 1)
                pool.wait_ge(pool_step, made[0])

            pool.memset(ones, 1.0).then_inc(ones_ready, 1)
            pool.wait_ge(idx_ready, 4)

            def gather_cache(u, col):
                pool.tensor_copy(idx_now[:, 4 * u:4 * u + 4], idx[:, col]).then_inc(idx_copied, 1)

            def start_cache(u):
                for s in range(4):
                    off = bass.IndirectOffsetOnAxis(ap=idx_now[:, 4 * u + s:4 * u + s + 1], axis=0)
                    pool.indirect_dma_start(cache_c[u][:, 4 * C * s:4 * C * s + 4 * C], None, cache_c_rows, off
                                            ).then_inc(in_cache[u], 16)
                    pool.indirect_dma_start(cache_r[u][:, 4 * R * s:4 * R * s + 4 * R], None, cache_r_rows, off
                                            ).then_inc(in_cache[u], 16)

            for u in range(2):
                gather_cache(u, slice(4 * u, 4 * u + 4))
                pool.wait_ge(idx_copied, u + 1)
                if u == 0:
                    start_cache(u)
            for j in range(2):
                pool.wait_ge(in_qkv[j], 16)
            link(pool.tensor_copy(w_kr[:, :, 0:R], w_qkv[:, :, 2 * C:QKV]))
            link(pool.tensor_scalar(w_kr[:, :, R:R + 16], w_qkv[:, :, 2 * C + 16:QKV], -1.0, None, ALU.mult))
            pool.tensor_copy(w_kr[:, :, R + 16:2 * R], w_qkv[:, :, 2 * C:2 * C + 16]).then_inc(kr_weights, 1)
            pool.wait_ge(in_uq, 16)
            pool.wait_ge(vec_ready, 1)
            for k in range(CT):
                g = vecT[:, 2 * KD + k:2 * KD + k + 1]
                link(pool.tensor_scalar(w_uqx[:, k, :, 0:QK], w_uq[:, k, :, :], g, None, ALU.mult))
                link(pool.tensor_scalar(w_uqx[:, k, :, QK:QK + 16], w_uq[:, k, :, NO + 16:QK], g, -1.0,
                                        ALU.mult, ALU.mult))
                pool.tensor_scalar(w_uqx[:, k, :, QK + 16:P], w_uq[:, k, :, NO:NO + 16], g, None,
                                   ALU.mult).then_inc(uq_weights, 1)
            pool.memset(qL[:], 0.0).then_inc(zeros_ready, 1)
            pool.memset(qR[:], 0.0).then_inc(zeros_ready, 1)
            pool.memset(p_ext[:, :, 0:16], 0.0).then_inc(zeros_ready, 1)
            pool.memset(qT[:, :, T:TQ], 0.0).then_inc(zeros_ready, 1)
            pool.wait_ge(pe_q, H)
            start_cache(1)
            pool.wait_ge(p_prompt, G)
            pool.wait_ge(zeros_ready, 4)
            for g in range(G):
                w = 2 << g
                src = p_ext[:, g, :]
                link(pool.tensor_tensor(pool_a, src[:, 16:16 + LP], src[:, 15:15 + LP], ALU.add))
                now, other = pool_a, pool_b
                n = 2
                while n < w:
                    link(pool.tensor_copy(other[:, 0:n], now[:, 0:n]))
                    link(pool.tensor_tensor(other[:, n:LP], now[:, n:LP], now[:, 0:LP - n], ALU.add))
                    now, other = other, now
                    n *= 2
                link(pool.tensor_scalar(other[:, 16:LP], now[:, 16:LP], 1.0 / w, None, ALU.mult))
                link(pool.tensor_tensor(other[:, 0:16], now[:, 0:16],
                                        const["invcnt"].rearrange("p (g t) -> p g t", g=G)[:, g, :], ALU.mult))
                pool.tensor_tensor(pooled[:, g, 0:LP], other, src[:, 16:16 + LP], ALU.subtract
                                   ).then_inc(pooled_ready, 1)
                pool.wait_ge(pooled_ready, g + 1)
            with pool.Fori(1, NB // 2) as i:
                for u in range(2):
                    pool.wait_ge(pv_done, 2 * i + u - 1)
                    gather_cache(u, bass.ds((2 * i + u) * 4, 4))
                    pool.wait_ge(idx_copied, 2 * i + u + 1)
                    pool.tensor_tensor(pool_cell[0:1, u:u + 1], ones[0:1, 0:1], ones[0:1, 0:1], ALU.add)
                    start_cache(u)

        @block.tensor
        def _(pe):
            mm = nc.tensor.matmul

            pe.wait_ge(in_vec, 64)
            pe.wait_ge(in_const, 16)
            nc.tensor.transpose(ps[:, 7, 0:VECS], vrow, ident[0:VECS, 0:VECS]).then_inc(pe_vec, 1)
            pe.wait_ge(xn_ready, NT)
            for k in range(KD):
                if k >= 4:
                    pe.wait_ge(hT_act if k % 2 == 0 else hT_dve, (k - 4) // 2 + 1)
                for t in range(NT):
                    m = nc.tensor.transpose(ps[:, k % 4, P * t:P * t + ROWS[t]],
                                            xn[0:ROWS[t], t, P * k:P * k + P], ident[0:ROWS[t], 0:ROWS[t]])
                m.then_inc(pe_hT, 1)
            pe.wait_ge(vec_ready, 1)
            for k in range(KD):
                pe.wait_ge(hT_act if k % 2 == 0 else hT_dve, k // 2 + 1)
                if k % 4 == 0:
                    pe.wait_ge(in_qkv[k // 4], 16)
                for j in range(4):
                    m = mm(ps[:, 4 + j, 0:T], w_qkv[:, k, P * j:P * j + P], hT[:, k, :],
                           start=(k == 0), stop=(k == KD - 1))
                    if k == KD - 1:
                        m.then_inc(pe_z, 1)
            pe.wait_ge(kr_weights, 1)
            for k in range(KD):
                m = mm(ps[0:2 * R, 0, 0:T], w_kr[:, k, :], hT[:, k, :], start=(k == 0), stop=(k == KD - 1))
            m.then_inc(pe_z, 1)
            pe.wait_ge(in_uk, 16)
            for k in range(CT):
                bank = 3 if k == 0 else 4
                if k == 1:
                    pe.wait_ge(zsq_ready, 1)
                    pe.wait_ge(z_copied, 1)
                for h in range(H):
                    m = nc.tensor.transpose(ps[:, bank, NO * h:NO * h + NO], w_uk[:, h, P * k:P * k + P],
                                            ident[0:NO, 0:NO])
                m.then_inc(pe_ukT, 1)
            pe.wait_ge(ones_ready, 1)
            for j in range(2):
                pe.wait_ge(zsq_ready, 2 * j + 2)
                for k in range(CT):
                    m = mm(ps[:, 1 + j, 0:T], ones, zsq[:, 2 * j + k, :], start=(k == 0), stop=(k == CT - 1))
                m.then_inc(pe_stat, 1)
            pe.wait_ge(in_hist, 16)
            pe.wait_ge(z_copied, 2)
            for g in range(G):
                m = nc.tensor.transpose(ps[:, 5, P * g:P * g + NB * HIST], sp_rows[:, P * g:P * g + P],
                                        ident[0:NB * HIST, 0:NB * HIST])
            m.then_inc(pe_hist, 1)
            pe.wait_ge(kr_rot, 1)
            mm(ps[:, 0, 0:T], const["fold"][0:2 * R, :], kr_cs[0:2 * R, :], start=True, stop=True).then_inc(pe_kr, 1)
            pe.wait_ge(in_p, 16)
            pe.wait_ge(zsq_ready, 4)
            pe.wait_ge(z_copied, 4)
            for g in range(G):
                bank = (6, 7, 6, 7)[g]
                if g >= 2:
                    pe.wait_ge(p_prompt, g - 1)
                    pe.wait_ge(p_sample, g - 1)
                for k in range(KD):
                    m = mm(ps[:, bank, 0:T], w_p[:, k, P * g:P * g + P], hT[:, k, :],
                           start=(k == 0), stop=(k == KD - 1))
                m.then_inc(pe_p, 1)
            pe.wait_ge(uq_weights, CT)
            pe.wait_ge(r_ready, 2)
            pe.wait_ge(ukT_ready, 2)
            for h in range(H):
                bank = 1 + h % 4
                if h >= 4:
                    pe.wait_ge(q_ready, h - 3)
                for k in range(CT):
                    m = mm(ps[:, bank, 0:T], w_uqx[:, k, h, :], zT[:, k, :], start=(k == 0), stop=(k == CT - 1))
                m.then_inc(pe_q, 1)
            pe.wait_ge(p_prompt, G)
            pe.wait_ge(p_sample, G)
            pe.wait_ge(hist_ready, 1)
            for g in range(G):
                m = nc.tensor.transpose(ps[0:HIST, 5, P * g:P * g + P], p_ext[:, g, 16 + LP - HIST:16 + LP], ident)
            for g in range(G):
                m = nc.tensor.transpose(ps[0:NB, 6, P * g:P * g + P], s_ext[:, g, :, HIST], ident)
            m.then_inc(pe_prow, 1)
            pe.wait_ge(q_ready, H)
            pe.wait_ge(zeros_ready, 4)
            for h in range(H):
                for k in range(CT):
                    m = mm(ps[:, 7, (k * H + h) * NB:(k * H + h) * NB + NB], w_uk[:, h, P * k:P * k + P],
                           qT[0:NO, h, LP:T], start=True, stop=True)
            m.then_inc(pe_ql, 1)
            pe.wait_ge(kr_ready, 1)
            mm(ps[0:R, 0, 0:H * NB].rearrange("p (h b) -> p h b", h=H), const["fold_hi"][NO:P, :],
               qT[NO:P, :, LP:T], start=True, stop=True).then_inc(pe_ql, 1)
            pe.wait_ge(c_ready, 2)
            pe.wait_ge(in_uv, 16)
            for t in range(NT):
                rows = ROWS[t] if t < 2 else LAST
                for n in range(2):
                    g = 2 * t + n
                    if g >= 4:
                        pe.wait_ge(v_ready, g - 3)
                    for k in range(CT):
                        m = mm(ps[0:rows, 1 + g % 4, :], cT[:, k, P * t:P * t + rows],
                               w_uv[:, 4 * n:4 * n + 4, k, :],
                               start=(k == 0), stop=(k == CT - 1))
                    m.then_inc(pe_v, 1)
            pe.wait_ge(prow_ready, 1)
            pe.wait_ge(ql_ready, 3)
            for t in range(NT):
                bank = 5 + t
                for k in range(CT):
                    nc.tensor.transpose(ps[0:ROWS[t], bank, P * k:P * k + P], cT[:, k, P * t:P * t + ROWS[t]], ident)
                nc.tensor.transpose(ps[0:ROWS[t], bank, C:C + R], krT[0:R, P * t:P * t + ROWS[t]],
                                    ident[0:R, 0:R]).then_inc(pe_cout, 1)
            pe.wait_ge(v_ready, 6)
            pe.wait_ge(cout_ready, 3)

            def turn_keys(u, b):
                for s in range(4):
                    if s >= 2:
                        pe.wait_ge(kt_act, 6 * b + (1, 3)[s - 2])
                        pe.wait_ge(kt_dve, 6 * b + (2, 3)[s - 2])
                    for i in range(4):
                        key = cache_c[u][:, (4 * s + i) * C:(4 * s + i + 1) * C]
                        for k in range(CT):
                            nc.tensor.transpose(ps[:, 3 * (s % 2) + k, P * i:P * i + P], key[:, P * k:P * k + P], ident)
                        m = nc.tensor.transpose(ps[0:R, 3 * (s % 2) + 2, P * i:P * i + P],
                                                cache_r[u][:, (4 * s + i) * R:(4 * s + i + 1) * R], ident)
                    m.then_inc(pe_kt, 1)
                pe.wait_ge(kt_act, 6 * b + 6)
                pe.wait_ge(kt_dve, 6 * b + 6)

            def score(u, b):
                pe.wait_ge(q_batch, 2 * b + 2)
                pe.wait_ge(e_ready, b)
                for k in range(3):
                    for s in range(4):
                        lhs = qLb[:, u, k, :] if k < 2 else qRb[0:R, u, :]
                        rhs = keysT[0:(P if k < 2 else R), k, 512 * s:512 * s + 512]
                        m = mm(ps[32 * s:32 * s + 32, 6, :], lhs, rhs, start=(k == 0), stop=(k == 2))
                m.then_inc(s_done, 1)

            def turn_probs(u, b):
                pe.wait_ge(e_ready, b + 1)
                pe.wait_ge(pt_ready, b)
                for i in range(4):
                    m = nc.tensor.transpose(ps[:, 7, P * i:P * i + P], probs[:, u, P * i:P * i + P], ident)
                m.then_inc(pe_pt, 1)

            def weigh(u, b):
                pe.wait_ge(pt_ready, b + 1)
                for i in range(4):
                    for s in range(4):
                        m = mm(ps[32 * s:32 * s + 32, u, 0:C], probsT[:, u, P * i + 32 * s:P * i + 32 * s + 32],
                               cache_c[u][:, (4 * s + i) * C:(4 * s + i + 1) * C], start=(i == 0), stop=(i == 3))
                m.then_inc(pv_done, 1)

            with pe.Fori(0, NB // 2) as i:
                b = [2 * i, 2 * i + 1]
                pe.wait_ge(o_ready, b[0])
                pe.wait_ge(in_cache[0], 128 * i + 128)
                turn_keys(0, b[0])
                score(0, b[0])
                pe.wait_ge(in_cache[1], 128 * i + 128)
                turn_keys(1, b[1])
                turn_probs(0, b[0])
                score(1, b[1])
                weigh(0, b[0])
                turn_probs(1, b[1])
                weigh(1, b[1])
            pe.wait_ge(o_ready, NB)
            pe.wait_ge(merge_in, 1)
            for k in range(3):
                n = P if k < 2 else R
                src = at(merge0, 3 * 64)[0:n, 64 * k:64 * k + 64]
                m = mm(ps[0:NB, 0, 0:64], ones[0:n, 0:NB], src, start=(k == 0), stop=(k == 2))
            nc.tensor.transpose(ps[0:NB, 1, 0:P], stats[:, 0, :], ident)
            nc.tensor.transpose(ps[0:NB, 1, P:2 * P], stats[:, 1, :], ident).then_inc(pe_merge, 1)
            pe.wait_ge(merge_in, 3)
            nc.tensor.transpose(ps[:, 2, 0:NB], at(merge0 + 448, P)[0:NB, :], ident[0:NB, 0:NB])
            mm(ps[:, 3, 0:64], ones[0:NB, :], at(merge0 + 576, 64)[0:NB, :], start=True, stop=True).then_inc(pe_merge, 1)
            pe.wait_ge(merge_in, 5)
            for b in range(NB):
                for k in range(CT):
                    m = mm(ps[:, 4, (k * NB + b) * H:(k * NB + b) * H + H], o_part[:, b, P * k:P * k + P],
                           at(merge0 + 640, 64)[:, H * b:H * b + H], start=True, stop=True)
            m.then_inc(pe_merge, 1)
            pe.wait_ge(merge_in, 7)
            oL = at(merge0 + 768, CT * 64).rearrange("p (k b h) -> p k b h", k=CT, b=NB)
            for h in range(H):
                for k in range(CT):
                    m = mm(ps[:, 5, NB * h:NB * h + NB], w_uv[:, h, k, :], oL[:, k, :, h],
                           start=(k == 0), stop=(k == CT - 1))
            m.then_inc(pe_merge, 1)
            pe.wait_ge(merge_in, 8)

            def keys(h):
                if h >= 2:
                    pe.wait_ge(k_ready, h)
                for k in range(CT):
                    m = mm(ps[0:NO, 0, 0:LP], w_ukT[:, k, NO * h:NO * h + NO], cT[:, k, 0:LP],
                           start=(k == 0), stop=(k == CT - 1))
                m.then_inc(pe_k, 1)

            pe.wait_ge(kT_rope, 2)
            keys(0)
            for h in range(H):
                g = h // 4
                pe.wait_ge(k_ready, h + 1)
                if h:
                    pe.wait_ge(s_masked, h)
                    if h % 4 == 0:
                        pe.wait_ge(s2_masked, g)
                k = kT[:, h % 2, :]
                mm(ps[:, 1, 0:P], qT[:, h, 0:P], k[:, 0:P], start=True, stop=True)
                mm(ps[:, 1, P:3 * P], qT[:, h, P:2 * P], k[:, 0:2 * P], start=True, stop=True).then_inc(pe_s, 1)
                r = 32 * (h % 4)
                if h % 4 == 0 and g:
                    pe.wait_ge(a2_merged, g)
                mm(ps[r:r + 32, 7, 0:LP], qT[:, h, 2 * P:2 * P + 32], k, start=True, stop=True,
                   ).then_inc(pe_s, 1)
                if h % 2 == 0:
                    pe.wait_ge(in_gab[h // 2], 32)
                if h:
                    pe.wait_ge(gab_exp, h)
                w = slot[h // 2].rearrange("p (k u n) -> p k u n", k=KD, u=2)
                for u in range(2):
                    for kk in range(KD):
                        m = mm(ps[:, 4 + u, 0:T], w[:, kk, u, P * (h % 2):P * (h % 2) + P], hT[:, kk, :],
                               start=(kk == 0), stop=(kk == KD - 1))
                m.then_inc(pe_gab, 1)
                if h == 0:
                    pe.wait_ge(pooled_ready, G)
                    pe.wait_ge(p_sample, G + 1)
                    pe.wait_ge(in_pool, 16)
                else:
                    pe.wait_ge(y_merged, h)
                m = mm(ps[:, 6, 0:T], w_pool[:, h // 2, P * (h % 2):P * (h % 2) + P], pooled[:, h // 2, :],
                       start=True, stop=True)
                m.then_inc(pe_y, 1)
                if h + 1 < H:
                    keys(h + 1)
                pe.wait_ge(p_norm, h + 1)
                if h:
                    pe.wait_ge(pT_ready, h)
                E = probs[:, h % 2, :]
                nc.tensor.transpose(ps[:, 2, 0:P], E[:, 0:P], ident)
                nc.tensor.transpose(ps[:, 2, P:2 * P], E[:, P:2 * P], ident)
                nc.tensor.transpose(ps[:, 2, 2 * P:3 * P], E[:, 2 * P:3 * P], ident).then_inc(pe_pT, 1)
                pe.wait_ge(pT_ready, h + 1)
                if h:
                    pe.wait_ge(a_merged, h)
                ET = probsT[:, h % 2, :]
                mm(ps[:, 3, 0:2 * P], vals[:, 0, P * h:P * h + P], ET[:, 0:2 * P], start=True, stop=False,
                   skip_group_check=True)
                mm(ps[:, 3, P:2 * P], vals[:, 1, P * h:P * h + P], ET[:, 2 * P:3 * P], start=False, stop=True,
                   skip_group_check=True).then_inc(pe_a, 1)
                if h % 4 == 3:
                    pe.wait_ge(p2_norm, g + 1)
                    pe.wait_ge(pT_ready, h + 1)
                    E2 = probs_last
                    for kb in range(3):
                        n = P if kb < 2 else LAST
                        m = nc.tensor.transpose(ps[0:n, 2, P * kb:P * kb + P], E2[:, P * kb:P * kb + n], ident)
                    m.then_inc(pe_p2T, 1)
                    pe.wait_ge(p2T_ready, 2 * g + 2)
                    for hh in range(4):
                        for kb in range(3):
                            n = P if kb < 2 else LAST
                            m = mm(ps[:, 7, LAST * hh:LAST * hh + LAST],
                                   vals[0:n, kb, P * (4 * g + hh):P * (4 * g + hh) + P],
                                   probs2T[0:n, g, kb, 32 * hh:32 * hh + LAST], start=(kb == 0), stop=(kb == 2))
                    m.then_inc(pe_a2, 1)
                if h % 2:
                    pe.wait_ge(gab_exp, h + 1)
                    pe.sem_inc(slot_free[h // 2], 1)
            pe.wait_ge(a2_merged, 2)
            pe.wait_ge(y_merged, H)
            pe.wait_ge(a_merged, H)
            for n in range(2):
                pe.wait_ge(in_wo[n], 16)
                w = slot[4 + n].rearrange("p (k n) -> p k n", k=KD)
                for t in range(NT):
                    out = ps[:, 3 * n + t, :] if t < 2 else ps[0:ROWS[2], 3 * n + 2, :]
                    for k in range(KD):
                        m = mm(out, mT[:, k, P * t:P * t + ROWS[t]], w[:, k, :], start=(k == 0), stop=(k == KD - 1))
                    m.then_inc(pe_wo, 1)
                pe.wait_ge(x_mid, 3 * n + 3)
                pe.sem_inc(slot_free[4 + n], 1)
            pe.wait_ge(h2_ready, 1 + NT)
            for k in range(KD):
                if k >= 4:
                    pe.wait_ge(h2T_act if k % 2 == 0 else h2T_dve, (k - 4) // 2 + 1)
                for t in range(NT):
                    m = nc.tensor.transpose(ps[:, k % 4, P * t:P * t + ROWS[t]], h2[0:ROWS[t], t, P * k:P * k + P],
                                            ident[0:ROWS[t], 0:ROWS[t]])
                m.then_inc(pe_h2T, 1)
            pe.wait_ge(in_router, 32)
            pe.wait_ge(h2T_act, 4)
            pe.wait_ge(h2T_dve, 4)
            for t in range(NT):
                for k in range(KD):
                    m = mm(ps[0:ROWS[t], 4, NE * t:NE * t + NE], hT[:, k, P * t:P * t + ROWS[t]], w_rt[:, k, :],
                           start=(k == 0), stop=(k == KD - 1))
            m.then_inc(pe_logit, 1)
            pe.wait_ge(sel_ready, 1)
            for t in range(NT):
                for s in range(t + 1):
                    mm(ps[:, 5, NE * t:NE * t + NE], const["before"] if s == t else ones, sel[:, s, :],
                       start=(s == 0), stop=(s == t))
            for s in range(NT):
                m = mm(ps[0:1, 5, NE * NT:NE * NT + NE], ones[:, 0:1], sel[:, s, :], start=(s == 0), stop=(s == NT - 1))
            m.then_inc(pe_rank, 1)

            def gather(count):
                pe.wait_ge(pick_ready, count)
                for k in range(KD):
                    for t in range(NT):
                        m = mm(ps[:, 5, SL * k:SL * k + SL], h2[:, t, P * k:P * k + P], pick[:, t, :],
                               start=(t == 0), stop=(t == NT - 1))
                m.then_inc(pe_gather, 1)

            def expert(n, extra, ahead):
                if not ahead:
                    gather(n + extra + 1)
                pe.wait_ge(xg_ready, n + extra + 1)
                for c in range(4):
                    pe.wait_ge(in_chunk[c], 16 * n + 16)
                    w = slot[c].rearrange("p (k g u n) -> p k g u n", k=2, g=2, u=2)
                    for kk in range(2):
                        k = 2 * c + kk
                        for g in range(2):
                            for u in range(2):
                                m = mm(ps[SL * u:SL * u + SL, g, :], xg[:, k, :], w[:, kk, g, u, :],
                                       start=(k == 0), stop=False, skip_group_check=True)
                    m.then_inc(slot_free[c], 1)
                pe.wait_ge(in_bias, 32 * n + 32)
                for g in range(2):
                    m = mm(ps[:, g, :], half, bias[:, g, :], start=False, stop=True, skip_group_check=True)
                m.then_inc(pe_gu, 1)
                pe.wait_ge(pickg_ready, n + extra + 1)
                for t in range(NT):
                    m = nc.tensor.transpose(ps[:, 2, P * t:P * t + P], pickg[:, t, :, :].rearrange("p u s -> p (u s)"),
                                            ident)
                m.then_inc(pe_pick, 1)
                pe.wait_ge(hid_ready, n + 1)
                for j in range(4):
                    m = nc.tensor.transpose(ps[:, 3, P * j:P * j + P], hid[:, P * j:P * j + P], ident)
                m.then_inc(pe_hidT, 1)
                pe.wait_ge(hidT_ready, n + 1)
                for c in range(2):
                    pe.wait_ge(in_chunk[4 + c], 16 * n + 16)
                    w = slot[4 + c].rearrange("p (k u n) -> p k u n", k=4, u=2)
                    for kk in range(4):
                        for u in range(2):
                            m = mm(ps[SL * u:SL * u + SL, 4, :], hidT[:, kk, SL * c:SL * c + SL], w[:, kk, u, :],
                                   start=(c == 0 and kk == 0), stop=False, skip_group_check=True)
                    m.then_inc(slot_free[4 + c], 1)
                mm(ps[:, 4, :], half, bias[:, 2, :], start=False, stop=True, skip_group_check=True).then_inc(pe_down, 1)
                if ahead:
                    gather(n + 2)
                pe.wait_ge(ye_ready, n + 1)
                pe.wait_ge(pickT_ready, n + 1)
                for t in range(NT):
                    if t != 1:
                        pe.wait_ge(y_added, 3 * n + t // 2)
                    first = 6 if t != 1 else 0
                    for u in range(2):
                        m = mm(ps[:, first + u, :], pickT[SL * u:SL * u + SL, t, :], ye[SL * u:SL * u + SL, :],
                               start=True, stop=True)
                    m.then_inc(pe_comb, 1)
                pe.wait_ge(y_added, 3 * n + 2)

            gather(1)
            with pe.Fori(0, NE) as e:
                expert(e, 0, True)
            pe.wait_ge(most_ready, 1)
            count = pe.value_load(most_i[0:1, 0:1], min_val=0, max_val=T)
            with pe.If(count > SL):
                with pe.Fori(0, PASSES - 1) as j:
                    with pe.Fori(0, NE) as e:
                        expert(j * NE + e + NE, 1, False)

        def row_norm(act, n0):
            for t in range(NT):
                act.activation(sq_junk2[0:ROWS[t], :], x[0:ROWS[t], t, :], ACT.Square,
                               accum_out=small[0:ROWS[t], t:t + 1]).then_inc(sumsq, 1)
                act.wait_ge(sumsq, 3 * n0 + t + 1)
            act.wait_ge(meansq, n0 + 1 if n0 == 0 else n0 + 3)
            act.activation(small[:, 8:8 + NT], small[:, 4:4 + NT], ACT.Sqrt).then_inc(root, 1)

        sq_junk2 = xn[:, 0, :]

        @block.scalar
        def _(act):
            def copy(out, in_):
                return act.activation(out, in_, ACT.Copy)

            for r0, name, n in ((0, "norm1_g", KD), (KD, "pool_scale", KD), (2 * KD, "q_norm_g", CT),
                                (2 * KD + CT, "kv_norm_g", CT)):
                act.dma_start(vrow[r0:r0 + n, :], a[name].rearrange("l (k p) -> (l k) p", p=P)).then_inc(in_vec, 16)
            act.dma_start(pt, a["page_table"].rearrange("(a b) s -> a (b s)", a=1).to_broadcast([P, NB * PAGES])
                          ).then_inc(in_pt, 16)
            act.wait_ge(in_x, 80)
            act.wait_ge(x_zero, 1)
            row_norm(act, 0)
            act.wait_ge(pe_vec, 1)
            copy(vecT, ps[:, 7, 0:VECS]).then_inc(vec_ready, 1)
            act.wait_ge(vec_ready, 1)
            for k in range(0, KD, 2):
                act.wait_ge(pe_hT, k + 1)
                act.activation(hT[:, k, :], ps[:, k % 4, 0:T], ACT.Copy, scale=vecT[:, k:k + 1]).then_inc(hT_act, 1)
            for j in range(4):
                act.wait_ge(z_copied, j + 1)
                act.activation(zsq[:, j, :], zT[:, j, :], ACT.Square).then_inc(zsq_ready, 1)
            for k in range(CT):
                act.wait_ge(pe_ukT, k + 1)
                copy(w_ukT[:, k, :], ps[:, 3 + k, :]).then_inc(ukT_ready, 1)
            for j in range(2):
                act.wait_ge(meansq, 2 + j)
                act.activation(r_bc[:, j, :], r_bc[:, j, :], ACT.Sqrt).then_inc(root, 1)
            act.wait_ge(pe_hist, 1)
            copy(s_ext[:, :, :, 0:HIST], ps[:, 5, :].rearrange("p (g n) -> p g n", g=G)[:, :, 0:NB * HIST]
                 .rearrange("p g (b t) -> p g b t", b=NB)).then_inc(hist_ready, 1)
            act.wait_ge(pe_kr, 1)
            copy(krT, ps[:, 0, 0:T]).then_inc(kr_ready, 1)
            act.wait_ge(kr_ready, 1)
            for u in range(2):
                copy(kT[NO:P, u, :], krT[NO:P, 0:LP]).then_inc(kT_rope, 1)
            for g in range(G):
                act.wait_ge(pe_p, g + 1)
                copy(p_ext[:, g, 16:16 + LP], ps[:, 6 + g % 2, 0:LP]).then_inc(p_prompt, 1)
            for j in range(6):
                act.wait_ge(pe_v, j + 1)
                rows = P if j < 4 else LAST
                copy(vals[0:rows, j // 2, 512 * (j % 2):512 * (j % 2) + 512], ps[0:rows, 1 + j % 4, :]
                     ).then_inc(v_ready, 1)

            act.wait_ge(prow_ready, 1)
            act.dma_start(o["pool_p"][0, 0, :, :], p_rows).then_inc(out_pool, 16)
            act.dma_start(o["pool_s"][0, :, HIST - 1, :], s_rows).then_inc(out_pool, 16)
            act.wait_ge(cout_ready, 3)
            for dst, col, n in (("ckv", 0, C), ("krope", C, R)):
                act.dma_start(o[dst + "_p"][0, 0, 0:P, :], c_out[:, 0, col:col + n]).then_inc(out_small, 16)
                act.dma_start(o[dst + "_p"][0, 0, P:2 * P, :], c_out[:, 1, col:col + n]).then_inc(out_small, 16)
                act.dma_start(o[dst + "_p"][0, 0, 2 * P:LP, :], c_out[0:LAST, 2, col:col + n]).then_inc(out_small, 16)
                act.dma_start(o[dst + "_s"][0, :, 0, :], c_out[LAST:LAST + NB, 2, col:col + n]).then_inc(out_small, 16)

            act.wait_ge(pooled_ready, G)

            def take_keys(u, b):
                act.wait_ge(s_done, b)
                for s in range(4):
                    act.wait_ge(pe_kt, 4 * b + s + 1)
                    copy(keysT[:, 0, 512 * s:512 * s + 512], ps[:, 3 * (s % 2), :]).then_inc(kt_act, 1)
                    if s % 2:
                        copy(keysT[0:R, 2, 512 * s:512 * s + 512], ps[0:R, 3 * (s % 2) + 2, :]).then_inc(kt_act, 1)

            def exponents(u, b):
                act.wait_ge(s_max, 2 * b + 2)
                act.activation(probs[:, u, :], ps[:, 6, :], ACT.Exp, bias=small[:, 12 + u:13 + u], scale=SCALE,
                               accum_out=small[:, 14 + u:15 + u]).then_inc(e_ready, 1)

            def take_probs(u, b):
                act.wait_ge(pe_pt, b + 1)
                copy(probsT[:, u, :], ps[:, 7, :]).then_inc(pt_ready, 1)

            def take_out(u, b):
                act.wait_ge(pv_done, b + 1)
                copy(o_part[:, bass.ds(b, 1), :].rearrange("p b c -> p (b c)"), ps[:, u, 0:C]).then_inc(o_ready, 1)

            with act.Fori(0, NB // 2) as i:
                b = [2 * i, 2 * i + 1]
                take_keys(0, b[0])
                exponents(0, b[0])
                take_keys(1, b[1])
                take_probs(0, b[0])
                exponents(1, b[1])
                take_out(0, b[0])
                take_probs(1, b[1])
                take_out(1, b[1])
            act.wait_ge(merge_in, 2)
            act.activation(at(merge0 + 320, P)[0:NB, :], at(merge0 + 192, P)[0:NB, :], ACT.Exp,
                           scale=SCALE).then_inc(merge_act, 1)
            act.activation(at(merge0 + 904, 32)[0:NB, 0:H], at(merge0 + 896, 8)[0:NB, :], ACT.Exp,
                           scale=SCALE).then_inc(merge_act, 1)
            for h in range(H):
                if h == 0:
                    act.wait_ge(pe_k, 1)
                    copy(kT[0:NO, 0, :], ps[0:NO, 0, 0:LP]).then_inc(k_ready, 1)
                act.wait_ge(s_masked, h + 1)
                for j, (lo, hi) in enumerate(((0, P), (P, 3 * P))):
                    e = probs[:, h % 2, lo:hi]
                    act.activation(e, e, ACT.Exp, bias=small[:, 20 + j:21 + j], scale=SCALE,
                                   accum_out=small[:, 24 + j:25 + j]).then_inc(p_exp, 1)
                if h % 4 == 3:
                    act.wait_ge(s2_masked, h // 4 + 1)
                    act.activation(probs_last, probs_last, ACT.Exp, bias=small[:, 28:29], scale=SCALE,
                                   accum_out=small[:, 30:31]).then_inc(p2_exp, 1)
                act.wait_ge(pe_gab, h + 1)
                if h:
                    act.wait_ge(a_merged, h)
                act.activation(sig[:, :, :], ps[:, 4:6, 0:T], ACT.Exp, scale=-1.0).then_inc(gab_exp, 1)
                if h + 1 < H:
                    act.wait_ge(pe_k, h + 2)
                    copy(kT[0:NO, (h + 1) % 2, :], ps[0:NO, 0, 0:LP]).then_inc(k_ready, 1)
                act.wait_ge(pe_pT, h + 1)
                copy(probsT[:, h % 2, 0:3 * P], ps[:, 2, 0:3 * P]).then_inc(pT_ready, 1)
                if h % 4 == 3:
                    g = h // 4
                    act.wait_ge(pe_p2T, g + 1)
                    copy(probs2T[:, g, 0:2, :], ps[:, 2, 0:2 * P].rearrange("p (k q) -> p k q", k=2)
                         ).then_inc(p2T_ready, 1)
                    copy(probs2T[0:LAST, g, 2, :], ps[0:LAST, 2, 2 * P:3 * P]).then_inc(p2T_ready, 1)
            act.wait_ge(pe_k, H)
            act.dma_start(norm2_g, a["norm2_g"].to_broadcast([P, D])).then_inc(in_g2, 16)
            act.wait_ge(x_mid, 6)
            row_norm(act, 1)
            for k in range(0, KD, 2):
                act.wait_ge(pe_h2T, k + 1)
                copy(hT[:, k, :], ps[:, k % 4, 0:T]).then_inc(h2T_act, 1)
            act.wait_ge(top_ready, 1)
            act.activation(rt[:, 1, :, :], rt[:, 0, :, :], ACT.Exp).then_inc(e_top, 1)

            def take_gathered(count):
                act.wait_ge(pe_gather, count)
                copy(xg, ps[:, 5, :].rearrange("p (k s) -> p k s", k=KD)).then_inc(xg_ready, 1)

            def expert(n, extra, ahead):
                if not ahead:
                    take_gathered(n + extra + 1)
                act.wait_ge(gate_ready, n + 1)
                act.activation(sgm, gate, ACT.Sigmoid, scale=ALPHA).then_inc(sgm_ready, 1)
                act.wait_ge(pe_pick, n + 1)
                act.wait_ge(pe_comb, 3 * n)
                copy(pickT, ps[:, 2, 0:NT * P].rearrange("p (t n) -> p t n", t=NT)).then_inc(pickT_ready, 1)
                act.wait_ge(pe_hidT, n + 1)
                copy(hidT, ps[:, 3, :].rearrange("p (j n) -> p j n", j=4)).then_inc(hidT_ready, 1)
                act.wait_ge(pe_down, n + 1)
                copy(ye, ps[:, 4, :]).then_inc(ye_ready, 1)
                if ahead:
                    take_gathered(n + 2)

            take_gathered(1)
            with act.Fori(0, NE) as e:
                expert(e, 0, True)
            act.wait_ge(most_ready, 1)
            count = act.value_load(most_i[0:1, 0:1], min_val=0, max_val=T)
            with act.If(count > SL):
                with act.Fori(0, PASSES - 1) as j:
                    with act.Fori(0, NE) as e:
                        expert(j * NE + e + NE, 1, False)
            act.wait_ge(y_final, 1)
            row_norm(act, 2)

        @block.vector
        def _(dve):
            steps = [0]

            def link(ins):
                steps[0] += 1
                ins.then_inc(dve_step, 1)
                dve.wait_ge(dve_step, steps[0])

            def row_scale(n0):
                dve.wait_ge(sumsq, 3 * n0 + 3)
                dve.tensor_scalar(small[:, 4:4 + NT], small[:, 0:NT], 1.0 / D, EPS, ALU.mult, ALU.add
                                  ).then_inc(meansq, 1)
                dve.wait_ge(root, n0 + 1 if n0 == 0 else n0 + 3)
                link(dve.reciprocal(small[:, 16:16 + NT], small[:, 8:8 + NT]))

            link(dve.memset(small, 1.0))
            dve.memset(x[:, 2, :], 0.0).then_inc(x_zero, 1)
            dve.wait_ge(in_pt, 16)
            dve.wait_ge(in_const, 16)
            for g in range(4):
                q = slice(32 * g, 32 * g + 32)
                dve.tensor_scalar(idx[q, :], pt[q, g::4], 32.0, const["mod32"][q, :], ALU.mult, ALU.add
                                  ).then_inc(idx_ready, 1)
            row_scale(0)
            for t in range(NT):
                n = ROWS[t]
                dve.tensor_scalar(xn[0:n, t, :], x[0:n, t, :], small[0:n, 16 + t:17 + t], None, ALU.mult
                                  ).then_inc(xn_ready, 1)
            dve.wait_ge(vec_ready, 1)
            for k in range(1, KD, 2):
                dve.wait_ge(pe_hT, k + 1)
                dve.tensor_scalar(hT[:, k, :], ps[:, k % 4, 0:T], vecT[:, k:k + 1], None, ALU.mult).then_inc(hT_dve, 1)
            for j in range(4):
                dve.wait_ge(pe_z, j + 1)
                dve.tensor_copy(zT[:, j, :], ps[:, 4 + j, 0:T]).then_inc(z_copied, 1)
            dve.wait_ge(pe_z, 5)
            dve.tensor_tensor(kr_cs[0:2 * R, :], ps[0:2 * R, 0, 0:T], const["rope0"][0:2 * R, :], ALU.mult
                              ).then_inc(kr_rot, 1)
            for j in range(2):
                dve.wait_ge(pe_stat, j + 1)
                dve.tensor_scalar(r_bc[:, j, :], ps[:, 1 + j, 0:T], 1.0 / C, EPS, ALU.mult, ALU.add
                                  ).then_inc(meansq, 1)
            for j in range(2):
                dve.wait_ge(root, 2 + j)
                dve.reciprocal(r_bc[:, j, :], r_bc[:, j, :]).then_inc(r_ready, 1)
            dve.wait_ge(r_ready, 2)
            dve.wait_ge(z_copied, 4)
            link(dve.tensor_tensor(rope_q, const["rope"], r_bc[:, 0, :], ALU.mult))
            for k in range(CT):
                col = 2 * KD + CT + k
                dve.scalar_tensor_tensor(out=cT[:, k, :], in0=zT[:, 2 + k, :], scalar=vecT[:, col:col + 1],
                                         in1=r_bc[:, 1, :], op0=ALU.mult, op1=ALU.mult).then_inc(c_ready, 1)
            for g in range(G):
                dve.wait_ge(p_prompt, g + 1)
                dve.tensor_copy(s_ext[:, g, :, HIST], ps[:, 6 + g % 2, LP:T]).then_inc(p_sample, 1)
            for h in range(H):
                dve.wait_ge(pe_q, h + 1)
                dve.tensor_tensor(qT[:, h, 0:T], ps[:, 1 + h % 4, 0:T], rope_q, ALU.mult).then_inc(q_ready, 1)
            dve.wait_ge(pe_prow, 1)
            link(dve.tensor_copy(p_rows[0:HIST, :], ps[0:HIST, 5, :]))
            dve.tensor_copy(s_rows[0:NB, :], ps[0:NB, 6, :]).then_inc(prow_ready, 1)
            dve.wait_ge(hist_ready, 1)
            dve.wait_ge(p_sample, G)
            for g in range(G):
                w = 2 << g
                link(dve.tensor_reduce(small[:, 32:32 + NB], s_ext[:, g, :, 16 - w:16], AX.X, ALU.add))
                m = dve.scalar_tensor_tensor(out=pooled[:, g, LP:T], in0=small[:, 32:32 + NB], scalar=1.0 / w,
                                             in1=s_ext[:, g, :, HIST], op0=ALU.mult, op1=ALU.subtract)
                if g < G - 1:
                    link(m)
            m.then_inc(p_sample, 1)
            dve.wait_ge(pe_ql, 2)
            dve.wait_ge(zeros_ready, 4)
            for k in range(CT):
                dve.tensor_copy(qL[:, k, :, 0:H], ps[:, 7, k * 64:k * 64 + 64].rearrange("p (h b) -> p b h", h=H)
                                ).then_inc(ql_ready, 1)
            dve.tensor_copy(qR[0:R, :, 0:H], ps[0:R, 0, 0:64].rearrange("p (h b) -> p b h", h=H)).then_inc(ql_ready, 1)
            for t in range(NT):
                dve.wait_ge(pe_cout, t + 1)
                dve.tensor_copy(c_out[0:ROWS[t], t, :], ps[0:ROWS[t], 5 + t, 0:C + R]).then_inc(cout_ready, 1)
            dve.wait_ge(ql_ready, 3)

            def take_keys(u, b):
                dve.wait_ge(s_done, b)
                dve.tensor_copy(qLb[:, u, :, :], qL[:, :, bass.ds(b, 1), :].rearrange("p k b h -> p k (b h)")
                                ).then_inc(q_batch, 1)
                dve.tensor_copy(qRb[0:R, u, :], qR[0:R, bass.ds(b, 1), :].rearrange("p b h -> p (b h)")
                                ).then_inc(q_batch, 1)
                for s in range(4):
                    dve.wait_ge(pe_kt, 4 * b + s + 1)
                    dve.tensor_copy(keysT[:, 1, 512 * s:512 * s + 512], ps[:, 3 * (s % 2) + 1, :]).then_inc(kt_dve, 1)
                    if s % 2 == 0:
                        dve.tensor_copy(keysT[0:R, 2, 512 * s:512 * s + 512], ps[0:R, 3 * (s % 2) + 2, :]
                                        ).then_inc(kt_dve, 1)

            def maxima(u, b):
                dve.wait_ge(s_done, b + 1)
                dve.tensor_reduce(stats[:, 0, bass.ds(b, 1)], ps[:, 6, :], AX.X, ALU.max).then_inc(s_max, 1)
                dve.wait_ge(s_max, 2 * b + 1)
                dve.tensor_scalar(small[:, 12 + u:13 + u], stats[:, 0, bass.ds(b, 1)], -SCALE, None, ALU.mult
                                  ).then_inc(s_max, 1)

            def sums(u, b):
                dve.wait_ge(e_ready, b + 1)
                dve.tensor_copy(stats[:, 1, bass.ds(b, 1)], small[:, 14 + u:15 + u]).then_inc(sum_kept, 1)

            with dve.Fori(0, NB // 2) as i:
                b = [2 * i, 2 * i + 1]
                take_keys(0, b[0])
                maxima(0, b[0])
                take_keys(1, b[1])
                sums(0, b[0])
                maxima(1, b[1])
                sums(1, b[1])
            dve.wait_ge(sum_kept, NB)
            dve.wait_ge(o_ready, NB)
            prod = at(merge0, 3 * 64)
            for k in range(CT):
                link(dve.tensor_tensor(prod[:, 64 * k:64 * k + 64].rearrange("p (b h) -> p b h", b=NB),
                                       qL[:, k, :, 0:H], cT[:, k, LP:T].unsqueeze(2).to_broadcast([P, NB, H]),
                                       ALU.mult))
            dve.tensor_tensor(prod[0:R, 128:192].rearrange("p (b h) -> p b h", b=NB), qR[0:R, :, 0:H],
                              krT[0:R, LP:T].unsqueeze(2).to_broadcast([R, NB, H]), ALU.mult).then_inc(merge_in, 1)
            dve.wait_ge(pe_merge, 1)
            sN = at(merge0 + 912 + 32, 8)[0:NB, :]
            top1 = at(merge0 + 912 + 40, 8)[0:NB, :]
            tmp = at(merge0 + 192, P)[0:NB, :]
            link(dve.tensor_tensor(tmp[:, 0:64], ps[0:NB, 0, 0:64], const["diag"][0:NB, :], ALU.mult))
            link(dve.tensor_reduce(sN, tmp[:, 0:64].rearrange("p (b h) -> p h b", b=NB), AX.X, ALU.add))
            mx = ps[0:NB, 1, 0:P].rearrange("p (s h) -> p s h", s=4)
            link(dve.tensor_reduce(top1, mx[:, :, 0:H].rearrange("p s h -> p h s"), AX.X, ALU.max))
            link(dve.tensor_tensor(top1, top1, sN, ALU.max))
            link(dve.memset(tmp, 0.0))
            link(dve.tensor_tensor(tmp.rearrange("p (s h) -> p s h", s=4)[:, :, 0:H], mx[:, :, 0:H],
                                   top1.unsqueeze(1).to_broadcast([NB, 4, H]), ALU.subtract))
            dve.tensor_tensor(at(merge0 + 896, 8)[0:NB, :], sN, top1, ALU.subtract).then_inc(merge_in, 1)
            dve.wait_ge(merge_act, 2)
            w4 = at(merge0 + 320, P)[0:NB, :]
            wN = at(merge0 + 904, 32)[0:NB, 0:H]
            den = at(merge0 + 912 + 48, 8)[0:NB, :]
            link(dve.tensor_tensor(tmp, w4, ps[0:NB, 1, P:2 * P], ALU.mult))
            link(dve.tensor_reduce(den, tmp.rearrange("p (s h) -> p s h", s=4)[:, :, 0:H]
                                   .rearrange("p s h -> p h s"), AX.X, ALU.add))
            link(dve.tensor_tensor(den, den, wN, ALU.add))
            link(dve.reciprocal(den, den))
            wrow = at(merge0 + 448, P)[0:NB, :]
            link(dve.memset(wrow, 0.0))
            link(dve.tensor_tensor(wrow.rearrange("p (s h) -> p s h", s=4)[:, :, 0:H],
                                   w4.rearrange("p (s h) -> p s h", s=4)[:, :, 0:H],
                                   den.unsqueeze(1).to_broadcast([NB, 4, H]), ALU.mult))
            link(dve.tensor_tensor(wN, wN, den, ALU.mult))
            dve.tensor_tensor(at(merge0 + 576, 64)[0:NB, :].rearrange("p (b h) -> p b h", b=NB),
                              const["diag"][0:NB, :].rearrange("p (b h) -> p b h", b=NB),
                              wN.unsqueeze(1).to_broadcast([NB, NB, H]), ALU.mult).then_inc(merge_in, 1)
            dve.wait_ge(pe_merge, 2)
            wcol = at(merge0 + 704, 8)
            dve.tensor_copy(wcol, ps[:, 2, 0:NB]).then_inc(merge_in, 1)
            dve.wait_ge(merge_in, 4)
            dve.tensor_tensor(at(merge0 + 640, 64).rearrange("p (b h) -> p b h", b=NB),
                              const["headsel"].unsqueeze(1).to_broadcast([P, NB, H]),
                              wcol.unsqueeze(2).to_broadcast([P, NB, H]), ALU.mult).then_inc(merge_in, 1)
            dve.wait_ge(pe_merge, 3)
            oL = at(merge0 + 768, CT * 64)
            dve.tensor_tensor(prod[:, 0:128].rearrange("p (k b h) -> p k b h", k=CT, b=NB),
                              cT[:, :, LP:T].unsqueeze(3).to_broadcast([P, CT, NB, H]),
                              ps[:, 3, 0:64].rearrange("p (b h) -> p b h", b=NB).unsqueeze(1).to_broadcast([P, CT, NB, H]), ALU.mult).then_inc(merge_in, 1)
            dve.wait_ge(merge_in, 6)
            dve.tensor_tensor(oL, prod[:, 0:128], ps[:, 4, 0:128], ALU.add).then_inc(merge_in, 1)
            dve.wait_ge(merge_in, 7)
            dve.wait_ge(pe_merge, 4)
            dve.tensor_copy(aS, ps[:, 5, 0:64].rearrange("p (h b) -> p h b", h=H)).then_inc(merge_in, 1)
            dve.wait_ge(merge_in, 8)
            dve.wait_ge(out_pool, 32)

            for h in range(H):
                E = probs[:, h % 2, :]
                dve.wait_ge(pe_s, 2 * h + 1)
                if h >= 2:
                    dve.wait_ge(pe_pT, h - 1)
                m1 = const["mask1"]
                link(dve.tensor_tensor_reduce(E[:, 0:P], ps[:, 1, 0:P], m1[:, P:2 * P], 1.0, NEG, ALU.add, ALU.max,
                                              small[:, 18:19]))
                link(dve.tensor_tensor_reduce(E[:, P:3 * P], ps[:, 1, P:3 * P], m1, 1.0, NEG, ALU.add, ALU.max,
                                              small[:, 19:20]))
                if h:
                    dve.wait_ge(p_exp, 2 * h)
                dve.tensor_scalar(small[:, 20:22], small[:, 18:20], -SCALE, None, ALU.mult).then_inc(s_masked, 1)
                dve.wait_ge(p_exp, 2 * h + 2)
                link(dve.reciprocal(small[:, 26:28], small[:, 24:26]))
                link(dve.tensor_scalar(E[:, 0:P], E[:, 0:P], small[:, 26:27], None, ALU.mult))
                dve.tensor_scalar(E[:, P:3 * P], E[:, P:3 * P], small[:, 27:28], None, ALU.mult).then_inc(p_norm, 1)
                if h % 4 == 3:
                    g = h // 4
                    dve.wait_ge(pe_s, 2 * h + 2)
                    link(dve.tensor_tensor_reduce(probs_last, ps[:, 7, 0:LP], const["mask2"], 1.0, NEG, ALU.add,
                                                  ALU.max, small[:, 29:30]))
                    dve.tensor_scalar(small[:, 28:29], small[:, 29:30], -SCALE, None, ALU.mult).then_inc(s2_masked, 1)
                    dve.wait_ge(p2_exp, g + 1)
                    link(dve.reciprocal(small[:, 31:32], small[:, 30:31]))
                    dve.tensor_scalar(probs_last, probs_last, small[:, 31:32], None, ALU.mult).then_inc(p2_norm, 1)
                dve.wait_ge(gab_exp, h + 1)
                link(dve.tensor_scalar(sig[:, :, :], sig[:, :, :], 1.0, None, ALU.add))
                link(dve.reciprocal(sig[:, :, :], sig[:, :, :]))
                dve.wait_ge(pe_y, h + 1)
                dve.scalar_tensor_tensor(out=mT[:, h, :], in0=ps[:, 6, 0:T], scalar=vecT[:, KD + h:KD + h + 1],
                                         in1=sig[:, 1, :], op0=ALU.mult, op1=ALU.mult).then_inc(y_merged, 1)
                dve.wait_ge(y_merged, h + 1)
                link(dve.tensor_copy(sga_last[:, h, :], sig[:, 0, 2 * P:LP]))
                link(dve.tensor_tensor(small[:, 48:48 + NB], aS[:, h, :], sig[:, 0, LP:T], ALU.mult))
                link(dve.tensor_tensor(mT[:, h, LP:T], mT[:, h, LP:T], small[:, 48:48 + NB], ALU.add))
                dve.wait_ge(pe_a, h + 1)
                link(dve.tensor_tensor(sig[:, 0, 0:2 * P], ps[:, 3, 0:2 * P], sig[:, 0, 0:2 * P], ALU.mult))
                dve.tensor_tensor(mT[:, h, 0:2 * P], mT[:, h, 0:2 * P], sig[:, 0, 0:2 * P], ALU.add
                                  ).then_inc(a_merged, 1)
                if h % 4 == 3:
                    g = h // 4
                    last = small2.rearrange("p (h t) -> p h t", h=4)
                    dve.wait_ge(pe_a2, g + 1)
                    link(dve.tensor_tensor(last, ps[:, 7, 0:4 * LAST].rearrange("p (h t) -> p h t", h=4),
                                           sga_last[:, 4 * g:4 * g + 4, :], ALU.mult))
                    dve.tensor_tensor(mT[:, 4 * g:4 * g + 4, 2 * P:LP], mT[:, 4 * g:4 * g + 4, 2 * P:LP], last,
                                      ALU.add).then_inc(a2_merged, 1)
            for j in range(6):
                n, t = j // 3, j % 3
                dve.wait_ge(pe_wo, j + 1)
                xr = x[0:ROWS[t], t, 512 * n:512 * n + 512]
                dve.tensor_tensor(xr, xr, ps[0:ROWS[t], j, :], ALU.add).then_inc(x_mid, 1)
            dve.wait_ge(x_mid, 6)
            row_scale(1)
            dve.wait_ge(in_g2, 16)
            dve.memset(h2[:, 2, :], 0.0).then_inc(h2_ready, 1)
            dve.wait_ge(h2_ready, 1)
            for t in range(NT):
                n = ROWS[t]
                dve.scalar_tensor_tensor(out=h2[0:n, t, :], in0=x[0:n, t, :], scalar=small[0:n, 16 + t:17 + t],
                                         in1=norm2_g[0:n, :], op0=ALU.mult, op1=ALU.mult).then_inc(h2_ready, 1)
            for k in range(1, KD, 2):
                dve.wait_ge(pe_h2T, k + 1)
                dve.tensor_copy(hT[:, k, :], ps[:, k % 4, 0:T]).then_inc(h2T_dve, 1)
            dve.wait_ge(out_small, 144)
            link(dve.memset(lg, 0.0))
            dve.wait_ge(pe_logit, 1)
            dve.wait_ge(in_router, 32)
            for t in range(NT):
                n = ROWS[t]
                link(dve.tensor_tensor(lg[0:n, t, :], ps[0:n, 4, NE * t:NE * t + NE], b_rt[0:n, :], ALU.add))
            for t in range(NT):
                link(dve.max(top8[:, t, :], lg[:, t, :]))
            best = top8[:, :, 0:1].to_broadcast([P, NT, NE])
            fourth = top8[:, :, 3:4].to_broadcast([P, NT, NE])
            dve.tensor_tensor(rt[:, 0, :, :], lg, best, ALU.subtract).then_inc(top_ready, 1)
            link(dve.tensor_tensor(rt[:, 2, :, :], lg, fourth, ALU.is_gt))
            link(dve.tensor_tensor(rt[:, 3, :, :], lg, fourth, ALU.is_equal))
            left = small[:, 36:36 + NT]
            link(dve.tensor_reduce(left, rt[:, 2, :, :], AX.X, ALU.add))
            link(dve.tensor_scalar(left, left, -1.0, 4.0, ALU.mult, ALU.add))
            for t in range(NT):
                link(dve.tensor_tensor_scan(sel[:, t, :], rt[:, 3, t, :], rt[:, 3, t, :], 0.0, ALU.add, ALU.max))
            link(dve.tensor_tensor(sel, sel, left.unsqueeze(2).to_broadcast([P, NT, NE]), ALU.is_le))
            link(dve.tensor_tensor(sel, sel, rt[:, 3, :, :], ALU.mult))
            link(dve.tensor_tensor(sel, sel, rt[:, 2, :, :], ALU.add))
            dve.tensor_tensor(sel, sel, const["valid"].unsqueeze(2).to_broadcast([P, NT, NE]), ALU.mult
                              ).then_inc(sel_ready, 1)
            dve.wait_ge(sel_ready, 1)
            dve.wait_ge(e_top, 1)
            link(dve.memset(gates, 0.0))
            link(dve.memset(rank, -1.0))
            link(dve.tensor_tensor(rt[:, 2, :, :], rt[:, 1, :, :], sel, ALU.mult))
            link(dve.tensor_reduce(left, rt[:, 2, :, :], AX.X, ALU.add))
            link(dve.tensor_scalar(left, left, 1.0e-30, None, ALU.max))
            link(dve.reciprocal(left, left))
            link(dve.tensor_tensor(gates[:, :, 0:NE], rt[:, 2, :, :], left.unsqueeze(2).to_broadcast([P, NT, NE]),
                                   ALU.mult))
            dve.wait_ge(pe_rank, 1)
            pr = ps[:, 5, 0:NT * NE].rearrange("p (t e) -> p t e", t=NT)
            link(dve.scalar_tensor_tensor(out=rank[:, :, 0:NE], in0=pr, scalar=1.0, in1=sel, op0=ALU.add,
                                          op1=ALU.mult))
            dve.tensor_scalar(rank[:, :, 0:NE], rank[:, :, 0:NE], -1.0, None, ALU.add).then_inc(rank_ready, 1)
            link(dve.tensor_reduce(most[0:1, 0:1], ps[0:1, 5, NT * NE:NT * NE + NE], AX.X, ALU.max))
            dve.tensor_copy(most_i[0:1, 0:1], most[0:1, 0:1]).then_inc(most_ready, 1)
            dve.wait_ge(rank_ready, 1)

            def choose(e, count, first):
                iota = const["iota"][:, first].unsqueeze(1).to_broadcast([P, NT, SL])
                dve.tensor_tensor(pick, iota, rank[:, :, e].to_broadcast([P, NT, SL]), ALU.is_equal
                                  ).then_inc(pick_ready, 1)
                dve.wait_ge(pick_ready, count)
                dve.tensor_tensor(pickg, pick.unsqueeze(2).to_broadcast([P, NT, 2, SL]),
                                  gates[:, :, e].unsqueeze(2).to_broadcast([P, NT, 2, SL]), ALU.mult
                                  ).then_inc(pickg_ready, 1)

            def expert(e, n, extra, first, ahead):
                if not ahead:
                    choose(bass.ds(e, 1), n + extra + 1, first)
                dve.wait_ge(pe_gu, n + 1)
                dve.tensor_scalar(gate, ps[:, 0, :], LIMIT, None, ALU.min).then_inc(gate_ready, 1)
                dve.tensor_scalar(up, ps[:, 1, :], LIMIT, -LIMIT, ALU.min, ALU.max).then_inc(up_ready, 1)
                dve.wait_ge(gate_ready, n + 1)
                dve.wait_ge(up_ready, n + 1)
                dve.scalar_tensor_tensor(out=upg, in0=up, scalar=1.0, in1=gate, op0=ALU.add, op1=ALU.mult
                                         ).then_inc(upg_ready, 1)
                dve.wait_ge(upg_ready, n + 1)
                dve.wait_ge(sgm_ready, n + 1)
                dve.tensor_tensor(hid, upg, sgm, ALU.mult).then_inc(hid_ready, 1)
                if ahead:
                    dve.wait_ge(pe_gather, n + 1)
                    dve.wait_ge(pe_pick, n + 1)
                    choose(bass.ds(e + 1, 1), n + 2, first)
                dve.wait_ge(y_added, 3 * n)
                for t in range(NT):
                    dve.wait_ge(pe_comb, 3 * n + t + 1)
                    b0 = 6 if t != 1 else 0
                    dve.tensor_tensor(x[:, t, :], x[:, t, :], ps[:, b0:b0 + 2, :].rearrange("p b n -> p (b n)"),
                                      ALU.add).then_inc(y_added, 1)

            choose(slice(0, 1), 1, slice(0, SL))
            with dve.Fori(0, NE) as e:
                expert(e, e, 0, slice(0, SL), True)
            dve.wait_ge(y_added, 3 * NE)
            dve.wait_ge(most_ready, 1)
            count = dve.value_load(most_i[0:1, 0:1], min_val=0, max_val=T)
            with dve.If(count > SL):
                with dve.Fori(0, PASSES - 1) as j:
                    with dve.Fori(0, NE) as e:
                        expert(e, j * NE + e + NE, 1, bass.ds((j + 1) * SL, SL), False)
                dve.wait_ge(y_added, 3 * NE * PASSES)
            dve.memset(small[:, 40:41], 0.0).then_inc(y_final, 1)
            row_scale(2)
            dve.wait_ge(in_final, 16)
            for t in range(NT):
                n = ROWS[t]
                dve.scalar_tensor_tensor(out=h2[0:n, t, :], in0=x[0:n, t, :], scalar=small[0:n, 16 + t:17 + t],
                                         in1=final_g[0:n, :], op0=ALU.mult, op1=ALU.mult).then_inc(y_final, 1)


INS = ("x_prompt", "x_sample", "cache_ckv", "cache_krope", "state_pool", "page_table", "meta_tokens", "norm1_g",
       "w_in", "q_norm_g", "w_uq", "kv_norm_g", "w_uk", "w_uv", "w_pool", "pool_scale", "w_out", "norm2_g",
       "w_router", "b_router", "w_gate_up", "b_gate_up", "w_down", "b_down", "final_norm_g")
OUTS = (("y_p", (1, SEQ, D)), ("y_s", (NB, 1, D)), ("ckv_p", (1, 1, LP, C)), ("krope_p", (1, 1, LP, R)),
        ("pool_p", (1, 1, HIST, PW)), ("ckv_s", (1, NB, 1, C)), ("krope_s", (1, NB, 1, R)),
        ("pool_s", (1, NB, HIST, PW)))


def constants():
    import numpy as np
    c = np.zeros((P, NCONST), np.float32)

    def put(name, value):
        start, n = CONST[name]
        c[:, start:start + n] = value

    row = np.arange(P)[:, None]
    pos = np.concatenate([np.arange(LP), np.full(NB, PAST)]).astype(np.float32)
    inv = (np.float32(10000.0) ** (-np.arange(R // 2, dtype=np.float32) / np.float32(R // 2))).astype(np.float32)
    angle = pos[None, :] * inv[:, None]
    cos, sin = np.cos(angle), np.sin(angle)
    put("ident", np.eye(P))
    put("rope", np.concatenate([np.ones((NO, T)), cos, cos, sin, sin]))
    put("rope0", np.concatenate([cos, cos, sin, sin, np.zeros((NO, T))]))
    put("fold", (row % R == np.arange(P) % R) & (row < 2 * R))
    put("fold_hi", (row % R == np.arange(R)) & (row >= NO))
    put("half", (row < 2) & (np.arange(P) // SL == row))
    put("before", row < np.arange(P))
    put("iota", np.arange(PASSES * SL))
    put("mask1", np.where(np.arange(2 * P) <= P + row, 0.0, NEG))
    put("mask2", np.where(np.arange(LP) <= 2 * P + row % R, 0.0, NEG))
    put("headsel", row % R == np.arange(H))
    put("diag", np.arange(NB * H) // H == row)
    put("invcnt", 1.0 / np.minimum(np.repeat(2 << np.arange(G), 16), np.tile(np.arange(16), G) + 1))
    put("valid", np.arange(NT) * P + row < T)
    put("mod32", row % R)
    return c


def kernel(**inputs):
    import numpy as np
    import concourse.bacc as bacc
    from concourse.bass_utils import run_bass_kernel_spmd

    nc = bacc.Bacc("TRN2", target_bir_lowering=False, num_devices=1)
    arrays, a = {}, {}
    for name in INS:
        v = np.ascontiguousarray(inputs[name])
        arrays[f"in_{name}"] = v
        a[name] = nc.dram_tensor(f"in_{name}", v.shape, mybir.dt.from_np(v.dtype), kind="ExternalInput").ap()
    arrays["in_consts"] = constants()
    a["consts"] = nc.dram_tensor("in_consts", (P, NCONST), F32, kind="ExternalInput").ap()
    o = {name: nc.dram_tensor(f"out_{name}", shape, F32, kind="ExternalOutput").ap() for name, shape in OUTS}
    build(nc, a, o)
    r = run_bass_kernel_spmd(nc, [arrays], core_ids=[0]).results[0]
    return tuple(r[f"out_{name}"] for name, _ in OUTS)
```

```python
from contextlib import ExitStack

import concourse.bass as bass
from concourse import mybir

F32 = mybir.dt.float32
I32 = mybir.dt.int32
U32 = mybir.dt.uint32
ALU = mybir.AluOpType
ACT = mybir.ActivationFunctionType
AX = mybir.AxisListType

P = 128
D = 1024
KD = D // P
SEQ, META, NB = 256, 16, 8
LP = META + SEQ
T = LP + NB
ROWS = (P, P, T - 2 * P)
NT = len(ROWS)
LAST = LP - 2 * P
H = 8
C = 256
CT = C // P
R = 32
NO = 64
QK = NO + R
PW = 512
G = 4
HIST = 15
PAGES, PAGE, PAST = 16, 128, 2048
NE = 32
SL = 64
NP = NE // 2
PASSES = -(-T // SL)
SCALE = (NO + R) ** -0.5
EPS = 1e-6
LIMIT, ALPHA = 7.0, 1.702
QKV = 2 * C + R
SLOT = 4096
NSLOT = 6
NBUF = 3
NEG = -1.0e30

CONST = {}
_at = 0
for _name, _n in (("ident", P), ("rope", T), ("rope0", T), ("fold", P), ("fold_hi", P), ("half", P),
                  ("before", P), ("iota", PASSES * SL), ("mask1", 2 * P), ("mask2", LP), ("headsel", H),
                  ("diag", NB * H), ("invcnt", G * 16), ("valid", NT), ("mod32", 1), ("block", 4)):
    CONST[_name] = (_at, _n)
    _at += _n
NCONST = _at
VECS = 2 * KD + 2 * CT


def build(nc, a, o):
    with ExitStack() as ctx:
        def sem(name):
            return ctx.enter_context(nc.semaphore(name))

        arena = ctx.enter_context(nc.sbuf_tensor("arena", [P, 53200], F32))
        ps = ctx.enter_context(nc.psum_tensor("ps", [P, 8, 512], F32))
        top = [0]

        def at(start, n):
            return arena[:, start:start + n]

        def take(n):
            start = top[0]
            top[0] += n
            assert top[0] <= 53200, top[0]
            return start

        ring0 = take(NSLOT * SLOT)
        slot = [at(ring0 + SLOT * c, SLOT) for c in range(NSLOT)]
        w_uk = at(ring0, H * C)[0:NO, :].rearrange("p (h c) -> p h c", h=H)
        p_ext = at(ring0 + 2048, G * (16 + LP)).rearrange("p (g t) -> p g t", g=G)
        s_ext = at(ring0 + 2048 + G * (16 + LP), G * NB * 16).rearrange("p (g b t) -> p g b t", g=G, b=NB)
        sample0 = ring0 + SLOT
        keysT = at(sample0, 2 * PAST).rearrange("p (t k) -> p t k", t=2)
        kropeT = at(sample0 + 2 * PAST, 512)
        w_qkv = at(sample0, KD * QKV).rearrange("p (k n) -> p k n", k=KD)
        cache0 = sample0 + 2 * PAST + 512
        cache_c, cache_r = [], []
        for u in range(NBUF):
            base = cache0 + u * (PAGES * (C + R))
            cache_c.append(at(base, PAGES * C))
            cache_r.append(at(base + PAGES * C, PAGES * R))
        o_part = at(cache0 + NBUF * PAGES * (C + R), NB * C).rearrange("p (b c) -> p b c", b=NB)
        assert cache0 + NBUF * PAGES * (C + R) + NB * C <= ring0 + NSLOT * SLOT
        base = cache0 + PAGES * (C + R)
        w_uq = at(base, CT * H * QK).rearrange("p (k h n) -> p k h n", k=CT, h=H)
        w_uqx = at(base + CT * H * QK, CT * H * P).rearrange("p (k h n) -> p k h n", k=CT, h=H)
        w_kr = at(base + CT * H * (QK + P), KD * 2 * R).rearrange("p (k n) -> p k n", k=KD)
        w_p = slot[5].rearrange("p (k n) -> p k n", k=KD)

        x = at(take(NT * D), NT * D).rearrange("p (t d) -> p t d", t=NT)
        start = take(NT * D)
        xn = at(start, NT * D).rearrange("p (t d) -> p t d", t=NT)
        vals = xn
        h2 = xn
        hT0 = take(KD * T)
        hT = at(hT0, KD * T).rearrange("p (k t) -> p k t", k=KD)
        start = take(KD * T)
        zT = at(start, 4 * T).rearrange("p (k t) -> p k t", k=4)
        zsq0 = start + 4 * T
        zsq = at(zsq0, 4 * T).rearrange("p (k t) -> p k t", k=4)
        mT = at(start, KD * T).rearrange("p (k t) -> p k t", k=KD)
        start = take(CT * H * NO)
        norm2_g = at(start, D)
        w_ukT = at(start, CT * H * NO).rearrange("p (k n) -> p k n", k=CT)
        start = take(CT * H * P)
        w_uv = at(start, CT * H * P).rearrange("p (h k v) -> p h k v", h=H, k=CT)
        w_rt = at(start, KD * NE).rearrange("p (k e) -> p k e", k=KD)
        b_rt = at(start + KD * NE, NE)
        final_g = at(start + 512, D)
        w_pool = at(take(G * 256), G * 256).rearrange("p (g n) -> p g n", g=G)
        start = take(3 * T)
        r_bc = at(start, 2 * T).rearrange("p (k t) -> p k t", k=2)
        rope_q = at(start + 2 * T, T)
        probs2T = at(start, 2 * 3 * P).rearrange("p (g k q) -> p g k q", g=2, k=3)
        con0 = take(NCONST)
        const = {k: at(con0 + s, n) for k, (s, n) in CONST.items()}
        ones = at(take(P), P)
        vrow = at(take(P), P)[0:VECS, :]
        vecT = at(take(VECS), VECS)
        small = at(take(64), 64)
        small2 = at(take(64), 64)
        idx = at(take(NB * 4), NB * 4).bitcast(U32)

        pt = at(take(NB * PAGES), NB * PAGES).bitcast(I32)
        stats = at(take(2 * NB), 2 * NB).rearrange("p (k b) -> p k b", k=2)
        aS = at(take(H * NB), H * NB).rearrange("p (h b) -> p h b", h=H)
        sga_last = at(take(H * LAST), H * LAST).rearrange("p (h t) -> p h t", h=H)
        overlay = top[0]
        TQ = T + 8
        qT = at(take(H * TQ), H * TQ).rearrange("p (h t) -> p h t", h=H)
        kT = at(take(2 * LP), 2 * LP).rearrange("p (u t) -> p u t", u=2)
        krT = at(take(T), T)
        kr_cs = at(take(T), T)
        cT = at(take(CT * T), CT * T).rearrange("p (k t) -> p k t", k=CT)
        c_out = at(take(NT * (C + R)), NT * (C + R)).rearrange("p (t c) -> p t c", t=NT)
        start = take(G * T)
        pooled = at(start, G * T).rearrange("p (g t) -> p g t", g=G)
        qL = at(take(CT * NB * 32), CT * NB * 32).rearrange("p (k b h) -> p k b h", k=CT, b=NB)
        qR = at(take(NB * 32), NB * 32).rearrange("p (b h) -> p b h", b=NB)
        qLb = at(take(NBUF * CT * 32), NBUF * CT * 32).rearrange("p (u k h) -> p u k h", u=NBUF, k=CT)
        qRb = at(take(NBUF * 4 * 32), NBUF * 4 * 32).rearrange("p (u i h) -> p u i h", u=NBUF, i=4)
        probs0 = take(2 * 512)
        probs = at(probs0, 2 * 512).rearrange("p (u k) -> p u k", u=2)
        probsT0 = take(2 * 512)
        probsT = at(probsT0, 2 * 512).rearrange("p (u k) -> p u k", u=2)
        sig0 = take(2 * T + 16)
        sig = at(sig0, 2 * T).rearrange("p (k t) -> p k t", k=2)
        probs_s, probsT_s = at(probs0, 512), at(probs0 + 512, 512)
        pool_a = at(probsT0, LP)
        pool_b = at(probsT0 + 512, LP)
        sp_rows = at(probsT0, PW)[0:NB * HIST, :]
        p_rows = at(zsq0, PW)[0:HIST, :]
        s_rows = at(zsq0 + PW, PW)[0:NB, :]
        probs_last = kr_cs[:, 0:LP]
        merge0 = probs0
        y_short = at(probs0, 512)
        sq_mid = at(probsT0, D)
        top_front = top[0]
        top[0] = overlay
        lg = at(take(NT * NE), NT * NE).rearrange("p (t e) -> p t e", t=NT)
        top8 = at(take(NT * 8), NT * 8).rearrange("p (t e) -> p t e", t=NT)
        rt = at(take(4 * NT * NE), 4 * NT * NE).rearrange("p (n t e) -> p n t e", n=4, t=NT)
        sel = at(take(NT * NE), NT * NE).rearrange("p (t e) -> p t e", t=NT)
        rank = at(take(NT * (NE + 2)), NT * (NE + 2)).rearrange("p (t e) -> p t e", t=NT)
        gates = at(take(NT * (NE + 2)), NT * (NE + 2)).rearrange("p (t e) -> p t e", t=NT)
        most = at(take(2), 2)
        most_i = at(take(2), 2).bitcast(I32)
        pick = at(take(NT * P), NT * P).rearrange("p (t u s) -> p t u s", t=NT, u=2)
        pickg = at(take(NT * P), NT * P).rearrange("p (t u s) -> p t u s", t=NT, u=2)
        pickT = at(take(NT * P), NT * P).rearrange("p (t n) -> p t n", t=NT)
        xg = at(take(KD * P), KD * P).rearrange("p (k s) -> p k s", k=KD)
        y_last = at(take(512), 512)[0:64, :]
        b_gate, b_up, b_down = x[32:34, 2, :], xn[32:34, 2, :], xn[64:66, 2, :]
        assert 4 * D <= 2 * KD * T
        gate, sgm, up = (at(hT0 + D * j, D) for j in range(3))
        hidT = at(hT0 + 3 * D, D).rearrange("p (j n) -> p j n", j=KD)
        hid, ye = up, gate
        top[0] = max(top[0], top_front)

        ident = const["ident"]
        half = [const["half"][r:r + 2, :] for r in (0, 32, 64)]

        in_x, in_const, in_vec, in_g2 = sem("in_x"), sem("in_const"), sem("in_vec"), sem("in_g2")
        in_qkv = [sem("in_qkv_a"), sem("in_qkv_b")]
        in_uq, in_uk, in_uv, in_pool, in_p, in_hist, in_pt = (
            sem(n) for n in ("in_uq", "in_uk", "in_uv", "in_pool", "in_p", "in_hist", "in_pt"))
        in_gab = [sem(f"in_gab{j}") for j in range(4)]
        in_wo = [sem("in_wo0"), sem("in_wo1")]
        in_router, in_final = sem("in_router"), sem("in_final")
        in_cache = [sem(f"in_cache{u}") for u in range(NBUF)]
        in_chunk = [sem(f"in_chunk{c}") for c in range(NSLOT)]
        in_bias, in_b_down = sem("in_bias"), sem("in_b_down")
        out_small, out_y = sem("out_small"), sem("out_y")
        ones_ready, kr_weights, uq_weights, zeros_ready, idx_ready = (
            sem(n) for n in ("ones_ready", "kr_weights", "uq_weights", "zeros_ready", "idx_ready"))
        dve_step, act_step, pool_step = sem("dve_step"), sem("act_step"), sem("pool_step")
        sumsq, meansq, root, xn_ready = sem("sumsq"), sem("meansq"), sem("root"), sem("xn_ready")
        pe_vec, vec_ready, pe_hT, hT_act, hT_dve = (
            sem(n) for n in ("pe_vec", "vec_ready", "pe_hT", "hT_act", "hT_dve"))
        pe_z, zsq_ready, z_copied, kr_rot = (sem(n) for n in ("pe_z", "zsq_ready", "z_copied", "kr_rot"))
        pe_stat, r_ready, c_ready = sem("pe_stat"), sem("r_ready"), sem("c_ready")
        pe_ukT, ukT_ready, pe_hist, hist_ready = (
            sem(n) for n in ("pe_ukT", "ukT_ready", "pe_hist", "hist_ready"))
        pe_p, p_prompt, p_sample, pooled_ready = (
            sem(n) for n in ("pe_p", "p_prompt", "p_sample", "pooled_ready"))
        pe_kr, kr_ready, kT_rope = sem("pe_kr"), sem("kr_ready"), sem("kT_rope")
        pe_q, q_ready, pe_v, v_ready = sem("pe_q"), sem("q_ready"), sem("pe_v"), sem("v_ready")
        pe_cout, cout_ready, pe_prow, prow_ready = (
            sem(n) for n in ("pe_cout", "cout_ready", "pe_prow", "prow_ready"))
        pe_ql, ql_ready = sem("pe_ql"), sem("ql_ready")
        pe_kt, kt_act, kt_dve, q_batch, s_done, s_max, e_ready = (
            sem(n) for n in ("pe_kt", "kt_act", "kt_dve", "q_batch", "s_done", "s_max", "e_ready"))
        pe_pt, pt_ready, pv_done, o_ready = (sem(n) for n in ("pe_pt", "pt_ready", "pv_done", "o_ready"))
        merge_in, pe_merge, merge_act = sem("merge_in"), sem("pe_merge"), sem("merge_act")
        pe_k, k_ready, pe_s, s_masked, p_exp, p_norm = (
            sem(n) for n in ("pe_k", "k_ready", "pe_s", "s_masked", "p_exp", "p_norm"))
        pe_pT, pT_ready, pe_a, a_merged = (sem(n) for n in ("pe_pT", "pT_ready", "pe_a", "a_merged"))
        pe_gab, gab_exp, sig_ready, pe_y, y_merged = (
            sem(n) for n in ("pe_gab", "gab_exp", "sig_ready", "pe_y", "y_merged"))
        s2_masked, p2_exp, p2_norm, pe_p2T, p2T_ready, pe_a2, a2_merged = (
            sem(n) for n in ("s2_masked", "p2_exp", "p2_norm", "pe_p2T", "p2T_ready", "pe_a2", "a2_merged"))
        pe_wo, x_mid = sem("pe_wo"), sem("x_mid")
        h2_ready, pe_h2T, h2T_act, h2T_dve = (sem(n) for n in ("h2_ready", "pe_h2T", "h2T_act", "h2T_dve"))
        pe_logit, top_ready, e_top, sel_ready, pe_rank, rank_ready, most_ready = (
            sem(n) for n in ("pe_logit", "top_ready", "e_top", "sel_ready", "pe_rank", "rank_ready", "most_ready"))
        slot_free = [sem(f"slot_free{c}") for c in range(NSLOT)]
        x_zero, out_pool, sum_kept = sem("x_zero"), sem("out_pool"), sem("sum_kept")
        pick_ready, pickg_ready, pe_gather, xg_ready = (
            sem(n) for n in ("pick_ready", "pickg_ready", "pe_gather", "xg_ready"))
        pe_gu, gate_ready, up_ready, sgm_ready, hid_ready = (
            sem(n) for n in ("pe_gu", "gate_ready", "up_ready", "sgm_ready", "hid_ready"))
        pe_pick, pickT_ready, pe_hidT, hidT_act, hidT_dve, pe_down, ye_ready = (
            sem(n) for n in ("pe_pick", "pickT_ready", "pe_hidT", "hidT_act", "hidT_dve", "pe_down", "ye_ready"))
        short_out = sem("short_out")
        pe_comb, y_added, y_final = sem("pe_comb"), sem("y_added"), sem("y_final")

        block = ctx.enter_context(nc.Block())

        win = a["w_in"].rearrange("l (k p) n -> p (l k) n", p=P)
        cache_c_rows = a["cache_ckv"].rearrange("l n (q i) c -> (l n q) (i c)", i=4)
        cache_r_rows = a["cache_krope"].rearrange("l n (q i) c -> (l n q) (i c)", i=4)
        gu_rows = a["w_gate_up"].rearrange("l e (k p) n -> p (l e k) n", p=P)
        dn_rows = a["w_down"].rearrange("l e (k p) n -> p (l e k) n", p=P)

        @block.sync
        def _(sp):
            sp.dma_start(x[0:META, 0, :], a["meta_tokens"]).then_inc(in_x, 16)
            sp.dma_start(x[META:P, 0, :], a["x_prompt"][0, 0:P - META, :]).then_inc(in_x, 16)
            sp.dma_start(x[:, 1, :], a["x_prompt"][0, P - META:2 * P - META, :]).then_inc(in_x, 16)
            sp.wait_ge(x_zero, 1)
            sp.dma_start(x[0:LAST, 2, :], a["x_prompt"][0, 2 * P - META:SEQ, :]).then_inc(in_x, 16)
            sp.dma_start(x[LAST:LAST + NB, 2, :], a["x_sample"][:, 0, :]).then_inc(in_x, 16)
            sp.dma_start(at(con0, NCONST), a["consts"]).then_inc(in_const, 16)
            for j in range(2):
                sp.dma_start(w_qkv[:, 4 * j:4 * j + 4, :], win[:, 4 * j:4 * j + 4, 0:QKV]).then_inc(in_qkv[j], 16)
            sp.dma_start(w_uk, a["w_uk"][0].rearrange("h n c -> n h c")).then_inc(in_uk, 16)
            sp.dma_start(w_uq, a["w_uq"][0].rearrange("(k p) (h n) -> p k h n", p=P, h=H)).then_inc(in_uq, 16)
            sp.dma_start(w_p, win[:, :, QKV:QKV + PW]).then_inc(in_p, 16)
            sp.dma_start(sp_rows, a["state_pool"][0].rearrange("b t c -> (b t) c")).then_inc(in_hist, 16)
            sp.dma_start(w_uv, a["w_uv"][0].rearrange("h (k p) v -> p h k v", p=P)).then_inc(in_uv, 16)
            sp.dma_start(w_pool, a["w_pool"][0].rearrange("g p n -> p g n")).then_inc(in_pool, 16)
            sp.dma_start(o["pool_s"][0, :, 0:HIST - 1, :], a["state_pool"][0, :, 1:HIST, :]).then_inc(out_small, 16)
            for j in range(4):
                if j == 0:
                    sp.wait_ge(pe_ql, 1)
                    sp.wait_ge(pe_prow, 1)
                    sp.wait_ge(pooled_ready, G)
                    sp.wait_ge(p_sample, G + 1)
                else:
                    sp.wait_ge(pv_done, NB)
                dst = slot[j].rearrange("p (k u n) -> p k u n", k=KD, u=2)
                for u in range(2):
                    col = QKV + PW + u * D + j * 256
                    sp.dma_start(dst[:, :, u, :], win[:, :, col:col + 256]).then_inc(in_gab[j], 16)
            for n in range(2):
                if n == 1:
                    sp.wait_ge(pe_merge, 3)
                sp.dma_start(slot[4 + n].rearrange("p (k n) -> p k n", k=KD),
                             a["w_out"][0].rearrange("(k p) n -> p k n", p=P)[:, :, 512 * n:512 * n + 512]
                             ).then_inc(in_wo[n], 16)
            sp.wait_ge(pe_merge, 4)
            sp.dma_start(w_rt, a["w_router"][0].rearrange("(k p) e -> p k e", p=P)).then_inc(in_router, 16)
            sp.dma_start(b_rt, a["b_router"].to_broadcast([P, NE])).then_inc(in_router, 16)
            sp.dma_start(final_g, a["final_norm_g"].rearrange("(a n) -> a n", a=1).to_broadcast([P, D])
                         ).then_inc(in_final, 16)

            def pair_weights(p, n):
                def load(c, second, rows, k, count):
                    sp.wait_ge(slot_free[c], 2 * n + 1 + second)
                    e = 2 * p + c % 2
                    sp.dma_start(slot[c].rearrange("p (k n) -> p k n", k=count),
                                 rows[:, bass.ds(e * KD + k, count), :]).then_inc(in_chunk[c], 16)

                sp.wait_ge(slot_free[0], 2 * n + 1)
                for dst, col in ((b_gate, 0), (b_up, D)):
                    sp.dma_start(dst, a["b_gate_up"][0, bass.ds(2 * p, 2), col:col + D]).then_inc(in_bias, 16)
                for c in range(NSLOT):
                    load(c, 0, gu_rows, 2 * (c // 2), 2)
                sp.dma_start(b_down, a["b_down"][0, bass.ds(2 * p, 2), :]).then_inc(in_b_down, 16)
                for c in range(2):
                    load(c, 1, gu_rows, 6, 2)
                for c in range(2, NSLOT):
                    load(c, 1, dn_rows, 4 * (c // 2 - 1), 4)

            with sp.Fori(0, NP) as p:
                pair_weights(p, p)
            sp.wait_ge(most_ready, 1)
            count = sp.value_load(most_i[0:1, 0:1], min_val=0, max_val=T)
            with sp.If(count > SL):
                with sp.Fori(0, PASSES - 1) as j:
                    with sp.Fori(0, NP) as p:
                        pair_weights(p, j * NP + p + NP)
            sp.wait_ge(y_final, 2 + NT)
            sp.dma_start(o["y_p"][0, 0:P - META, :], h2[META:P, 0, :]).then_inc(out_y, 16)
            sp.dma_start(o["y_p"][0, P - META:2 * P - META, :], h2[:, 1, :]).then_inc(out_y, 16)
            sp.dma_start(o["y_p"][0, 2 * P - META:SEQ, :], h2[0:LAST, 2, :]).then_inc(out_y, 16)
            sp.dma_start(o["y_s"][:, 0, :], h2[LAST:LAST + NB, 2, :]).then_inc(out_y, 16)
            sp.wait_ge(out_y, 64)

        @block.gpsimd
        def _(pool):
            made = [0]

            def link(ins):
                made[0] += 1
                ins.then_inc(pool_step, 1)
                pool.wait_ge(pool_step, made[0])

            pool.memset(ones, 1.0).then_inc(ones_ready, 1)
            pool.wait_ge(idx_ready, 4)

            def start_cache(b):
                u = b % NBUF
                for s in range(4):
                    off = bass.IndirectOffsetOnAxis(ap=idx[:, 4 * b + s:4 * b + s + 1], axis=0)
                    pool.indirect_dma_start(cache_c[u][:, 4 * C * s:4 * C * s + 4 * C], None, cache_c_rows, off
                                            ).then_inc(in_cache[u], 16)
                    pool.indirect_dma_start(cache_r[u][:, 4 * R * s:4 * R * s + 4 * R], None, cache_r_rows, off
                                            ).then_inc(in_cache[u], 16)

            start_cache(0)
            for j in range(2):
                pool.wait_ge(in_qkv[j], 16)
            link(pool.tensor_copy(w_kr[:, :, 0:R], w_qkv[:, :, 2 * C:QKV]))
            link(pool.tensor_scalar(w_kr[:, :, R:R + 16], w_qkv[:, :, 2 * C + 16:QKV], -1.0, None, ALU.mult))
            pool.tensor_copy(w_kr[:, :, R + 16:2 * R], w_qkv[:, :, 2 * C:2 * C + 16]).then_inc(kr_weights, 1)
            pool.wait_ge(in_uq, 16)
            pool.wait_ge(vec_ready, 1)
            for k in range(CT):
                g = vecT[:, 2 * KD + k:2 * KD + k + 1]
                link(pool.tensor_scalar(w_uqx[:, k, :, 0:QK], w_uq[:, k, :, :], g, None, ALU.mult))
                link(pool.tensor_scalar(w_uqx[:, k, :, QK:QK + 16], w_uq[:, k, :, NO + 16:QK], g, -1.0,
                                        ALU.mult, ALU.mult))
                pool.tensor_scalar(w_uqx[:, k, :, QK + 16:P], w_uq[:, k, :, NO:NO + 16], g, None,
                                   ALU.mult).then_inc(uq_weights, 1)
            pool.memset(qL[:], 0.0).then_inc(zeros_ready, 1)
            pool.memset(qR[:], 0.0).then_inc(zeros_ready, 1)
            pool.memset(p_ext[:, :, 0:16], 0.0).then_inc(zeros_ready, 1)
            pool.memset(qT[:, :, T:TQ], 0.0).then_inc(zeros_ready, 1)
            pool.wait_ge(pe_p, G)
            start_cache(2)
            pool.wait_ge(pe_q, H)
            start_cache(1)
            pool.wait_ge(p_prompt, G)
            pool.wait_ge(zeros_ready, 4)
            for g in range(G):
                w = 2 << g
                src = p_ext[:, g, :]
                link(pool.tensor_tensor(pool_a, src[:, 16:16 + LP], src[:, 15:15 + LP], ALU.add))
                now, other = pool_a, pool_b
                n = 2
                while n < w:
                    link(pool.tensor_copy(other[:, 0:n], now[:, 0:n]))
                    link(pool.tensor_tensor(other[:, n:LP], now[:, n:LP], now[:, 0:LP - n], ALU.add))
                    now, other = other, now
                    n *= 2
                link(pool.tensor_scalar(other[:, 16:LP], now[:, 16:LP], 1.0 / w, None, ALU.mult))
                link(pool.tensor_tensor(other[:, 0:16], now[:, 0:16],
                                        const["invcnt"].rearrange("p (g t) -> p g t", g=G)[:, g, :], ALU.mult))
                pool.tensor_tensor(pooled[:, g, 0:LP], other, src[:, 16:16 + LP], ALU.subtract
                                   ).then_inc(pooled_ready, 1)
                pool.wait_ge(pooled_ready, g + 1)
            for b in range(NBUF, NB):
                pool.wait_ge(pv_done, b - NBUF + 1)
                start_cache(b)

        @block.tensor
        def _(pe):
            mm = nc.tensor.matmul

            pe.wait_ge(in_vec, 64)
            pe.wait_ge(in_const, 16)
            nc.tensor.transpose(ps[:, 7, 0:VECS], vrow, ident[0:VECS, 0:VECS]).then_inc(pe_vec, 1)
            pe.wait_ge(xn_ready, NT)
            for k in range(KD):
                if k >= 4:
                    pe.wait_ge(hT_act if k % 2 == 0 else hT_dve, (k - 4) // 2 + 1)
                for t in range(NT):
                    m = nc.tensor.transpose(ps[:, k % 4, P * t:P * t + ROWS[t]],
                                            xn[0:ROWS[t], t, P * k:P * k + P], ident[0:ROWS[t], 0:ROWS[t]])
                m.then_inc(pe_hT, 1)
            pe.wait_ge(vec_ready, 1)
            for k in range(KD):
                pe.wait_ge(hT_act if k % 2 == 0 else hT_dve, k // 2 + 1)
                if k % 4 == 0:
                    pe.wait_ge(in_qkv[k // 4], 16)
                for j in range(4):
                    m = mm(ps[:, 4 + j, 0:T], w_qkv[:, k, P * j:P * j + P], hT[:, k, :],
                           start=(k == 0), stop=(k == KD - 1))
                    if k == KD - 1:
                        m.then_inc(pe_z, 1)
            pe.wait_ge(kr_weights, 1)
            for k in range(KD):
                m = mm(ps[0:2 * R, 0, 0:T], w_kr[:, k, :], hT[:, k, :], start=(k == 0), stop=(k == KD - 1))
            m.then_inc(pe_z, 1)
            pe.wait_ge(in_uk, 16)
            for k in range(CT):
                bank = 3 if k == 0 else 4
                if k == 1:
                    pe.wait_ge(zsq_ready, 1)
                    pe.wait_ge(z_copied, 1)
                for h in range(H):
                    m = nc.tensor.transpose(ps[:, bank, NO * h:NO * h + NO], w_uk[:, h, P * k:P * k + P],
                                            ident[0:NO, 0:NO])
                m.then_inc(pe_ukT, 1)
            pe.wait_ge(ones_ready, 1)
            for j in range(2):
                pe.wait_ge(zsq_ready, 2 * j + 2)
                for k in range(CT):
                    m = mm(ps[:, 1 + j, 0:T], ones, zsq[:, 2 * j + k, :], start=(k == 0), stop=(k == CT - 1))
                m.then_inc(pe_stat, 1)
            pe.wait_ge(in_hist, 16)
            pe.wait_ge(z_copied, 2)
            for g in range(G):
                m = nc.tensor.transpose(ps[:, 5, P * g:P * g + NB * HIST], sp_rows[:, P * g:P * g + P],
                                        ident[0:NB * HIST, 0:NB * HIST])
            m.then_inc(pe_hist, 1)
            pe.wait_ge(kr_rot, 1)
            mm(ps[:, 0, 0:T], const["fold"][0:2 * R, :], kr_cs[0:2 * R, :], start=True, stop=True).then_inc(pe_kr, 1)
            pe.wait_ge(in_p, 16)
            pe.wait_ge(zsq_ready, 4)
            pe.wait_ge(z_copied, 4)
            for g in range(G):
                bank = (6, 7, 6, 7)[g]
                if g >= 2:
                    pe.wait_ge(p_prompt, g - 1)
                    pe.wait_ge(p_sample, g - 1)
                for k in range(KD):
                    m = mm(ps[:, bank, 0:T], w_p[:, k, P * g:P * g + P], hT[:, k, :],
                           start=(k == 0), stop=(k == KD - 1))
                m.then_inc(pe_p, 1)
            pe.wait_ge(uq_weights, CT)
            pe.wait_ge(r_ready, 2)
            pe.wait_ge(ukT_ready, 2)
            for h in range(H):
                bank = 1 + h % 4
                if h >= 4:
                    pe.wait_ge(q_ready, h - 3)
                for k in range(CT):
                    m = mm(ps[:, bank, 0:T], w_uqx[:, k, h, :], zT[:, k, :], start=(k == 0), stop=(k == CT - 1))
                m.then_inc(pe_q, 1)
            pe.wait_ge(p_prompt, G)
            pe.wait_ge(p_sample, G)
            pe.wait_ge(hist_ready, 1)
            for g in range(G):
                m = nc.tensor.transpose(ps[0:HIST, 5, P * g:P * g + P], p_ext[:, g, 16 + LP - HIST:16 + LP], ident)
            for g in range(G):
                m = nc.tensor.transpose(ps[0:NB, 6, P * g:P * g + P], s_ext[:, g, :, HIST], ident)
            m.then_inc(pe_prow, 1)
            pe.wait_ge(q_ready, H)
            pe.wait_ge(zeros_ready, 4)
            for h in range(H):
                for k in range(CT):
                    m = mm(ps[:, 7, (k * H + h) * NB:(k * H + h) * NB + NB], w_uk[:, h, P * k:P * k + P],
                           qT[0:NO, h, LP:T], start=True, stop=True)
            m.then_inc(pe_ql, 1)
            pe.wait_ge(kr_ready, 1)
            mm(ps[:, 0, 0:H * NB].rearrange("p (h b) -> p h b", h=H), const["fold_hi"][NO:P, :],
               qT[NO:P, :, LP:T], start=True, stop=True).then_inc(pe_ql, 1)
            pe.wait_ge(c_ready, 2)
            pe.wait_ge(in_uv, 16)
            for t in range(NT):
                rows = ROWS[t] if t < 2 else LAST
                for n in range(2):
                    g = 2 * t + n
                    if g >= 4:
                        pe.wait_ge(v_ready, g - 3)
                    for k in range(CT):
                        m = mm(ps[0:rows, 1 + g % 4, :], cT[:, k, P * t:P * t + rows],
                               w_uv[:, 4 * n:4 * n + 4, k, :],
                               start=(k == 0), stop=(k == CT - 1))
                    m.then_inc(pe_v, 1)
            pe.wait_ge(prow_ready, 1)
            pe.wait_ge(ql_ready, 3)
            for t in range(NT):
                bank = 5 + t
                for k in range(CT):
                    nc.tensor.transpose(ps[0:ROWS[t], bank, P * k:P * k + P], cT[:, k, P * t:P * t + ROWS[t]], ident)
                nc.tensor.transpose(ps[0:ROWS[t], bank, C:C + R], krT[0:R, P * t:P * t + ROWS[t]],
                                    ident[0:R, 0:R]).then_inc(pe_cout, 1)
            pe.wait_ge(v_ready, 6)
            pe.wait_ge(cout_ready, 3)

            def turn_latents(b, u, s):
                for i in range(4):
                    key = cache_c[u][:, (4 * s + i) * C:(4 * s + i + 1) * C]
                    for k in range(CT):
                        m = nc.tensor.transpose(ps[:, 3 * (s % 2) + k, P * i:P * i + P], key[:, P * k:P * k + P], ident)
                m.then_inc(pe_kt, 1)

            def turn_rope(u):
                for s in range(4):
                    m = nc.tensor.transpose(ps[:, 2, P * s:P * s + P], cache_r[u][:, P * s:P * s + P], ident)
                m.then_inc(pe_kt, 1)

            def score(b, u, first):
                pe.wait_ge(kt_act, 4 * b + 4)
                pe.wait_ge(kt_dve, 5 * b + 5)
                pe.wait_ge(q_batch, 2 * b + 2)
                if not first:
                    pe.wait_ge(e_ready, b)
                for k in range(CT):
                    for s in range(4):
                        mm(ps[32 * s:32 * s + 32, 6, :], qLb[:, u, k, :], keysT[:, k, 512 * s:512 * s + 512],
                           start=(k == 0), stop=False, skip_group_check=True)
                for i in range(4):
                    for s in range(4):
                        m = mm(ps[32 * s:32 * s + 32, 6, P * i:P * i + P], qRb[:, u, i, :],
                               kropeT[:, P * s:P * s + P], start=False, stop=True,
                               skip_group_check=True)
                m.then_inc(s_done, 1)

            def turn_probs(b, first):
                pe.wait_ge(e_ready, b + 1)
                if not first:
                    pe.wait_ge(pt_ready, b)
                for i in range(4):
                    m = nc.tensor.transpose(ps[:, 7, P * i:P * i + P], probs_s[:, P * i:P * i + P], ident)
                m.then_inc(pe_pt, 1)

            def weigh(b, u, first):
                pe.wait_ge(pt_ready, b + 1)
                if not first:
                    pe.wait_ge(o_ready, b)
                for i in range(4):
                    for s in range(4):
                        m = mm(ps[32 * s:32 * s + 32, 5, 0:C], probsT_s[:, P * i + 32 * s:P * i + 32 * s + 32],
                               cache_c[u][:, (4 * s + i) * C:(4 * s + i + 1) * C], start=(i == 0), stop=(i == 3))
                m.then_inc(pv_done, 1)

            def batch(b, u, loads, count):
                pe.wait_ge(in_cache[u], 128 * loads)
                turn_latents(b, u, 0)
                turn_latents(b, u, 1)
                turn_rope(u)
                if count != 0:
                    turn_probs(b - 1, count == 1)
                pe.wait_ge(kt_act, 4 * b + 1)
                pe.wait_ge(kt_dve, 5 * b + 1)
                turn_latents(b, u, 2)
                if count != 0:
                    weigh(b - 1, (u - 1) % NBUF, count == 1)
                pe.wait_ge(kt_act, 4 * b + 2)
                pe.wait_ge(kt_dve, 5 * b + 2)
                turn_latents(b, u, 3)
                score(b, u, count == 0)

            batch(0, 0, 1, 0)
            batch(1, 1, 1, 1)
            with pe.Fori(0, (NB - 2) // NBUF) as i:
                batch(3 * i + 2, 2, i + 1, None)
                batch(3 * i + 3, 0, i + 2, None)
                batch(3 * i + 4, 1, i + 2, None)
            turn_probs(NB - 1, False)
            weigh(NB - 1, (NB - 1) % NBUF, False)
            pe.wait_ge(o_ready, NB)
            pe.wait_ge(merge_in, 1)
            for k in range(3):
                n = P if k < 2 else R
                src = at(merge0, 3 * 64)[0:n, 64 * k:64 * k + 64]
                m = mm(ps[0:NB, 0, 0:64], ones[0:n, 0:NB], src, start=(k == 0), stop=(k == 2))
            nc.tensor.transpose(ps[0:NB, 1, 0:P], stats[:, 0, :], ident)
            nc.tensor.transpose(ps[0:NB, 1, P:2 * P], stats[:, 1, :], ident).then_inc(pe_merge, 1)
            pe.wait_ge(merge_in, 3)
            nc.tensor.transpose(ps[:, 2, 0:NB], at(merge0 + 448, P)[0:NB, :], ident[0:NB, 0:NB])
            mm(ps[:, 3, 0:64], ones[0:NB, :], at(merge0 + 576, 64)[0:NB, :], start=True, stop=True).then_inc(pe_merge, 1)
            pe.wait_ge(merge_in, 5)
            for b in range(NB):
                for k in range(CT):
                    m = mm(ps[:, 4, (k * NB + b) * H:(k * NB + b) * H + H], o_part[:, b, P * k:P * k + P],
                           at(merge0 + 640, 64)[:, H * b:H * b + H], start=True, stop=True)
            m.then_inc(pe_merge, 1)
            pe.wait_ge(merge_in, 7)
            oL = at(merge0 + 768, CT * 64).rearrange("p (k b h) -> p k b h", k=CT, b=NB)
            for h in range(H):
                for k in range(CT):
                    m = mm(ps[:, 5, NB * h:NB * h + NB], w_uv[:, h, k, :], oL[:, k, :, h],
                           start=(k == 0), stop=(k == CT - 1))
            m.then_inc(pe_merge, 1)
            pe.wait_ge(merge_in, 8)

            def keys(h):
                if h >= 2:
                    pe.wait_ge(k_ready, h)
                for k in range(CT):
                    m = mm(ps[0:NO, 0, 0:LP], w_ukT[:, k, NO * h:NO * h + NO], cT[:, k, 0:LP],
                           start=(k == 0), stop=(k == CT - 1))
                m.then_inc(pe_k, 1)

            pe.wait_ge(kT_rope, 2)
            keys(0)
            for h in range(H):
                g = h // 4
                pe.wait_ge(k_ready, h + 1)
                if h:
                    pe.wait_ge(s_masked, h)
                    if h % 4 == 0:
                        pe.wait_ge(s2_masked, g)
                k = kT[:, h % 2, :]
                mm(ps[:, 1, 0:P], qT[:, h, 0:P], k[:, 0:P], start=True, stop=True)
                mm(ps[:, 1, P:3 * P], qT[:, h, P:2 * P], k[:, 0:2 * P], start=True, stop=True).then_inc(pe_s, 1)
                r = 32 * (h % 4)
                if h % 4 == 0 and g:
                    pe.wait_ge(a2_merged, g)
                mm(ps[r:r + 32, 7, 0:LP], qT[:, h, 2 * P:2 * P + 32], k, start=True, stop=True,
                   ).then_inc(pe_s, 1)
                if h % 2 == 0:
                    pe.wait_ge(in_gab[h // 2], 32)
                if h:
                    pe.wait_ge(gab_exp, h)
                w = slot[h // 2].rearrange("p (k u n) -> p k u n", k=KD, u=2)
                for u in range(2):
                    for kk in range(KD):
                        m = mm(ps[:, 4 + u, 0:T], w[:, kk, u, P * (h % 2):P * (h % 2) + P], hT[:, kk, :],
                               start=(kk == 0), stop=(kk == KD - 1))
                m.then_inc(pe_gab, 1)
                if h == 0:
                    pe.wait_ge(pooled_ready, G)
                    pe.wait_ge(p_sample, G + 1)
                    pe.wait_ge(in_pool, 16)
                else:
                    pe.wait_ge(y_merged, h)
                m = mm(ps[:, 6, 0:T], w_pool[:, h // 2, P * (h % 2):P * (h % 2) + P], pooled[:, h // 2, :],
                       start=True, stop=True)
                m.then_inc(pe_y, 1)
                if h + 1 < H:
                    keys(h + 1)
                pe.wait_ge(p_norm, h + 1)
                if h:
                    pe.wait_ge(pT_ready, h)
                E = probs[:, h % 2, :]
                nc.tensor.transpose(ps[:, 2, 0:P], E[:, 0:P], ident)
                nc.tensor.transpose(ps[:, 2, P:2 * P], E[:, P:2 * P], ident)
                nc.tensor.transpose(ps[:, 2, 2 * P:3 * P], E[:, 2 * P:3 * P], ident).then_inc(pe_pT, 1)
                pe.wait_ge(pT_ready, h + 1)
                if h:
                    pe.wait_ge(a_merged, h)
                ET = probsT[:, h % 2, :]
                mm(ps[:, 3, 0:2 * P], vals[:, 0, P * h:P * h + P], ET[:, 0:2 * P], start=True, stop=False,
                   skip_group_check=True)
                mm(ps[:, 3, P:2 * P], vals[:, 1, P * h:P * h + P], ET[:, 2 * P:3 * P], start=False, stop=True,
                   skip_group_check=True).then_inc(pe_a, 1)
                if h % 4 == 3:
                    pe.wait_ge(p2_norm, g + 1)
                    pe.wait_ge(pT_ready, h + 1)
                    E2 = probs_last
                    for kb in range(3):
                        n = P if kb < 2 else LAST
                        m = nc.tensor.transpose(ps[0:n, 2, P * kb:P * kb + P], E2[:, P * kb:P * kb + n], ident)
                    m.then_inc(pe_p2T, 1)
                    pe.wait_ge(p2T_ready, 2 * g + 2)
                    for hh in range(4):
                        for kb in range(3):
                            n = P if kb < 2 else LAST
                            m = mm(ps[:, 7, LAST * hh:LAST * hh + LAST],
                                   vals[0:n, kb, P * (4 * g + hh):P * (4 * g + hh) + P],
                                   probs2T[0:n, g, kb, 32 * hh:32 * hh + LAST], start=(kb == 0), stop=(kb == 2))
                    m.then_inc(pe_a2, 1)
                if h % 2:
                    pe.wait_ge(gab_exp, h + 1)
                    pe.sem_inc(slot_free[h // 2], 1)
            pe.wait_ge(a2_merged, 2)
            pe.wait_ge(y_merged, H)
            pe.wait_ge(a_merged, H)
            pe.wait_ge(in_wo[0], 16)
            pe.wait_ge(in_wo[1], 16)
            w_out = [slot[4 + n].rearrange("p (k n) -> p k n", k=KD) for n in range(2)]
            rows = ROWS[2]
            for k in range(KD):
                for n in range(2):
                    m = mm(ps[32 * n:32 * n + rows, 0, :], mT[:, k, 2 * P:T], w_out[n][:, k, :],
                           start=(k == 0), stop=(k == KD - 1))
            m.then_inc(pe_wo, 1)

            def project(t, bank):
                for n in range(2):
                    for k in range(KD):
                        m = mm(ps[:, bank + n, :], mT[:, k, P * t:P * t + P], w_out[n][:, k, :],
                               start=(k == 0), stop=(k == KD - 1))
                    m.then_inc(pe_wo, 1)

            def turn_h2(t, j, banks):
                n = ROWS[t]
                pe.wait_ge(h2_ready, 1 + j)
                for k in range(KD):
                    m = nc.tensor.transpose(ps[:, banks[k // 4], P * (k % 4):P * (k % 4) + n],
                                            h2[0:n, t, P * k:P * k + P], ident[0:n, 0:n])
                    if k % 4 == 3:
                        m.then_inc(pe_h2T, 1)

            def logits(t, j):
                pe.wait_ge(h2T_act, j + 1)
                pe.wait_ge(h2T_dve, j + 1)
                for k in range(KD):
                    m = mm(ps[0:ROWS[t], 7, NE * t:NE * t + NE], hT[:, k, P * t:P * t + ROWS[t]], w_rt[:, k, :],
                           start=(k == 0), stop=(k == KD - 1))
                m.then_inc(pe_logit, 1)

            project(0, 2)
            pe.wait_ge(short_out, 1)
            mm(ps[0:rows, 1, :], ident[32:32 + rows, 32:32 + rows], y_short[32:32 + rows, :], start=True, stop=True
               ).then_inc(pe_wo, 1)
            project(1, 4)
            pe.wait_ge(x_mid, 6)
            for n in range(2):
                pe.sem_inc(slot_free[4 + n], 1)
            turn_h2(2, 0, (0, 1))
            turn_h2(0, 1, (2, 3))
            pe.wait_ge(in_router, 32)
            logits(2, 0)
            logits(0, 1)
            turn_h2(1, 2, (4, 5))
            logits(1, 2)
            pe.wait_ge(h2T_dve, 3)
            pe.wait_ge(sel_ready, 1)
            for t in range(NT):
                for s in range(t + 1):
                    mm(ps[:, 5, NE * t:NE * t + NE], const["before"] if s == t else ones, sel[:, s, :],
                       start=(s == 0), stop=(s == t))
            for s in range(NT):
                m = mm(ps[0:1, 5, NE * NT:NE * NT + NE], ones[:, 0:1], sel[:, s, :], start=(s == 0), stop=(s == NT - 1))
            m.then_inc(pe_rank, 1)

            pe.sem_inc(pe_comb, 1)

            def gather(count):
                pe.wait_ge(pick_ready, count)
                for k in range(KD):
                    for t in range(NT):
                        n = ROWS[t]
                        m = mm(ps[:, 6 + k // 4, P * (k % 4):P * (k % 4) + P], h2[0:n, t, P * k:P * k + P],
                               pick[0:n, t, :, :].rearrange("p u s -> p (u s)"), start=(t == 0), stop=(t == NT - 1))
                m.then_inc(pe_gather, 1)

            def pair(n, extra, ahead):
                if not ahead:
                    pe.wait_ge(y_added, 3 * n + 3)
                    gather(n + extra + 1)
                pe.wait_ge(xg_ready, n + extra + 1)
                pe.wait_ge(pickg_ready, n + extra + 1)
                for t in range(NT):
                    m = nc.tensor.transpose(ps[:, 7, P * t:P * t + P], pickg[:, t, :, :].rearrange("p u s -> p (u s)"),
                                            ident)
                m.then_inc(pe_pick, 1)
                pe.wait_ge(in_bias, 32 * n + 32)
                pe.wait_ge(y_added, 3 * n + 1)
                for b in range(4):
                    row = b_gate if b < 2 else b_up
                    mm(ps[:, b, :], half[1], row[:, 512 * (b % 2):512 * (b % 2) + 512], start=True, stop=False,
                       skip_group_check=True)
                for c in range(4):
                    s0 = 2 * (c % 3)
                    w = []
                    for e in range(2):
                        pe.wait_ge(in_chunk[s0 + e], 32 * n + 16 + 16 * (c // 3))
                        w.append(slot[s0 + e].rearrange("p (k b n) -> p k b n", k=2, b=4))
                    order = ([(kk, b) for b in (0, 2, 1, 3) for kk in range(2)] if c == 3 else
                             [(kk, b) for kk in range(2) for b in range(4)])
                    for j, (kk, b) in enumerate(order):
                        for e in range(2):
                            m = mm(ps[SL * e:SL * e + SL, b, :], xg[:, 2 * c + kk, SL * e:SL * e + SL],
                                   w[e][:, kk, b, :], start=False, stop=(c == 3 and kk == 1),
                                   skip_group_check=True)
                            if j == 7:
                                m.then_inc(slot_free[s0 + e], 1)
                        if c == 3 and j == 3:
                            m.then_inc(pe_gu, 1)
                if ahead:
                    pe.wait_ge(pickT_ready, n + 1)
                    pe.wait_ge(y_added, 3 * n + 3)
                    gather(n + 2)
                pe.wait_ge(gate_ready, 2 * n + 2)
                pe.wait_ge(in_b_down, 16 * n + 16)
                for u in range(2):
                    mm(ps[:, u, :], half[2], b_down[:, 512 * u:512 * u + 512], start=True, stop=False,
                       skip_group_check=True)
                pe.wait_ge(y_added, 3 * n + 2)
                for u in range(2):
                    pe.wait_ge(hid_ready, 2 * n + u + 1)
                    for j in range(4):
                        m = nc.tensor.transpose(ps[:, 4 + u, P * j:P * j + P],
                                                hid[:, 512 * u + P * j:512 * u + P * j + P], ident)
                    m.then_inc(pe_hidT, 1)
                for c in range(2):
                    s0 = 2 + 2 * c
                    pe.wait_ge(hidT_act if c == 0 else hidT_dve, n + 1)
                    w = []
                    for e in range(2):
                        pe.wait_ge(in_chunk[s0 + e], 32 * n + 32)
                        w.append(slot[s0 + e].rearrange("p (k u n) -> p k u n", k=4, u=2))
                    order = ([(kk, u) for u in range(2) for kk in range(4)] if c == 1 else
                             [(kk, u) for kk in range(4) for u in range(2)])
                    for j, (kk, u) in enumerate(order):
                        for e in range(2):
                            m = mm(ps[SL * e:SL * e + SL, u, :], hidT[:, 4 * c + kk, SL * e:SL * e + SL],
                                   w[e][:, kk, u, :], start=False, stop=(c == 1 and kk == 3),
                                   skip_group_check=True)
                            if j == 7:
                                m.then_inc(slot_free[s0 + e], 1)
                        if c == 1 and j == 3:
                            m.then_inc(pe_down, 1)
                pe.wait_ge(pickT_ready, n + 1)
                pe.wait_ge(ye_ready, 2 * n + 1)
                pe.wait_ge(hid_ready, 2 * n + 2)
                for u in range(2):
                    if u == 1:
                        pe.wait_ge(ye_ready, 2 * n + 2)
                    for t in range(2):
                        m = mm(ps[:, 2 + 2 * t + u, :], pickT[:, t, :], ye[:, 512 * u:512 * u + 512],
                               start=True, stop=True)
                        if u == 1:
                            m.then_inc(pe_comb, 1)
                pe.wait_ge(xg_ready, n + extra + (2 if ahead else 1))
                for u in range(2):
                    m = mm(ps[32 * u:32 * u + 32, 6, :], pickT[:, 2, 0:32], ye[:, 512 * u:512 * u + 512],
                           start=True, stop=True)
                m.then_inc(pe_comb, 1)

            gather(1)
            with pe.Fori(0, NP) as p:
                pair(p, 0, True)
            pe.wait_ge(most_ready, 1)
            count = pe.value_load(most_i[0:1, 0:1], min_val=0, max_val=T)
            with pe.If(count > SL):
                with pe.Fori(0, PASSES - 1) as j:
                    with pe.Fori(0, NP) as p:
                        pair(j * NP + p + NP, 1, False)
            pe.wait_ge(y_final, 1)
            for u in range(2):
                m = mm(ps[0:32, u, :], ident[0:64, 32 * u:32 * u + 32], y_last, start=True, stop=True)
            m.then_inc(pe_wo, 1)

        def row_norm(act, n0):
            for t in range(NT):
                act.activation(sq_junk2[0:ROWS[t], :], x[0:ROWS[t], t, :], ACT.Square,
                               accum_out=small[0:ROWS[t], t:t + 1]).then_inc(sumsq, 1)
                act.wait_ge(sumsq, 3 * n0 + t + 1)
            act.wait_ge(meansq, 1 if n0 == 0 else 7)
            act.activation(small[:, 8:8 + NT], small[:, 4:4 + NT], ACT.Sqrt).then_inc(root, 1)

        sq_junk2 = xn[:, 0, :]

        @block.scalar
        def _(act):
            def copy(out, in_):
                return act.activation(out, in_, ACT.Copy)

            for r0, name, n in ((0, "norm1_g", KD), (KD, "pool_scale", KD), (2 * KD, "q_norm_g", CT),
                                (2 * KD + CT, "kv_norm_g", CT)):
                act.dma_start(vrow[r0:r0 + n, :], a[name].rearrange("l (k p) -> (l k) p", p=P)).then_inc(in_vec, 16)
            act.dma_start(pt, a["page_table"].rearrange("(a b) s -> a (b s)", a=1).to_broadcast([P, NB * PAGES])
                          ).then_inc(in_pt, 16)
            act.wait_ge(in_x, 80)
            act.wait_ge(x_zero, 1)
            row_norm(act, 0)
            act.wait_ge(pe_vec, 1)
            copy(vecT, ps[:, 7, 0:VECS]).then_inc(vec_ready, 1)
            act.wait_ge(vec_ready, 1)
            for k in range(0, KD, 2):
                act.wait_ge(pe_hT, k + 1)
                act.activation(hT[:, k, :], ps[:, k % 4, 0:T], ACT.Copy, scale=vecT[:, k:k + 1]).then_inc(hT_act, 1)
            for j in range(4):
                act.wait_ge(z_copied, j + 1)
                act.activation(zsq[:, j, :], zT[:, j, :], ACT.Square).then_inc(zsq_ready, 1)
            for k in range(CT):
                act.wait_ge(pe_ukT, k + 1)
                copy(w_ukT[:, k, :], ps[:, 3 + k, :]).then_inc(ukT_ready, 1)
            for j in range(2):
                act.wait_ge(meansq, 2 + j)
                act.activation(r_bc[:, j, :], r_bc[:, j, :], ACT.Sqrt).then_inc(root, 1)
            act.wait_ge(pe_hist, 1)
            copy(s_ext[:, :, :, 0:HIST], ps[:, 5, :].rearrange("p (g n) -> p g n", g=G)[:, :, 0:NB * HIST]
                 .rearrange("p g (b t) -> p g b t", b=NB)).then_inc(hist_ready, 1)
            act.wait_ge(pe_kr, 1)
            copy(krT, ps[:, 0, 0:T]).then_inc(kr_ready, 1)
            act.wait_ge(kr_ready, 1)
            for u in range(2):
                copy(kT[NO:P, u, :], krT[NO:P, 0:LP]).then_inc(kT_rope, 1)
            for g in range(G):
                act.wait_ge(pe_p, g + 1)
                copy(p_ext[:, g, 16:16 + LP], ps[:, 6 + g % 2, 0:LP]).then_inc(p_prompt, 1)
            for j in range(6):
                act.wait_ge(pe_v, j + 1)
                rows = P if j < 4 else LAST
                copy(vals[0:rows, j // 2, 512 * (j % 2):512 * (j % 2) + 512], ps[0:rows, 1 + j % 4, :]
                     ).then_inc(v_ready, 1)

            act.wait_ge(prow_ready, 1)
            act.dma_start(o["pool_p"][0, 0, :, :], p_rows).then_inc(out_pool, 16)
            act.dma_start(o["pool_s"][0, :, HIST - 1, :], s_rows).then_inc(out_pool, 16)
            act.wait_ge(cout_ready, 3)
            for dst, col, n in (("ckv", 0, C), ("krope", C, R)):
                act.dma_start(o[dst + "_p"][0, 0, 0:P, :], c_out[:, 0, col:col + n]).then_inc(out_small, 16)
                act.dma_start(o[dst + "_p"][0, 0, P:2 * P, :], c_out[:, 1, col:col + n]).then_inc(out_small, 16)
                act.dma_start(o[dst + "_p"][0, 0, 2 * P:LP, :], c_out[0:LAST, 2, col:col + n]).then_inc(out_small, 16)
                act.dma_start(o[dst + "_s"][0, :, 0, :], c_out[LAST:LAST + NB, 2, col:col + n]).then_inc(out_small, 16)

            def exponents(b):
                act.wait_ge(s_max, 2 * b + 2)
                act.activation(probs_s, ps[:, 6, :], ACT.Exp, bias=small[:, 12:13], scale=SCALE,
                               accum_out=small[:, 14:15]).then_inc(e_ready, 1)

            def take_probs(b):
                act.wait_ge(pe_pt, b + 1)
                copy(probsT_s, ps[:, 7, :]).then_inc(pt_ready, 1)

            def take_out(b, one):
                act.wait_ge(pv_done, b + 1)
                copy(o_part[:, one, :].rearrange("p b c -> p (b c)"), ps[:, 5, 0:C]).then_inc(o_ready, 1)

            def batch(b, count):
                if count != 0:
                    act.wait_ge(s_done, b)
                    exponents(b - 1)
                for s in range(4):
                    act.wait_ge(pe_kt, 5 * b + (1, 2, 4, 5)[s])
                    copy(keysT[:, 0, 512 * s:512 * s + 512], ps[:, 3 * (s % 2), :]).then_inc(kt_act, 1)
                    if count != 0:
                        if s == 1:
                            take_probs(b - 1)
                        if s == 2:
                            take_out(b - 1, slice(0, 1) if count == 1 else bass.ds(b - 1, 1))

            batch(0, 0)
            batch(1, 1)
            with act.Fori(0, (NB - 2) // NBUF) as i:
                for j in range(NBUF):
                    batch(3 * i + 2 + j, None)
            exponents(NB - 1)
            take_probs(NB - 1)
            take_out(NB - 1, slice(NB - 1, NB))
            act.wait_ge(merge_in, 2)
            act.activation(at(merge0 + 320, P)[0:NB, :], at(merge0 + 192, P)[0:NB, :], ACT.Exp,
                           scale=SCALE).then_inc(merge_act, 1)
            act.activation(at(merge0 + 904, 32)[0:NB, 0:H], at(merge0 + 896, 8)[0:NB, :], ACT.Exp,
                           scale=SCALE).then_inc(merge_act, 1)
            for h in range(H):
                if h == 0:
                    act.wait_ge(pe_k, 1)
                    copy(kT[0:NO, 0, :], ps[0:NO, 0, 0:LP]).then_inc(k_ready, 1)
                act.wait_ge(s_masked, h + 1)
                for j, (lo, hi) in enumerate(((0, P), (P, 3 * P))):
                    e = probs[:, h % 2, lo:hi]
                    act.activation(e, e, ACT.Exp, bias=small[:, 20 + j:21 + j], scale=SCALE,
                                   accum_out=small[:, 24 + j:25 + j]).then_inc(p_exp, 1)
                if h % 4 == 3:
                    act.wait_ge(s2_masked, h // 4 + 1)
                    act.activation(probs_last, probs_last, ACT.Exp, bias=small[:, 28:29], scale=SCALE,
                                   accum_out=small[:, 30:31]).then_inc(p2_exp, 1)
                act.wait_ge(pe_gab, h + 1)
                if h:
                    act.wait_ge(a_merged, h)
                act.activation(sig[:, :, :], ps[:, 4:6, 0:T], ACT.Exp, scale=-1.0).then_inc(gab_exp, 1)
                if h + 1 < H:
                    act.wait_ge(pe_k, h + 2)
                    copy(kT[0:NO, (h + 1) % 2, :], ps[0:NO, 0, 0:LP]).then_inc(k_ready, 1)
                act.wait_ge(pe_pT, h + 1)
                copy(probsT[:, h % 2, 0:3 * P], ps[:, 2, 0:3 * P]).then_inc(pT_ready, 1)
                if h % 4 == 3:
                    g = h // 4
                    act.wait_ge(pe_p2T, g + 1)
                    copy(probs2T[:, g, 0:2, :], ps[:, 2, 0:2 * P].rearrange("p (k q) -> p k q", k=2)
                         ).then_inc(p2T_ready, 1)
                    copy(probs2T[0:LAST, g, 2, :], ps[0:LAST, 2, 2 * P:3 * P]).then_inc(p2T_ready, 1)
            act.wait_ge(pe_k, H)
            act.dma_start(norm2_g, a["norm2_g"].to_broadcast([P, D])).then_inc(in_g2, 16)
            act.wait_ge(pe_wo, 1)
            copy(y_short[32:64, :], ps[32:64, 0, :]).then_inc(short_out, 1)
            for j, t in enumerate((2, 0, 1)):
                n = ROWS[t]
                act.wait_ge(x_mid, (4, 4, 6)[j])
                act.activation(sq_mid[0:n, :], x[0:n, t, :], ACT.Square, accum_out=small[0:n, t:t + 1]
                               ).then_inc(sumsq, 1)
                act.wait_ge(meansq, 4 + j)
                act.activation(small[0:n, 8 + t:9 + t], small[0:n, 4 + t:5 + t], ACT.Sqrt).then_inc(root, 1)
            for j, (t, bank) in enumerate(((2, 0), (0, 2), (1, 4))):
                act.wait_ge(pe_h2T, 2 * j + 1)
                copy(hT[:, 0:4, P * t:P * t + ROWS[t]],
                     ps[:, bank, :].rearrange("p (k n) -> p k n", k=4)[:, :, 0:ROWS[t]]).then_inc(h2T_act, 1)
            act.wait_ge(top_ready, 1)
            act.activation(rt[:, 1, :, :], rt[:, 0, :, :], ACT.Exp).then_inc(e_top, 1)

            def take_gathered(count):
                act.wait_ge(pe_gather, count)
                copy(xg, ps[:, 6:8, :].rearrange("p b (k s) -> p (b k) s", k=4)).then_inc(xg_ready, 1)

            def pair(n, extra, ahead):
                if not ahead:
                    take_gathered(n + extra + 1)
                act.wait_ge(pe_pick, n + 1)
                act.wait_ge(pe_comb, 3 * n + 1)
                copy(pickT, ps[:, 7, 0:NT * P].rearrange("p (t n) -> p t n", t=NT)).then_inc(pickT_ready, 1)
                for u in range(2):
                    half_row = slice(512 * u, 512 * u + 512)
                    act.wait_ge(gate_ready, 2 * n + u + 1)
                    act.activation(sgm[:, half_row], gate[:, half_row], ACT.Sigmoid, scale=ALPHA
                                   ).then_inc(sgm_ready, 1)
                act.wait_ge(pe_hidT, 2 * n + 1)
                copy(hidT[:, 0:4, :], ps[:, 4, :].rearrange("p (j n) -> p j n", j=4)).then_inc(hidT_act, 1)
                if ahead:
                    take_gathered(n + 2)
                for u in range(2):
                    if u == 0:
                        act.wait_ge(pe_down, n + 1)
                    else:
                        act.wait_ge(slot_free[5], 2 * n + 3)
                    copy(ye[:, 512 * u:512 * u + 512], ps[:, u, :]).then_inc(ye_ready, 1)

            act.wait_ge(rank_ready, 1)
            act.wait_ge(out_small, 144)
            take_gathered(1)
            with act.Fori(0, NP) as p:
                pair(p, 0, True)
            act.wait_ge(most_ready, 1)
            count = act.value_load(most_i[0:1, 0:1], min_val=0, max_val=T)
            with act.If(count > SL):
                with act.Fori(0, PASSES - 1) as j:
                    with act.Fori(0, NP) as p:
                        pair(j * NP + p + NP, 1, False)
            act.wait_ge(y_final, 2)
            row_norm(act, 2)

        @block.vector
        def _(dve):
            steps = [0]

            def link(ins):
                steps[0] += 1
                ins.then_inc(dve_step, 1)
                dve.wait_ge(dve_step, steps[0])

            def row_scale(n0):
                dve.wait_ge(sumsq, 3 * n0 + 3)
                dve.tensor_scalar(small[:, 4:4 + NT], small[:, 0:NT], 1.0 / D, EPS, ALU.mult, ALU.add
                                  ).then_inc(meansq, 1)
                dve.wait_ge(root, 1 if n0 == 0 else 7)
                link(dve.reciprocal(small[:, 16:16 + NT], small[:, 8:8 + NT]))

            link(dve.memset(small, 1.0))
            dve.memset(x[:, 2, :], 0.0).then_inc(x_zero, 1)
            dve.wait_ge(in_pt, 16)
            dve.wait_ge(in_const, 16)
            for g in range(4):
                q = slice(32 * g, 32 * g + 32)
                dve.tensor_scalar(idx[q, :], pt[q, g::4], 32.0, const["mod32"][q, :], ALU.mult, ALU.add
                                  ).then_inc(idx_ready, 1)
            row_scale(0)
            for t in range(NT):
                n = ROWS[t]
                dve.tensor_scalar(xn[0:n, t, :], x[0:n, t, :], small[0:n, 16 + t:17 + t], None, ALU.mult
                                  ).then_inc(xn_ready, 1)
            dve.wait_ge(vec_ready, 1)
            for k in range(1, KD, 2):
                dve.wait_ge(pe_hT, k + 1)
                dve.tensor_scalar(hT[:, k, :], ps[:, k % 4, 0:T], vecT[:, k:k + 1], None, ALU.mult).then_inc(hT_dve, 1)
            for j in range(4):
                dve.wait_ge(pe_z, j + 1)
                dve.tensor_copy(zT[:, j, :], ps[:, 4 + j, 0:T]).then_inc(z_copied, 1)
            dve.wait_ge(pe_z, 5)
            dve.tensor_tensor(kr_cs[0:2 * R, :], ps[0:2 * R, 0, 0:T], const["rope0"][0:2 * R, :], ALU.mult
                              ).then_inc(kr_rot, 1)
            for j in range(2):
                dve.wait_ge(pe_stat, j + 1)
                dve.tensor_scalar(r_bc[:, j, :], ps[:, 1 + j, 0:T], 1.0 / C, EPS, ALU.mult, ALU.add
                                  ).then_inc(meansq, 1)
            for j in range(2):
                dve.wait_ge(root, 2 + j)
                dve.reciprocal(r_bc[:, j, :], r_bc[:, j, :]).then_inc(r_ready, 1)
            dve.wait_ge(r_ready, 2)
            dve.wait_ge(z_copied, 4)
            link(dve.tensor_tensor(rope_q, const["rope"], r_bc[:, 0, :], ALU.mult))
            for k in range(CT):
                col = 2 * KD + CT + k
                dve.scalar_tensor_tensor(out=cT[:, k, :], in0=zT[:, 2 + k, :], scalar=vecT[:, col:col + 1],
                                         in1=r_bc[:, 1, :], op0=ALU.mult, op1=ALU.mult).then_inc(c_ready, 1)
            for g in range(G):
                dve.wait_ge(p_prompt, g + 1)
                dve.tensor_copy(s_ext[:, g, :, HIST], ps[:, 6 + g % 2, LP:T]).then_inc(p_sample, 1)
            for h in range(H):
                dve.wait_ge(pe_q, h + 1)
                dve.tensor_tensor(qT[:, h, 0:T], ps[:, 1 + h % 4, 0:T], rope_q, ALU.mult).then_inc(q_ready, 1)
            dve.wait_ge(pe_prow, 1)
            link(dve.tensor_copy(p_rows[0:HIST, :], ps[0:HIST, 5, :]))
            dve.tensor_copy(s_rows[0:NB, :], ps[0:NB, 6, :]).then_inc(prow_ready, 1)
            dve.wait_ge(hist_ready, 1)
            dve.wait_ge(p_sample, G)
            for g in range(G):
                w = 2 << g
                link(dve.tensor_reduce(small[:, 32:32 + NB], s_ext[:, g, :, 16 - w:16], AX.X, ALU.add))
                m = dve.scalar_tensor_tensor(out=pooled[:, g, LP:T], in0=small[:, 32:32 + NB], scalar=1.0 / w,
                                             in1=s_ext[:, g, :, HIST], op0=ALU.mult, op1=ALU.subtract)
                if g < G - 1:
                    link(m)
            m.then_inc(p_sample, 1)
            dve.wait_ge(pe_ql, 2)
            dve.wait_ge(zeros_ready, 4)
            for k in range(CT):
                dve.tensor_copy(qL[:, k, :, 0:H], ps[:, 7, k * 64:k * 64 + 64].rearrange("p (h b) -> p b h", h=H)
                                ).then_inc(ql_ready, 1)
            dve.tensor_copy(qR[:, :, 0:H], ps[:, 0, 0:64].rearrange("p (h b) -> p b h", h=H)).then_inc(ql_ready, 1)
            for t in range(NT):
                dve.wait_ge(pe_cout, t + 1)
                dve.tensor_copy(c_out[0:ROWS[t], t, :], ps[0:ROWS[t], 5 + t, 0:C + R]).then_inc(cout_ready, 1)
            dve.wait_ge(ql_ready, 3)

            def maxima(b, one):
                dve.wait_ge(s_done, b + 1)
                dve.tensor_reduce(stats[:, 0, one], ps[:, 6, :], AX.X, ALU.max).then_inc(s_max, 1)
                dve.wait_ge(s_max, 2 * b + 1)
                dve.tensor_scalar(small[:, 12:13], stats[:, 0, one], -SCALE, None, ALU.mult).then_inc(s_max, 1)

            def sums(b, one):
                dve.wait_ge(e_ready, b + 1)
                dve.tensor_copy(stats[:, 1, one], small[:, 14:15]).then_inc(sum_kept, 1)

            def batch(b, u, count):
                one = slice(b, b + 1) if count is not None else bass.ds(b, 1)
                before = slice(0, 1) if count == 1 else bass.ds(b - 1, 1)
                if count != 0:
                    maxima(b - 1, before)
                dve.tensor_copy(qLb[:, u, :, :], qL[:, :, one, :].rearrange("p k b h -> p k (b h)")
                                ).then_inc(q_batch, 1)
                dve.tensor_tensor(qRb[:, u, :, :], qR[:, one, :].to_broadcast([P, 4, 32]),
                                  const["block"].unsqueeze(2).to_broadcast([P, 4, 32]), ALU.mult
                                  ).then_inc(q_batch, 1)
                for s in range(4):
                    dve.wait_ge(pe_kt, 5 * b + (1, 2, 4, 5)[s])
                    dve.tensor_copy(keysT[:, 1, 512 * s:512 * s + 512], ps[:, 3 * (s % 2) + 1, :]).then_inc(kt_dve, 1)
                    if s == 1:
                        dve.wait_ge(pe_kt, 5 * b + 3)
                        dve.tensor_copy(kropeT, ps[:, 2, :]).then_inc(kt_dve, 1)
                        if count != 0:
                            sums(b - 1, before)

            batch(0, 0, 0)
            batch(1, 1, 1)
            with dve.Fori(0, (NB - 2) // NBUF) as i:
                for j in range(NBUF):
                    batch(3 * i + 2 + j, (2 + j) % NBUF, None)
            maxima(NB - 1, slice(NB - 1, NB))
            sums(NB - 1, slice(NB - 1, NB))
            dve.wait_ge(sum_kept, NB)
            dve.wait_ge(o_ready, NB)
            prod = at(merge0, 3 * 64)
            for k in range(CT):
                link(dve.tensor_tensor(prod[:, 64 * k:64 * k + 64].rearrange("p (b h) -> p b h", b=NB),
                                       qL[:, k, :, 0:H], cT[:, k, LP:T].unsqueeze(2).to_broadcast([P, NB, H]),
                                       ALU.mult))
            dve.tensor_tensor(prod[0:R, 128:192].rearrange("p (b h) -> p b h", b=NB), qR[0:R, :, 0:H],
                              krT[0:R, LP:T].unsqueeze(2).to_broadcast([R, NB, H]), ALU.mult).then_inc(merge_in, 1)
            dve.wait_ge(pe_merge, 1)
            sN = at(merge0 + 912 + 32, 8)[0:NB, :]
            top1 = at(merge0 + 912 + 40, 8)[0:NB, :]
            tmp = at(merge0 + 192, P)[0:NB, :]
            link(dve.tensor_tensor(tmp[:, 0:64], ps[0:NB, 0, 0:64], const["diag"][0:NB, :], ALU.mult))
            link(dve.tensor_reduce(sN, tmp[:, 0:64].rearrange("p (b h) -> p h b", b=NB), AX.X, ALU.add))
            mx = ps[0:NB, 1, 0:P].rearrange("p (s h) -> p s h", s=4)
            link(dve.tensor_reduce(top1, mx[:, :, 0:H].rearrange("p s h -> p h s"), AX.X, ALU.max))
            link(dve.tensor_tensor(top1, top1, sN, ALU.max))
            link(dve.memset(tmp, 0.0))
            link(dve.tensor_tensor(tmp.rearrange("p (s h) -> p s h", s=4)[:, :, 0:H], mx[:, :, 0:H],
                                   top1.unsqueeze(1).to_broadcast([NB, 4, H]), ALU.subtract))
            dve.tensor_tensor(at(merge0 + 896, 8)[0:NB, :], sN, top1, ALU.subtract).then_inc(merge_in, 1)
            dve.wait_ge(merge_act, 2)
            w4 = at(merge0 + 320, P)[0:NB, :]
            wN = at(merge0 + 904, 32)[0:NB, 0:H]
            den = at(merge0 + 912 + 48, 8)[0:NB, :]
            link(dve.tensor_tensor(tmp, w4, ps[0:NB, 1, P:2 * P], ALU.mult))
            link(dve.tensor_reduce(den, tmp.rearrange("p (s h) -> p s h", s=4)[:, :, 0:H]
                                   .rearrange("p s h -> p h s"), AX.X, ALU.add))
            link(dve.tensor_tensor(den, den, wN, ALU.add))
            link(dve.reciprocal(den, den))
            wrow = at(merge0 + 448, P)[0:NB, :]
            link(dve.memset(wrow, 0.0))
            link(dve.tensor_tensor(wrow.rearrange("p (s h) -> p s h", s=4)[:, :, 0:H],
                                   w4.rearrange("p (s h) -> p s h", s=4)[:, :, 0:H],
                                   den.unsqueeze(1).to_broadcast([NB, 4, H]), ALU.mult))
            link(dve.tensor_tensor(wN, wN, den, ALU.mult))
            dve.tensor_tensor(at(merge0 + 576, 64)[0:NB, :].rearrange("p (b h) -> p b h", b=NB),
                              const["diag"][0:NB, :].rearrange("p (b h) -> p b h", b=NB),
                              wN.unsqueeze(1).to_broadcast([NB, NB, H]), ALU.mult).then_inc(merge_in, 1)
            dve.wait_ge(pe_merge, 2)
            wcol = at(merge0 + 704, 8)
            dve.tensor_copy(wcol, ps[:, 2, 0:NB]).then_inc(merge_in, 1)
            dve.wait_ge(merge_in, 4)
            dve.tensor_tensor(at(merge0 + 640, 64).rearrange("p (b h) -> p b h", b=NB),
                              const["headsel"].unsqueeze(1).to_broadcast([P, NB, H]),
                              wcol.unsqueeze(2).to_broadcast([P, NB, H]), ALU.mult).then_inc(merge_in, 1)
            dve.wait_ge(pe_merge, 3)
            oL = at(merge0 + 768, CT * 64)
            dve.tensor_tensor(prod[:, 0:128].rearrange("p (k b h) -> p k b h", k=CT, b=NB),
                              cT[:, :, LP:T].unsqueeze(3).to_broadcast([P, CT, NB, H]),
                              ps[:, 3, 0:64].rearrange("p (b h) -> p b h", b=NB).unsqueeze(1).to_broadcast([P, CT, NB, H]), ALU.mult).then_inc(merge_in, 1)
            dve.wait_ge(merge_in, 6)
            dve.tensor_tensor(oL, prod[:, 0:128], ps[:, 4, 0:128], ALU.add).then_inc(merge_in, 1)
            dve.wait_ge(merge_in, 7)
            dve.wait_ge(pe_merge, 4)
            dve.tensor_copy(aS, ps[:, 5, 0:64].rearrange("p (h b) -> p h b", h=H)).then_inc(merge_in, 1)
            dve.wait_ge(merge_in, 8)
            dve.wait_ge(out_pool, 32)

            for h in range(H):
                E = probs[:, h % 2, :]
                dve.wait_ge(pe_s, 2 * h + 1)
                if h >= 2:
                    dve.wait_ge(pe_pT, h - 1)
                m1 = const["mask1"]
                link(dve.tensor_tensor_reduce(E[:, 0:P], ps[:, 1, 0:P], m1[:, P:2 * P], 1.0, NEG, ALU.add, ALU.max,
                                              small[:, 18:19]))
                link(dve.tensor_tensor_reduce(E[:, P:3 * P], ps[:, 1, P:3 * P], m1, 1.0, NEG, ALU.add, ALU.max,
                                              small[:, 19:20]))
                if h:
                    dve.wait_ge(p_exp, 2 * h)
                dve.tensor_scalar(small[:, 20:22], small[:, 18:20], -SCALE, None, ALU.mult).then_inc(s_masked, 1)
                dve.wait_ge(p_exp, 2 * h + 2)
                link(dve.reciprocal(small[:, 26:28], small[:, 24:26]))
                link(dve.tensor_scalar(E[:, 0:P], E[:, 0:P], small[:, 26:27], None, ALU.mult))
                dve.tensor_scalar(E[:, P:3 * P], E[:, P:3 * P], small[:, 27:28], None, ALU.mult).then_inc(p_norm, 1)
                if h % 4 == 3:
                    g = h // 4
                    dve.wait_ge(pe_s, 2 * h + 2)
                    link(dve.tensor_tensor_reduce(probs_last, ps[:, 7, 0:LP], const["mask2"], 1.0, NEG, ALU.add,
                                                  ALU.max, small[:, 29:30]))
                    dve.tensor_scalar(small[:, 28:29], small[:, 29:30], -SCALE, None, ALU.mult).then_inc(s2_masked, 1)
                    dve.wait_ge(p2_exp, g + 1)
                    link(dve.reciprocal(small[:, 31:32], small[:, 30:31]))
                    dve.tensor_scalar(probs_last, probs_last, small[:, 31:32], None, ALU.mult).then_inc(p2_norm, 1)
                dve.wait_ge(gab_exp, h + 1)
                link(dve.tensor_scalar(sig[:, :, :], sig[:, :, :], 1.0, None, ALU.add))
                link(dve.reciprocal(sig[:, :, :], sig[:, :, :]))
                dve.wait_ge(pe_y, h + 1)
                dve.scalar_tensor_tensor(out=mT[:, h, :], in0=ps[:, 6, 0:T], scalar=vecT[:, KD + h:KD + h + 1],
                                         in1=sig[:, 1, :], op0=ALU.mult, op1=ALU.mult).then_inc(y_merged, 1)
                dve.wait_ge(y_merged, h + 1)
                link(dve.tensor_copy(sga_last[:, h, :], sig[:, 0, 2 * P:LP]))
                link(dve.tensor_tensor(small[:, 48:48 + NB], aS[:, h, :], sig[:, 0, LP:T], ALU.mult))
                link(dve.tensor_tensor(mT[:, h, LP:T], mT[:, h, LP:T], small[:, 48:48 + NB], ALU.add))
                dve.wait_ge(pe_a, h + 1)
                link(dve.tensor_tensor(sig[:, 0, 0:2 * P], ps[:, 3, 0:2 * P], sig[:, 0, 0:2 * P], ALU.mult))
                dve.tensor_tensor(mT[:, h, 0:2 * P], mT[:, h, 0:2 * P], sig[:, 0, 0:2 * P], ALU.add
                                  ).then_inc(a_merged, 1)
                if h % 4 == 3:
                    g = h // 4
                    last = small2.rearrange("p (h t) -> p h t", h=4)
                    dve.wait_ge(pe_a2, g + 1)
                    link(dve.tensor_tensor(last, ps[:, 7, 0:4 * LAST].rearrange("p (h t) -> p h t", h=4),
                                           sga_last[:, 4 * g:4 * g + 4, :], ALU.mult))
                    dve.tensor_tensor(mT[:, 4 * g:4 * g + 4, 2 * P:LP], mT[:, 4 * g:4 * g + 4, 2 * P:LP], last,
                                      ALU.add).then_inc(a2_merged, 1)
            dve.wait_ge(out_small, 144)
            link(dve.memset(lg, 0.0))

            def add_half(t, n, bank, count):
                dve.wait_ge(pe_wo, count)
                xr = x[0:ROWS[t], t, 512 * n:512 * n + 512]
                dve.tensor_tensor(xr, xr, ps[0:ROWS[t], bank, :], ALU.add).then_inc(x_mid, 1)

            def scale_rows(t, j):
                n = ROWS[t]
                dve.wait_ge(sumsq, 4 + j)
                dve.tensor_scalar(small[0:n, 4 + t:5 + t], small[0:n, t:t + 1], 1.0 / D, EPS, ALU.mult, ALU.add
                                  ).then_inc(meansq, 1)
                dve.wait_ge(root, 4 + j)
                link(dve.reciprocal(small[0:n, 16 + t:17 + t], small[0:n, 8 + t:9 + t]))
                dve.scalar_tensor_tensor(out=h2[0:n, t, :], in0=x[0:n, t, :], scalar=small[0:n, 16 + t:17 + t],
                                         in1=norm2_g[0:n, :], op0=ALU.mult, op1=ALU.mult).then_inc(h2_ready, 1)

            def take_h2T(t, j, bank):
                dve.wait_ge(pe_h2T, 2 * j + 2)
                dve.tensor_copy(hT[:, 4:8, P * t:P * t + ROWS[t]],
                                ps[:, bank, :].rearrange("p (k n) -> p k n", k=4)[:, :, 0:ROWS[t]]
                                ).then_inc(h2T_dve, 1)

            dve.wait_ge(short_out, 1)
            add_half(2, 0, 0, 1)
            add_half(0, 0, 2, 2)
            add_half(0, 1, 3, 3)
            add_half(2, 1, 1, 4)
            dve.wait_ge(in_g2, 16)
            dve.wait_ge(x_mid, 4)
            scale_rows(2, 0)
            scale_rows(0, 1)
            add_half(1, 0, 4, 5)
            add_half(1, 1, 5, 6)
            take_h2T(2, 0, 1)
            take_h2T(0, 1, 3)
            dve.wait_ge(x_mid, 6)
            scale_rows(1, 2)
            take_h2T(1, 2, 5)
            dve.wait_ge(pe_logit, NT)
            dve.wait_ge(in_router, 32)
            for t in range(NT):
                n = ROWS[t]
                link(dve.tensor_tensor(lg[0:n, t, :], ps[0:n, 7, NE * t:NE * t + NE], b_rt[0:n, :], ALU.add))
            for t in range(NT):
                link(dve.max(top8[:, t, :], lg[:, t, :]))
            best = top8[:, :, 0:1].to_broadcast([P, NT, NE])
            fourth = top8[:, :, 3:4].to_broadcast([P, NT, NE])
            dve.tensor_tensor(rt[:, 0, :, :], lg, best, ALU.subtract).then_inc(top_ready, 1)
            link(dve.tensor_tensor(rt[:, 2, :, :], lg, fourth, ALU.is_gt))
            link(dve.tensor_tensor(rt[:, 3, :, :], lg, fourth, ALU.is_equal))
            left = small[:, 36:36 + NT]
            link(dve.tensor_reduce(left, rt[:, 2, :, :], AX.X, ALU.add))
            link(dve.tensor_scalar(left, left, -1.0, 4.0, ALU.mult, ALU.add))
            for t in range(NT):
                link(dve.tensor_tensor_scan(sel[:, t, :], rt[:, 3, t, :], rt[:, 3, t, :], 0.0, ALU.add, ALU.max))
            link(dve.tensor_tensor(sel, sel, left.unsqueeze(2).to_broadcast([P, NT, NE]), ALU.is_le))
            link(dve.tensor_tensor(sel, sel, rt[:, 3, :, :], ALU.mult))
            link(dve.tensor_tensor(sel, sel, rt[:, 2, :, :], ALU.add))
            dve.tensor_tensor(sel, sel, const["valid"].unsqueeze(2).to_broadcast([P, NT, NE]), ALU.mult
                              ).then_inc(sel_ready, 1)
            dve.wait_ge(sel_ready, 1)
            dve.wait_ge(e_top, 1)
            link(dve.memset(gates, 0.0))
            link(dve.memset(rank, -1.0))
            link(dve.tensor_tensor(rt[:, 2, :, :], rt[:, 1, :, :], sel, ALU.mult))
            link(dve.tensor_reduce(left, rt[:, 2, :, :], AX.X, ALU.add))
            link(dve.tensor_scalar(left, left, 1.0e-30, None, ALU.max))
            link(dve.reciprocal(left, left))
            link(dve.tensor_tensor(gates[:, :, 0:NE], rt[:, 2, :, :], left.unsqueeze(2).to_broadcast([P, NT, NE]),
                                   ALU.mult))
            dve.wait_ge(pe_rank, 1)
            pr = ps[:, 5, 0:NT * NE].rearrange("p (t e) -> p t e", t=NT)
            link(dve.scalar_tensor_tensor(out=rank[:, :, 0:NE], in0=pr, scalar=1.0, in1=sel, op0=ALU.add,
                                          op1=ALU.mult))
            dve.tensor_scalar(rank[:, :, 0:NE], rank[:, :, 0:NE], -1.0, None, ALU.add).then_inc(rank_ready, 1)
            link(dve.tensor_reduce(most[0:1, 0:1], ps[0:1, 5, NT * NE:NT * NE + NE], AX.X, ALU.max))
            dve.tensor_copy(most_i[0:1, 0:1], most[0:1, 0:1]).then_inc(most_ready, 1)
            dve.wait_ge(rank_ready, 1)

            def choose(experts, count, first):
                iota = const["iota"][:, first].unsqueeze(1).unsqueeze(1).to_broadcast([P, NT, 2, SL])
                dve.tensor_tensor(pick, iota, rank[:, :, experts].unsqueeze(3).to_broadcast([P, NT, 2, SL]),
                                  ALU.is_equal).then_inc(pick_ready, 1)
                dve.wait_ge(pick_ready, count)
                dve.tensor_tensor(pickg, pick, gates[:, :, experts].unsqueeze(3).to_broadcast([P, NT, 2, SL]),
                                  ALU.mult).then_inc(pickg_ready, 1)

            def pair(p, n, extra, first, ahead):
                if ahead:
                    dve.wait_ge(pe_gather, n + 1)
                    dve.wait_ge(pe_pick, n + 1)
                    choose(bass.ds(2 * p + 2, 2), n + 2, first)
                else:
                    choose(bass.ds(2 * p, 2), n + extra + 1, first)
                for u in range(2):
                    at_u = slice(512 * u, 512 * u + 512)
                    if u == 0:
                        dve.wait_ge(pe_gu, n + 1)
                    else:
                        dve.wait_ge(slot_free[1], 2 * n + 3)
                    dve.tensor_scalar(gate[:, at_u], ps[:, u, :], LIMIT, None, ALU.min).then_inc(gate_ready, 1)
                    dve.tensor_scalar(up[:, at_u], ps[:, 2 + u, :], LIMIT, -LIMIT, ALU.min, ALU.max
                                      ).then_inc(up_ready, 1)
                    dve.wait_ge(gate_ready, 2 * n + u + 1)
                    dve.wait_ge(up_ready, 4 * n + 2 * u + 1)
                    dve.scalar_tensor_tensor(out=up[:, at_u], in0=up[:, at_u], scalar=1.0, in1=gate[:, at_u],
                                             op0=ALU.add, op1=ALU.mult).then_inc(up_ready, 1)
                    dve.wait_ge(up_ready, 4 * n + 2 * u + 2)
                    dve.wait_ge(sgm_ready, 2 * n + u + 1)
                    dve.tensor_tensor(hid[:, at_u], up[:, at_u], sgm[:, at_u], ALU.mult).then_inc(hid_ready, 1)
                dve.wait_ge(pe_hidT, 2 * n + 2)
                dve.tensor_copy(hidT[:, 4:8, :], ps[:, 5, :].rearrange("p (j n) -> p j n", j=4)
                                ).then_inc(hidT_dve, 1)
                dve.wait_ge(y_added, 3 * n + 3)
                for t in range(2):
                    dve.wait_ge(pe_comb, 3 * n + t + 2)
                    dve.tensor_tensor(x[:, t, :], x[:, t, :],
                                      ps[:, 2 + 2 * t:4 + 2 * t, :].rearrange("p b n -> p (b n)"),
                                      ALU.add).then_inc(y_added, 1)
                dve.wait_ge(pe_comb, 3 * n + 4)
                dve.tensor_tensor(y_last, y_last, ps[0:64, 6, :], ALU.add).then_inc(y_added, 1)

            link(dve.memset(y_last, 0.0))
            dve.sem_inc(y_added, 3)
            choose(slice(0, 2), 1, slice(0, SL))
            with dve.Fori(0, NP) as p:
                pair(p, p, 0, slice(0, SL), True)
            dve.wait_ge(y_added, 3 * NP + 3)
            dve.wait_ge(most_ready, 1)
            count = dve.value_load(most_i[0:1, 0:1], min_val=0, max_val=T)
            with dve.If(count > SL):
                with dve.Fori(0, PASSES - 1) as j:
                    with dve.Fori(0, NP) as p:
                        pair(p, j * NP + p + NP, 1, bass.ds((j + 1) * SL, SL), False)
                dve.wait_ge(y_added, 3 * NP * PASSES + 3)
            dve.memset(small[:, 40:41], 0.0).then_inc(y_final, 1)
            dve.wait_ge(pe_wo, 7)
            last = x[0:ROWS[2], 2, :]
            dve.tensor_tensor(last, last, ps[0:ROWS[2], 0:2, :].rearrange("p b n -> p (b n)"), ALU.add
                              ).then_inc(y_final, 1)
            dve.wait_ge(y_final, 2)
            row_scale(2)
            dve.wait_ge(in_final, 16)
            for t in range(NT):
                n = ROWS[t]
                dve.scalar_tensor_tensor(out=h2[0:n, t, :], in0=x[0:n, t, :], scalar=small[0:n, 16 + t:17 + t],
                                         in1=final_g[0:n, :], op0=ALU.mult, op1=ALU.mult).then_inc(y_final, 1)


INS = ("x_prompt", "x_sample", "cache_ckv", "cache_krope", "state_pool", "page_table", "meta_tokens", "norm1_g",
       "w_in", "q_norm_g", "w_uq", "kv_norm_g", "w_uk", "w_uv", "w_pool", "pool_scale", "w_out", "norm2_g",
       "w_router", "b_router", "w_gate_up", "b_gate_up", "w_down", "b_down", "final_norm_g")
OUTS = (("y_p", (1, SEQ, D)), ("y_s", (NB, 1, D)), ("ckv_p", (1, 1, LP, C)), ("krope_p", (1, 1, LP, R)),
        ("pool_p", (1, 1, HIST, PW)), ("ckv_s", (1, NB, 1, C)), ("krope_s", (1, NB, 1, R)),
        ("pool_s", (1, NB, HIST, PW)))


def constants():
    import numpy as np
    c = np.zeros((P, NCONST), np.float32)

    def put(name, value):
        start, n = CONST[name]
        c[:, start:start + n] = value

    row = np.arange(P)[:, None]
    pos = np.concatenate([np.arange(LP), np.full(NB, PAST)]).astype(np.float32)
    inv = (np.float32(10000.0) ** (-np.arange(R // 2, dtype=np.float32) / np.float32(R // 2))).astype(np.float32)
    angle = pos[None, :] * inv[:, None]
    cos, sin = np.cos(angle), np.sin(angle)
    put("ident", np.eye(P))
    put("rope", np.concatenate([np.ones((NO, T)), cos, cos, sin, sin]))
    put("rope0", np.concatenate([cos, cos, sin, sin, np.zeros((NO, T))]))
    put("fold", (row % R == np.arange(P) % R) & (row < 2 * R))
    put("fold_hi", (row % R == np.arange(P) % R) & (row >= NO))
    put("half", (row % 32 < 2) & (np.arange(P) // SL == row % 32))
    put("before", row < np.arange(P))
    put("iota", np.arange(PASSES * SL))
    put("mask1", np.where(np.arange(2 * P) <= P + row, 0.0, NEG))
    put("mask2", np.where(np.arange(LP) <= 2 * P + row % R, 0.0, NEG))
    put("headsel", row % R == np.arange(H))
    put("diag", np.arange(NB * H) // H == row)
    put("invcnt", 1.0 / np.minimum(np.repeat(2 << np.arange(G), 16), np.tile(np.arange(16), G) + 1))
    put("valid", np.arange(NT) * P + row < T)
    put("mod32", row % R)
    put("block", row // R == np.arange(4))
    return c


def kernel(**inputs):
    import numpy as np
    import concourse.bacc as bacc
    from concourse.bass_utils import run_bass_kernel_spmd

    nc = bacc.Bacc("TRN2", target_bir_lowering=False, num_devices=1)
    arrays, a = {}, {}
    for name in INS:
        v = np.ascontiguousarray(inputs[name])
        arrays[f"in_{name}"] = v
        a[name] = nc.dram_tensor(f"in_{name}", v.shape, mybir.dt.from_np(v.dtype), kind="ExternalInput").ap()
    arrays["in_consts"] = constants()
    a["consts"] = nc.dram_tensor("in_consts", (P, NCONST), F32, kind="ExternalInput").ap()
    o = {name: nc.dram_tensor(f"out_{name}", shape, F32, kind="ExternalOutput").ap() for name, shape in OUTS}
    build(nc, a, o)
    r = run_bass_kernel_spmd(nc, [arrays], core_ids=[0]).results[0]
    return tuple(r[f"out_{name}"] for name, _ in OUTS)
```

```python
from contextlib import ExitStack

import concourse.bass as bass
from concourse import mybir

F32 = mybir.dt.float32
I32 = mybir.dt.int32
U32 = mybir.dt.uint32
ALU = mybir.AluOpType
ACT = mybir.ActivationFunctionType
AX = mybir.AxisListType

P = 128
D = 1024
KD = D // P
SEQ, META, NB = 256, 16, 8
LP = META + SEQ
T = LP + NB
ROWS = (P, P, T - 2 * P)
NT = len(ROWS)
LAST = LP - 2 * P
H = 8
C = 256
CT = C // P
R = 32
NO = 64
QK = NO + R
PW = 512
G = 4
HIST = 15
PAGES, PAGE, PAST = 16, 128, 2048
NE = 32
SL = 64
NP = NE // 2
PASSES = -(-T // SL)
SCALE = (NO + R) ** -0.5
EPS = 1e-6
LIMIT, ALPHA = 7.0, 1.702
QKV = 2 * C + R
SLOT = 4096
NSLOT = 6
NBUF = 3
NEG = -1.0e30

CONST = {}
_at = 0
FRONT = (("rope", T), ("rope0", T), ("fold", P), ("fold_hi", P), ("mask1", 2 * P), ("mask2", LP), ("invcnt", G * 16),
         ("diag", NB * H), ("headsel", H), ("mod32", 1), ("block", 4))
for _name, _n in FRONT + (("ident", P), ("half", P), ("before", P), ("iota", PASSES * SL), ("valid", NT)):
    CONST[_name] = (_at, _n)
    _at += _n
NCONST = _at
VECS = 2 * KD + 2 * CT


def build(nc, a, o):
    with ExitStack() as ctx:
        def sem(name):
            return ctx.enter_context(nc.semaphore(name))

        arena = ctx.enter_context(nc.sbuf_tensor("arena", [P, 53200], F32))
        ps = ctx.enter_context(nc.psum_tensor("ps", [P, 8, 512], F32))
        top = [0]

        def at(start, n):
            return arena[:, start:start + n]

        def take(n):
            start = top[0]
            top[0] += n
            assert top[0] <= 53200, top[0]
            return start

        ring0 = take(NSLOT * SLOT)
        slot = [at(ring0 + SLOT * c, SLOT) for c in range(NSLOT)]
        w_uk = at(ring0, H * C)[0:NO, :].rearrange("p (h c) -> p h c", h=H)
        p_ext = at(ring0 + 2048, G * (16 + LP)).rearrange("p (g t) -> p g t", g=G)
        s_ext = at(ring0 + 2048 + G * (16 + LP), G * NB * 16).rearrange("p (g b t) -> p g b t", g=G, b=NB)
        sample0 = ring0 + SLOT
        keysT = at(sample0, 2 * PAST).rearrange("p (t k) -> p t k", t=2)
        kropeT = at(sample0 + 2 * PAST, 512)
        w_qkv = at(sample0, KD * QKV).rearrange("p (k n) -> p k n", k=KD)
        cache0 = sample0 + 2 * PAST + 512
        cache_c, cache_r = [], []
        for u in range(NBUF):
            base = cache0 + u * (PAGES * (C + R))
            cache_c.append(at(base, PAGES * C))
            cache_r.append(at(base + PAGES * C, PAGES * R))
        o_part = at(cache0 + NBUF * PAGES * (C + R), NB * C).rearrange("p (b c) -> p b c", b=NB)
        assert cache0 + NBUF * PAGES * (C + R) + NB * C <= ring0 + NSLOT * SLOT
        base = cache0 + PAGES * (C + R)
        w_uq = at(base, CT * H * QK).rearrange("p (k h n) -> p k h n", k=CT, h=H)
        w_uqx = at(base + CT * H * QK, CT * H * P).rearrange("p (k h n) -> p k h n", k=CT, h=H)
        w_kr = at(base + CT * H * (QK + P), KD * 2 * R).rearrange("p (k n) -> p k n", k=KD)
        w_p = slot[5].rearrange("p (k n) -> p k n", k=KD)

        x = at(take(NT * D), NT * D).rearrange("p (t d) -> p t d", t=NT)
        start = take(NT * D)
        xn = at(start, NT * D).rearrange("p (t d) -> p t d", t=NT)
        vals = xn
        h2 = xn
        hT0 = take(KD * T)
        hT = at(hT0, KD * T).rearrange("p (k t) -> p k t", k=KD)
        start = take(KD * T)
        zT = at(start, 4 * T).rearrange("p (k t) -> p k t", k=4)
        zsq0 = start + 4 * T
        zsq = at(zsq0, 4 * T).rearrange("p (k t) -> p k t", k=4)
        mT = at(start, KD * T).rearrange("p (k t) -> p k t", k=KD)
        start = take(CT * H * NO)
        norm2_start = start
        norm2_g = at(start, D)
        w_ukT = at(start, CT * H * NO).rearrange("p (k n) -> p k n", k=CT)
        start = take(CT * H * P)
        w_uv = at(start, CT * H * P).rearrange("p (h k v) -> p h k v", h=H, k=CT)
        w_rt = at(start, KD * NE).rearrange("p (k e) -> p k e", k=KD)
        b_rt = at(start + KD * NE, NE)
        w_pool = at(take(G * 256), G * 256).rearrange("p (g n) -> p g n", g=G)
        start = take(3 * T)
        r_bc = at(start, 2 * T).rearrange("p (k t) -> p k t", k=2)
        rope_q = at(start + 2 * T, T)
        probs2T = at(start, 2 * 3 * P).rearrange("p (g k q) -> p g k q", g=2, k=3)
        con0 = take(NCONST)
        const = {k: at(con0 + s, n) for k, (s, n) in CONST.items()}
        ones = at(take(P), P)
        vrow = at(take(P), P)[0:VECS, :]
        vecT = at(take(VECS), VECS)
        small = at(take(64), 64)
        small2 = at(take(64), 64)
        idx = at(take(NB * 4), NB * 4).bitcast(U32)

        pt = at(take(NB * PAGES), NB * PAGES).bitcast(I32)
        stats = at(take(2 * NB), 2 * NB).rearrange("p (k b) -> p k b", k=2)
        aS = at(take(H * NB), H * NB).rearrange("p (h b) -> p h b", h=H)
        sga_last = at(take(H * ROWS[2]), H * ROWS[2]).rearrange("p (h t) -> p h t", h=H)
        overlay = top[0]
        TQ = T + 8
        qT = at(take(H * TQ), H * TQ).rearrange("p (h t) -> p h t", h=H)
        kT = at(take(2 * LP), 2 * LP).rearrange("p (u t) -> p u t", u=2)
        krT = at(take(T), T)
        kr_cs = at(take(T), T)
        cT = at(take(CT * T), CT * T).rearrange("p (k t) -> p k t", k=CT)
        c_out = at(take(NT * (C + R)), NT * (C + R)).rearrange("p (t c) -> p t c", t=NT)
        start = take(G * T)
        pooled = at(start, G * T).rearrange("p (g t) -> p g t", g=G)
        qL = at(take(CT * NB * 32), CT * NB * 32).rearrange("p (k b h) -> p k b h", k=CT, b=NB)
        qR = at(take(NB * 32), NB * 32).rearrange("p (b h) -> p b h", b=NB)
        qLb = at(take(NBUF * CT * 32), NBUF * CT * 32).rearrange("p (u k h) -> p u k h", u=NBUF, k=CT)
        qRb = at(take(NBUF * 4 * 32), NBUF * 4 * 32).rearrange("p (u i h) -> p u i h", u=NBUF, i=4)
        probs0 = take(2 * 512)
        probs = at(probs0, 2 * 512).rearrange("p (u k) -> p u k", u=2)
        probsT0 = take(2 * 512)
        probsT = at(probsT0, 2 * 512).rearrange("p (u k) -> p u k", u=2)
        sig0 = take(2 * T + 16)
        sig = at(sig0, 2 * T).rearrange("p (k t) -> p k t", k=2)
        probs_s, probsT_s = at(probs0, 512), at(probs0 + 512, 512)
        pool_a = at(probsT0, LP)
        pool_b = at(probsT0 + 512, LP)
        sp_rows = at(probsT0, PW)[0:NB * HIST, :]
        p_rows = at(zsq0, PW)[0:HIST, :]
        s_rows = at(zsq0 + PW, PW)[0:NB, :]
        probs_last = kr_cs[:, 0:LP]
        scratch = [ring0 + 5 * SLOT]

        def part(n, rows=P):
            scratch[0] += n
            return at(scratch[0] - n, n)[0:rows, :]

        qk_new, m_tmp, m_w4, m_wrow = part(3 * 64), part(P, NB), part(P, NB), part(P, NB)
        m_diag, m_weights, m_wcol = part(64, NB), part(NB * 32).rearrange("p (b h) -> p b h", b=NB), part(8)
        m_diff, m_wnew, m_snew, m_top, m_den = (part(8, NB) for _ in range(5))
        o_rows = part(2 * C).rearrange("p (g c) -> p g c", g=2)
        o_lat = part(CT * H * 32).rearrange("p (k h b) -> p k h b", k=CT, h=H)
        assert scratch[0] <= cache0 + NBUF * PAGES * (C + R)
        y_short = r_bc.rearrange("p k t -> p (k t)")[:, 0:512]
        top_front = top[0]
        top[0] = overlay
        lg = at(take(NT * NE), NT * NE).rearrange("p (t e) -> p t e", t=NT)
        top8 = at(take(NT * 8), NT * 8).rearrange("p (t e) -> p t e", t=NT)
        rt = at(hT0 + 3 * D, 4 * NT * NE).rearrange("p (n t e) -> p n t e", n=4, t=NT)
        sel = at(take(NT * NE), NT * NE).rearrange("p (t e) -> p t e", t=NT)
        rank = at(take(NT * NE), NT * NE).rearrange("p (t e) -> p t e", t=NT)
        gates = at(take(NT * NE), NT * NE).rearrange("p (t e) -> p t e", t=NT)
        most = at(take(2), 2)
        most_i = at(take(2), 2).bitcast(I32)
        pick = at(take(NT * P), NT * P).rearrange("p (t u s) -> p t u s", t=NT, u=2)
        pickg = at(take(NT * P), NT * P).rearrange("p (t u s) -> p t u s", t=NT, u=2)
        pickT = at(hT0 + 4 * D, NT * P).rearrange("p (t n) -> p t n", t=NT)
        xg = at(norm2_start + SLOT, KD * P).rearrange("p (k s) -> p k s", k=KD)
        y_last = at(take(512), 512)[0:64, :]
        b_gate, b_up, b_down = x[32:34, 2, :], xn[32:34, 2, :], xn[64:66, 2, :]
        assert 4 * D + NT * P <= 2 * KD * T
        gate, sgm, up = (at(hT0 + D * j, D) for j in range(3))
        hidT = at(hT0 + 3 * D, D).rearrange("p (j n) -> p j n", j=KD)
        hid, ye = up, gate
        final_g = at(norm2_start + SLOT + KD * P, D)
        spare = [at(take(SLOT), SLOT), at(norm2_start, SLOT), at(take(SLOT), SLOT)]
        assert norm2_start + SLOT + KD * P + D <= con0 + sum(n for _, n in FRONT)
        top[0] = max(top[0], top_front)

        ident = const["ident"]
        half = [const["half"][r:r + 2, :] for r in (0, 32, 64)]

        in_x, in_const, in_vec, in_g2 = sem("in_x"), sem("in_const"), sem("in_vec"), sem("in_g2")
        in_qkv = [sem("in_qkv_a"), sem("in_qkv_b")]
        in_uq, in_uk, in_uv, in_pool, in_p, in_hist, in_pt = (
            sem(n) for n in ("in_uq", "in_uk", "in_uv", "in_pool", "in_p", "in_hist", "in_pt"))
        in_gab = [sem(f"in_gab{j}") for j in range(4)]
        in_wo = [sem("in_wo0"), sem("in_wo1")]
        in_router, in_final = sem("in_router"), sem("in_final")
        in_cache = [sem(f"in_cache{u}") for u in range(NBUF)]
        in_chunk = [sem(f"in_chunk{c}") for c in range(NSLOT)]
        in_bias, in_b_down = sem("in_bias"), sem("in_b_down")
        out_small, out_y = sem("out_small"), sem("out_y")
        ones_ready, kr_weights, uq_weights, zeros_ready, idx_ready = (
            sem(n) for n in ("ones_ready", "kr_weights", "uq_weights", "zeros_ready", "idx_ready"))
        dve_step, merge_step, pool_step = sem("dve_step"), sem("merge_step"), sem("pool_step")
        sumsq, meansq, root, xn_ready = sem("sumsq"), sem("meansq"), sem("root"), sem("xn_ready")
        pe_vec, vec_ready, pe_hT, hT_act, hT_dve = (
            sem(n) for n in ("pe_vec", "vec_ready", "pe_hT", "hT_act", "hT_dve"))
        pe_z, zsq_ready, z_copied, kr_rot = (sem(n) for n in ("pe_z", "zsq_ready", "z_copied", "kr_rot"))
        pe_stat, r_ready, c_ready = sem("pe_stat"), sem("r_ready"), sem("c_ready")
        pe_ukT, ukT_ready, pe_hist, hist_ready = (
            sem(n) for n in ("pe_ukT", "ukT_ready", "pe_hist", "hist_ready"))
        pe_p, p_prompt, p_sample, pooled_ready = (
            sem(n) for n in ("pe_p", "p_prompt", "p_sample", "pooled_ready"))
        pe_kr, kr_ready, kT_rope = sem("pe_kr"), sem("kr_ready"), sem("kT_rope")
        pe_q, q_ready, pe_v, v_ready = sem("pe_q"), sem("q_ready"), sem("pe_v"), sem("v_ready")
        pe_cout, cout_ready, pe_prow, prow_ready = (
            sem(n) for n in ("pe_cout", "cout_ready", "pe_prow", "prow_ready"))
        pe_ql, ql_ready = sem("pe_ql"), sem("ql_ready")
        pe_kt, kt_act, kt_dve, q_batch, s_done, s_max, e_ready = (
            sem(n) for n in ("pe_kt", "kt_act", "kt_dve", "q_batch", "s_done", "s_max", "e_ready"))
        pe_pt, pt_ready, pv_done, o_ready = (sem(n) for n in ("pe_pt", "pt_ready", "pv_done", "o_ready"))
        merge_in, pe_merge, merge_act, merge_read = (
            sem(n) for n in ("merge_in", "pe_merge", "merge_act", "merge_read"))
        pe_k, k_ready, pe_s, s_masked, p_exp, p_norm = (
            sem(n) for n in ("pe_k", "k_ready", "pe_s", "s_masked", "p_exp", "p_norm"))
        pe_pT, pT_ready, pe_a, a_merged = (sem(n) for n in ("pe_pT", "pT_ready", "pe_a", "a_merged"))
        pe_gab, gab_exp, sig_ready, pe_y, y_merged = (
            sem(n) for n in ("pe_gab", "gab_exp", "sig_ready", "pe_y", "y_merged"))
        s2_masked, p2_exp, p2_norm, pe_p2T, p2T_ready, pe_a2, a2_merged = (
            sem(n) for n in ("s2_masked", "p2_exp", "p2_norm", "pe_p2T", "p2T_ready", "pe_a2", "a2_merged"))
        pe_wo, x_mid = sem("pe_wo"), sem("x_mid")
        h2_ready, pe_h2T, h2T_act, h2T_dve = (sem(n) for n in ("h2_ready", "pe_h2T", "h2T_act", "h2T_dve"))
        pe_logit, top_ready, e_top, sel_ready, pe_rank, rank_ready, most_ready = (
            sem(n) for n in ("pe_logit", "top_ready", "e_top", "sel_ready", "pe_rank", "rank_ready", "most_ready"))
        slot_free = [sem(f"slot_free{c}") for c in range(NSLOT)]
        x_zero, sum_kept = sem("x_zero"), sem("sum_kept")
        pick_ready, pickg_ready, pe_gather, xg_ready = (
            sem(n) for n in ("pick_ready", "pickg_ready", "pe_gather", "xg_ready"))
        pe_gu, gate_ready, up_ready, sgm_ready, hid_ready = (
            sem(n) for n in ("pe_gu", "gate_ready", "up_ready", "sgm_ready", "hid_ready"))
        pe_pick, pickT_ready, pe_hidT, hidT_act, hidT_dve, pe_down, ye_ready = (
            sem(n) for n in ("pe_pick", "pickT_ready", "pe_hidT", "hidT_act", "hidT_dve", "pe_down", "ye_ready"))
        short_out = sem("short_out")
        pe_comb, y_added, y_final = sem("pe_comb"), sem("y_added"), sem("y_final")

        block = ctx.enter_context(nc.Block())

        win = a["w_in"].rearrange("l (k p) n -> p (l k) n", p=P)
        cache_c_rows = a["cache_ckv"].rearrange("l n (q i) c -> (l n q) (i c)", i=4)
        cache_r_rows = a["cache_krope"].rearrange("l n (q i) c -> (l n q) (i c)", i=4)
        gu_rows = a["w_gate_up"].rearrange("l e (k p) n -> p (l e k) n", p=P)
        dn_rows = a["w_down"].rearrange("l e (k p) n -> p (l e k) n", p=P)

        @block.sync
        def _(sp):
            sp.dma_start(x[0:META, 0, :], a["meta_tokens"]).then_inc(in_x, 16)
            sp.dma_start(x[META:P, 0, :], a["x_prompt"][0, 0:P - META, :]).then_inc(in_x, 16)
            sp.dma_start(x[:, 1, :], a["x_prompt"][0, P - META:2 * P - META, :]).then_inc(in_x, 16)
            sp.wait_ge(x_zero, 1)
            sp.dma_start(x[0:LAST, 2, :], a["x_prompt"][0, 2 * P - META:SEQ, :]).then_inc(in_x, 16)
            sp.dma_start(x[LAST:LAST + NB, 2, :], a["x_sample"][:, 0, :]).then_inc(in_x, 16)
            sp.dma_start(at(con0, NCONST), a["consts"]).then_inc(in_const, 16)
            for j in range(2):
                sp.dma_start(w_qkv[:, 4 * j:4 * j + 4, :], win[:, 4 * j:4 * j + 4, 0:QKV]).then_inc(in_qkv[j], 16)
            sp.dma_start(w_uk, a["w_uk"][0].rearrange("h n c -> n h c")).then_inc(in_uk, 16)
            sp.dma_start(w_uq, a["w_uq"][0].rearrange("(k p) (h n) -> p k h n", p=P, h=H)).then_inc(in_uq, 16)
            sp.dma_start(w_p, win[:, :, QKV:QKV + PW]).then_inc(in_p, 16)
            sp.dma_start(sp_rows, a["state_pool"][0].rearrange("b t c -> (b t) c")).then_inc(in_hist, 16)
            sp.dma_start(w_uv, a["w_uv"][0].rearrange("h (k p) v -> p h k v", p=P)).then_inc(in_uv, 16)
            sp.dma_start(w_pool, a["w_pool"][0].rearrange("g p n -> p g n")).then_inc(in_pool, 16)
            sp.dma_start(o["pool_s"][0, :, 0:HIST - 1, :], a["state_pool"][0, :, 1:HIST, :]).then_inc(out_small, 16)
            for j in range(4):
                if j == 0:
                    sp.wait_ge(pe_ql, 1)
                    sp.wait_ge(pe_prow, 1)
                    sp.wait_ge(pooled_ready, G)
                    sp.wait_ge(p_sample, G + 1)
                else:
                    sp.wait_ge(pv_done, NB)
                dst = slot[j].rearrange("p (k u n) -> p k u n", k=KD, u=2)
                for u in range(2):
                    col = QKV + PW + u * D + j * 256
                    sp.dma_start(dst[:, :, u, :], win[:, :, col:col + 256]).then_inc(in_gab[j], 16)
            for n in range(2):
                if n == 1:
                    sp.wait_ge(pe_merge, 6)
                sp.dma_start(slot[4 + n].rearrange("p (k n) -> p k n", k=KD),
                             a["w_out"][0].rearrange("(k p) n -> p k n", p=P)[:, :, 512 * n:512 * n + 512]
                             ).then_inc(in_wo[n], 16)
            sp.dma_start(w_rt, a["w_router"][0].rearrange("(k p) e -> p k e", p=P)).then_inc(in_router, 16)
            sp.dma_start(b_rt, a["b_router"].to_broadcast([P, NE])).then_inc(in_router, 16)

            def load(p, c, dst, signal):
                rows, k, count = (gu_rows, 2 * (c // 2), 2) if c < 8 else (dn_rows, 4 * (c // 2 - 4), 4)
                sp.dma_start(dst.rearrange("p (k n) -> p k n", k=count),
                             rows[:, bass.ds((2 * p + c % 2) * KD + k, count), :]).then_inc(signal, 16)

            def load_slots(p, n, chunks):
                for c in chunks:
                    s = c % NSLOT
                    sp.wait_ge(slot_free[s], 2 * n + 1 + c // NSLOT)
                    load(p, c, slot[s], in_chunk[s])

            def load_gu_bias(p, n):
                sp.wait_ge(slot_free[0], 2 * n + 1)
                for dst, col in ((b_gate, 0), (b_up, D)):
                    sp.dma_start(dst, a["b_gate_up"][0, bass.ds(2 * p, 2), col:col + D]).then_inc(in_bias, 16)

            def load_down_bias(p):
                sp.dma_start(b_down, a["b_down"][0, bass.ds(2 * p, 2), :]).then_inc(in_b_down, 16)

            def pair_weights(p, n):
                load_gu_bias(p, n)
                load_slots(p, n, range(NSLOT))
                load_down_bias(p)
                load_slots(p, n, range(NSLOT, 2 * NSLOT))

            load_gu_bias(0, 0)
            load_slots(0, 0, range(4))
            sp.wait_ge(pe_wo, 2)
            sp.wait_ge(out_small, 176)
            load(0, 6, spare[0], in_wo[0])
            sp.dma_start(final_g, a["final_norm_g"].rearrange("(a n) -> a n", a=1).to_broadcast([P, D])
                         ).then_inc(in_final, 16)
            load_slots(0, 0, range(4, 6))
            load(0, 8, spare[2], in_p)
            sp.wait_ge(top_ready, 1)
            load(0, 7, spare[1], in_wo[1])
            load_down_bias(0)
            for c in range(3):
                sp.wait_ge(slot_free[c], 2)
                load(1, c, slot[c], in_chunk[c])
            load_slots(0, 0, range(9, 12))
            load_gu_bias(1, 1)
            load_slots(1, 1, range(3, NSLOT))
            load_down_bias(1)
            load_slots(1, 1, range(NSLOT, 2 * NSLOT))
            with sp.Fori(2, NP) as p:
                pair_weights(p, p)
            sp.wait_ge(most_ready, 1)
            count = sp.value_load(most_i[0:1, 0:1], min_val=0, max_val=T)
            with sp.If(count > SL):
                with sp.Fori(0, PASSES - 1) as j:
                    with sp.Fori(0, NP) as p:
                        pair_weights(p, j * NP + p + NP)
            sp.wait_ge(y_final, 3)
            sp.dma_start(o["y_p"][0, 0:P - META, :], h2[META:P, 0, :]).then_inc(out_y, 16)
            sp.wait_ge(y_final, 4)
            sp.dma_start(o["y_p"][0, P - META:2 * P - META, :], h2[:, 1, :]).then_inc(out_y, 16)
            sp.wait_ge(y_final, 5)
            sp.dma_start(o["y_p"][0, 2 * P - META:SEQ, :], h2[0:LAST, 2, :]).then_inc(out_y, 16)
            sp.dma_start(o["y_s"][:, 0, :], h2[LAST:LAST + NB, 2, :]).then_inc(out_y, 16)
            sp.wait_ge(out_y, 64)

        @block.gpsimd
        def _(pool):
            made = [0]

            def link(ins):
                made[0] += 1
                ins.then_inc(pool_step, 1)
                pool.wait_ge(pool_step, made[0])

            pool.memset(ones, 1.0).then_inc(ones_ready, 1)
            pool.wait_ge(idx_ready, 4)

            def start_cache(b):
                u = b % NBUF
                for s in range(4):
                    off = bass.IndirectOffsetOnAxis(ap=idx[:, 4 * b + s:4 * b + s + 1], axis=0)
                    pool.indirect_dma_start(cache_c[u][:, 4 * C * s:4 * C * s + 4 * C], None, cache_c_rows, off
                                            ).then_inc(in_cache[u], 16)
                    pool.indirect_dma_start(cache_r[u][:, 4 * R * s:4 * R * s + 4 * R], None, cache_r_rows, off
                                            ).then_inc(in_cache[u], 16)

            start_cache(0)
            for j in range(2):
                pool.wait_ge(in_qkv[j], 16)
            link(pool.tensor_copy(w_kr[:, :, 0:R], w_qkv[:, :, 2 * C:QKV]))
            link(pool.tensor_scalar(w_kr[:, :, R:R + 16], w_qkv[:, :, 2 * C + 16:QKV], -1.0, None, ALU.mult))
            pool.tensor_copy(w_kr[:, :, R + 16:2 * R], w_qkv[:, :, 2 * C:2 * C + 16]).then_inc(kr_weights, 1)
            pool.wait_ge(in_uq, 16)
            pool.wait_ge(vec_ready, 1)
            for k in range(CT):
                g = vecT[:, 2 * KD + k:2 * KD + k + 1]
                link(pool.tensor_scalar(w_uqx[:, k, :, 0:QK], w_uq[:, k, :, :], g, None, ALU.mult))
                link(pool.tensor_scalar(w_uqx[:, k, :, QK:QK + 16], w_uq[:, k, :, NO + 16:QK], g, -1.0,
                                        ALU.mult, ALU.mult))
                pool.tensor_scalar(w_uqx[:, k, :, QK + 16:P], w_uq[:, k, :, NO:NO + 16], g, None,
                                   ALU.mult).then_inc(uq_weights, 1)
            pool.memset(qL[:], 0.0).then_inc(zeros_ready, 1)
            pool.memset(qR[:], 0.0).then_inc(zeros_ready, 1)
            pool.memset(p_ext[:, :, 0:16], 0.0).then_inc(zeros_ready, 1)
            pool.memset(qT[:, :, T:TQ], 0.0).then_inc(zeros_ready, 1)
            pool.wait_ge(pe_p, G)
            start_cache(2)
            pool.wait_ge(pe_q, H)
            start_cache(1)
            pool.wait_ge(p_prompt, G)
            pool.wait_ge(zeros_ready, 4)
            for g in range(G):
                w = 2 << g
                src = p_ext[:, g, :]
                link(pool.tensor_tensor(pool_a, src[:, 16:16 + LP], src[:, 15:15 + LP], ALU.add))
                now, other = pool_a, pool_b
                n = 2
                while n < w:
                    link(pool.tensor_copy(other[:, 0:n], now[:, 0:n]))
                    link(pool.tensor_tensor(other[:, n:LP], now[:, n:LP], now[:, 0:LP - n], ALU.add))
                    now, other = other, now
                    n *= 2
                link(pool.tensor_scalar(other[:, 16:LP], now[:, 16:LP], 1.0 / w, None, ALU.mult))
                link(pool.tensor_tensor(other[:, 0:16], now[:, 0:16],
                                        const["invcnt"].rearrange("p (g t) -> p g t", g=G)[:, g, :], ALU.mult))
                pool.tensor_tensor(pooled[:, g, 0:LP], other, src[:, 16:16 + LP], ALU.subtract
                                   ).then_inc(pooled_ready, 1)
                pool.wait_ge(pooled_ready, g + 1)
            for b in range(NBUF, NB):
                pool.wait_ge(pv_done, b - NBUF + 1)
                start_cache(b)

        @block.tensor
        def _(pe):
            mm = nc.tensor.matmul

            pe.wait_ge(in_vec, 64)
            pe.wait_ge(in_const, 16)
            nc.tensor.transpose(ps[:, 7, 0:VECS], vrow, ident[0:VECS, 0:VECS]).then_inc(pe_vec, 1)
            pe.wait_ge(xn_ready, NT)
            for k in range(KD):
                if k >= 4:
                    pe.wait_ge(hT_act if k % 2 == 0 else hT_dve, (k - 4) // 2 + 1)
                for t in range(NT):
                    m = nc.tensor.transpose(ps[:, k % 4, P * t:P * t + ROWS[t]],
                                            xn[0:ROWS[t], t, P * k:P * k + P], ident[0:ROWS[t], 0:ROWS[t]])
                m.then_inc(pe_hT, 1)
            pe.wait_ge(vec_ready, 1)
            for k in range(KD):
                pe.wait_ge(hT_act if k % 2 == 0 else hT_dve, k // 2 + 1)
                if k % 4 == 0:
                    pe.wait_ge(in_qkv[k // 4], 16)
                for j in range(4):
                    m = mm(ps[:, 4 + j, 0:T], w_qkv[:, k, P * j:P * j + P], hT[:, k, :],
                           start=(k == 0), stop=(k == KD - 1))
                    if k == KD - 1:
                        m.then_inc(pe_z, 1)
            pe.wait_ge(kr_weights, 1)
            for k in range(KD):
                m = mm(ps[0:2 * R, 0, 0:T], w_kr[:, k, :], hT[:, k, :], start=(k == 0), stop=(k == KD - 1))
            m.then_inc(pe_z, 1)
            pe.wait_ge(in_uk, 16)
            for k in range(CT):
                bank = 3 if k == 0 else 4
                if k == 1:
                    pe.wait_ge(zsq_ready, 1)
                    pe.wait_ge(z_copied, 1)
                for h in range(H):
                    m = nc.tensor.transpose(ps[:, bank, NO * h:NO * h + NO], w_uk[:, h, P * k:P * k + P],
                                            ident[0:NO, 0:NO])
                m.then_inc(pe_ukT, 1)
            pe.wait_ge(ones_ready, 1)
            for j in range(2):
                pe.wait_ge(zsq_ready, 2 * j + 2)
                for k in range(CT):
                    m = mm(ps[:, 1 + j, 0:T], ones, zsq[:, 2 * j + k, :], start=(k == 0), stop=(k == CT - 1))
                m.then_inc(pe_stat, 1)
            pe.wait_ge(in_hist, 16)
            pe.wait_ge(z_copied, 2)
            for g in range(G):
                m = nc.tensor.transpose(ps[:, 5, P * g:P * g + NB * HIST], sp_rows[:, P * g:P * g + P],
                                        ident[0:NB * HIST, 0:NB * HIST])
            m.then_inc(pe_hist, 1)
            pe.wait_ge(kr_rot, 1)
            mm(ps[:, 0, 0:T], const["fold"][0:2 * R, :], kr_cs[0:2 * R, :], start=True, stop=True).then_inc(pe_kr, 1)
            pe.wait_ge(in_p, 16)
            pe.wait_ge(zsq_ready, 4)
            pe.wait_ge(z_copied, 4)
            for g in range(G):
                bank = (6, 7, 6, 7)[g]
                if g >= 2:
                    pe.wait_ge(p_prompt, g - 1)
                    pe.wait_ge(p_sample, g - 1)
                for k in range(KD):
                    m = mm(ps[:, bank, 0:T], w_p[:, k, P * g:P * g + P], hT[:, k, :],
                           start=(k == 0), stop=(k == KD - 1))
                m.then_inc(pe_p, 1)
            pe.wait_ge(uq_weights, CT)
            pe.wait_ge(r_ready, 2)
            pe.wait_ge(ukT_ready, 2)
            for h in range(H):
                bank = 1 + h % 4
                if h >= 4:
                    pe.wait_ge(q_ready, h - 3)
                for k in range(CT):
                    m = mm(ps[:, bank, 0:T], w_uqx[:, k, h, :], zT[:, k, :], start=(k == 0), stop=(k == CT - 1))
                m.then_inc(pe_q, 1)
            pe.wait_ge(p_prompt, G)
            pe.wait_ge(p_sample, G)
            pe.wait_ge(hist_ready, 1)
            for g in range(G):
                m = nc.tensor.transpose(ps[0:HIST, 5, P * g:P * g + P], p_ext[:, g, 16 + LP - HIST:16 + LP], ident)
            for g in range(G):
                m = nc.tensor.transpose(ps[0:NB, 6, P * g:P * g + P], s_ext[:, g, :, HIST], ident)
            m.then_inc(pe_prow, 1)
            pe.wait_ge(q_ready, H)
            pe.wait_ge(zeros_ready, 4)
            for h in range(H):
                for k in range(CT):
                    m = mm(ps[:, 7, (k * H + h) * NB:(k * H + h) * NB + NB], w_uk[:, h, P * k:P * k + P],
                           qT[0:NO, h, LP:T], start=True, stop=True)
            m.then_inc(pe_ql, 1)
            pe.wait_ge(kr_ready, 1)
            mm(ps[:, 0, 0:H * NB].rearrange("p (h b) -> p h b", h=H), const["fold_hi"][NO:P, :],
               qT[NO:P, :, LP:T], start=True, stop=True).then_inc(pe_ql, 1)
            pe.wait_ge(c_ready, 2)
            pe.wait_ge(in_uv, 16)
            for t in range(NT):
                rows = ROWS[t] if t < 2 else LAST
                for n in range(2):
                    g = 2 * t + n
                    if g >= 4:
                        pe.wait_ge(v_ready, g - 3)
                    for k in range(CT):
                        m = mm(ps[0:rows, 1 + g % 4, :], cT[:, k, P * t:P * t + rows],
                               w_uv[:, 4 * n:4 * n + 4, k, :],
                               start=(k == 0), stop=(k == CT - 1))
                    m.then_inc(pe_v, 1)
            pe.wait_ge(prow_ready, 1)
            pe.wait_ge(ql_ready, 3)
            for t in range(NT):
                bank = 5 + t
                for k in range(CT):
                    nc.tensor.transpose(ps[0:ROWS[t], bank, P * k:P * k + P], cT[:, k, P * t:P * t + ROWS[t]], ident)
                nc.tensor.transpose(ps[0:ROWS[t], bank, C:C + R], krT[0:R, P * t:P * t + ROWS[t]],
                                    ident[0:R, 0:R]).then_inc(pe_cout, 1)
            pe.wait_ge(v_ready, 6)
            pe.wait_ge(cout_ready, 3)

            def turn_latents(u, s):
                for i in range(4):
                    key = cache_c[u][:, (4 * s + i) * C:(4 * s + i + 1) * C]
                    for k in range(CT):
                        m = nc.tensor.transpose(ps[:, 3 * (s % 2) + k, P * i:P * i + P], key[:, P * k:P * k + P], ident)
                m.then_inc(pe_kt, 1)

            def turn_rope(u):
                for s in range(4):
                    m = nc.tensor.transpose(ps[:, 2, P * s:P * s + P], cache_r[u][:, P * s:P * s + P], ident)
                m.then_inc(pe_kt, 1)

            def score(b, u, first):
                pe.wait_ge(q_batch, 2 * b + 2)
                if not first:
                    pe.wait_ge(e_ready, b)
                for k in range(CT):
                    for s in range(4):
                        if s == 3:
                            pe.wait_ge(kt_act if k == 0 else kt_dve, (4 * b + 4) if k == 0 else (5 * b + 5))
                        mm(ps[32 * s:32 * s + 32, 6, :], qLb[:, u, k, :], keysT[:, k, 512 * s:512 * s + 512],
                           start=(k == 0), stop=False, skip_group_check=True)
                for i in range(4):
                    for s in range(4):
                        m = mm(ps[32 * s:32 * s + 32, 6, P * i:P * i + P], qRb[:, u, i, :],
                               kropeT[:, P * s:P * s + P], start=False, stop=True,
                               skip_group_check=True)
                m.then_inc(s_done, 1)

            def turn_probs(b, first):
                pe.wait_ge(e_ready, b + 1)
                if not first:
                    pe.wait_ge(pt_ready, b)
                for i in range(4):
                    m = nc.tensor.transpose(ps[:, 7, P * i:P * i + P], probs_s[:, P * i:P * i + P], ident)
                m.then_inc(pe_pt, 1)

            def weigh(b, u, first):
                pe.wait_ge(pt_ready, b + 1)
                if not first:
                    pe.wait_ge(o_ready, b)
                for i in range(4):
                    for s in range(4):
                        m = mm(ps[32 * s:32 * s + 32, 5, 0:C], probsT_s[:, P * i + 32 * s:P * i + 32 * s + 32],
                               cache_c[u][:, (4 * s + i) * C:(4 * s + i + 1) * C], start=(i == 0), stop=(i == 3))
                m.then_inc(pv_done, 1)

            def batch(b, u, loads, count):
                pe.wait_ge(in_cache[u], 128 * loads)
                turn_latents(u, 0)
                turn_latents(u, 1)
                turn_rope(u)
                if count != 0:
                    turn_probs(b - 1, count == 1)
                pe.wait_ge(kt_act, 4 * b + 1)
                pe.wait_ge(kt_dve, 5 * b + 1)
                turn_latents(u, 2)
                if count != 0:
                    weigh(b - 1, (u - 1) % NBUF, count == 1)
                pe.wait_ge(kt_act, 4 * b + 2)
                pe.wait_ge(kt_dve, 5 * b + 2)
                turn_latents(u, 3)
                pe.wait_ge(kt_act, 4 * b + 3)
                pe.wait_ge(kt_dve, 5 * b + 4)
                score(b, u, count == 0)

            batch(0, 0, 1, 0)
            batch(1, 1, 1, 1)
            with pe.Fori(0, (NB - 2) // NBUF) as i:
                batch(3 * i + 2, 2, i + 1, None)
                batch(3 * i + 3, 0, i + 2, None)
                batch(3 * i + 4, 1, i + 2, None)
            turn_probs(NB - 1, False)
            weigh(NB - 1, (NB - 1) % NBUF, False)
            def merge_stage(h):
                if h:
                    pe.wait_ge(y_merged, h)
                if h == 0:
                    pe.wait_ge(merge_in, 1)
                    for k in range(3):
                        n = P if k < 2 else R
                        mm(ps[0:NB, 6, 0:64], ones[0:n, 0:NB], qk_new[0:n, 64 * k:64 * k + 64],
                           start=(k == 0), stop=(k == 2))
                    for k in range(2):
                        m = nc.tensor.transpose(ps[0:NB, 6, 64 + P * k:64 + P * k + P], stats[:, k, :], ident)
                elif h == 1:
                    pe.wait_ge(merge_in, 3)
                    nc.tensor.transpose(ps[:, 6, 0:NB], m_wrow, ident[0:NB, 0:NB])
                    m = mm(ps[:, 6, 8:72], ones[0:NB, :], m_diag, start=True, stop=True)
                elif h == 2:
                    pe.wait_ge(merge_in, 4)
                    pe.wait_ge(o_ready, NB)
                    for g in range(2):
                        for j in range(4):
                            b = 4 * g + j
                            m = mm(ps[32 * j:32 * j + 32, 6, C * g:C * g + C], m_weights[:, b, :], o_part[:, b, :],
                                   start=True, stop=True)
                elif h == 3:
                    pe.wait_ge(merge_read, 3)
                    for g in range(2):
                        for k in range(CT):
                            m = nc.tensor.transpose(ps[:, 6, C * g + P * k:C * g + P * k + P],
                                                    o_rows[:, g, P * k:P * k + P], ident)
                elif h == 4:
                    pe.wait_ge(merge_in, 6)
                    for g in range(2):
                        for k in range(CT):
                            for j in range(4):
                                m = mm(ps[32 * j:32 * j + 32, 6, P * g:P * g + P], o_lat[:, k, 4 * g + j, :],
                                       w_uv[:, 4 * g + j, k, :], start=(k == 0), stop=(k == CT - 1))
                elif h == 5:
                    pe.wait_ge(merge_read, 5)
                    for g in range(2):
                        m = nc.tensor.transpose(ps[:, 6, P * g:P * g + P], o_rows[:, 0, P * g:P * g + P], ident)
                m.then_inc(pe_merge, 1)

            def keys(h):
                if h >= 2:
                    pe.wait_ge(k_ready, h)
                for k in range(CT):
                    m = mm(ps[0:NO, 0, 0:LP], w_ukT[:, k, NO * h:NO * h + NO], cT[:, k, 0:LP],
                           start=(k == 0), stop=(k == CT - 1))
                m.then_inc(pe_k, 1)

            def score_head(h):
                pe.wait_ge(k_ready, h + 1)
                if h:
                    pe.wait_ge(s_masked, h)
                k = kT[:, h % 2, :]
                mm(ps[:, 1, 0:P], qT[:, h, 0:P], k[:, 0:P], start=True, stop=True)
                mm(ps[:, 1, P:3 * P], qT[:, h, P:2 * P], k[:, 0:2 * P], start=True, stop=True).then_inc(pe_s, 1)

            w_out = [slot[4 + n].rearrange("p (k n) -> p k n", k=KD) for n in range(2)]

            def project(t, n, bank):
                pe.wait_ge(in_wo[n], 16)
                for k in range(KD):
                    if k == KD - 1:
                        pe.wait_ge(y_merged, H)
                        pe.wait_ge(a_merged, H)
                    m = mm(ps[:, bank, :], mT[:, k, P * t:P * t + P], w_out[n][:, k, :],
                           start=(k == 0), stop=(k == KD - 1))
                m.then_inc(pe_wo, 1)

            pe.wait_ge(kT_rope, 2)
            keys(0)
            score_head(0)
            for h in range(H):
                g = h // 4
                if h and h % 4 == 0:
                    pe.wait_ge(s2_masked, g)
                k = kT[:, h % 2, :]
                r = 32 * (h % 4)
                if h % 4 == 0 and g:
                    pe.wait_ge(a2_merged, g)
                mm(ps[r:r + 32, 7, 0:LP], qT[:, h, 2 * P:2 * P + 32], k, start=True, stop=True,
                   ).then_inc(pe_s, 1)
                if h % 2 == 0:
                    pe.wait_ge(in_gab[h // 2], 32)
                if h:
                    pe.wait_ge(gab_exp, h)
                w = slot[h // 2].rearrange("p (k u n) -> p k u n", k=KD, u=2)
                for u in range(2):
                    if u == 1 and h < 6:
                        merge_stage(h)
                    for kk in range(KD):
                        m = mm(ps[:, 4 + u, 0:T], w[:, kk, u, P * (h % 2):P * (h % 2) + P], hT[:, kk, :],
                               start=(kk == 0), stop=(kk == KD - 1))
                m.then_inc(pe_gab, 1)
                if h == 0:
                    pe.wait_ge(pooled_ready, G)
                    pe.wait_ge(p_sample, G + 1)
                    pe.wait_ge(in_pool, 16)
                elif h >= 6:
                    pe.wait_ge(y_merged, h)
                if h < 6:
                    pe.wait_ge(merge_read, h + 1)
                m = mm(ps[:, 6, 0:T], w_pool[:, h // 2, P * (h % 2):P * (h % 2) + P], pooled[:, h // 2, :],
                       start=True, stop=True)
                m.then_inc(pe_y, 1)
                if h + 1 < H:
                    keys(h + 1)
                pe.wait_ge(p_norm, h + 1)
                if h:
                    pe.wait_ge(pT_ready, h)
                E = probs[:, h % 2, :]
                nc.tensor.transpose(ps[:, 2, 0:P], E[:, 0:P], ident)
                nc.tensor.transpose(ps[:, 2, P:2 * P], E[:, P:2 * P], ident)
                nc.tensor.transpose(ps[:, 2, 2 * P:3 * P], E[:, 2 * P:3 * P], ident).then_inc(pe_pT, 1)
                if h + 1 < H:
                    score_head(h + 1)
                pe.wait_ge(pT_ready, h + 1)
                if h:
                    pe.wait_ge(a_merged, h)
                ET = probsT[:, h % 2, :]
                mm(ps[:, 3, 0:2 * P], vals[:, 0, P * h:P * h + P], ET[:, 0:2 * P], start=True, stop=False,
                   skip_group_check=True)
                mm(ps[:, 3, P:2 * P], vals[:, 1, P * h:P * h + P], ET[:, 2 * P:3 * P], start=False, stop=True,
                   skip_group_check=True).then_inc(pe_a, 1)
                if h % 4 == 3:
                    pe.wait_ge(p2_norm, g + 1)
                    pe.wait_ge(pT_ready, h + 1)
                    E2 = probs_last
                    for kb in range(3):
                        n = P if kb < 2 else LAST
                        m = nc.tensor.transpose(ps[0:n, 2, P * kb:P * kb + P], E2[:, P * kb:P * kb + n], ident)
                    m.then_inc(pe_p2T, 1)
                    if h == H - 1:
                        project(0, 0, 0)
                    pe.wait_ge(p2T_ready, 2 * g + 2)
                    for hh in range(4):
                        for kb in range(3):
                            n = P if kb < 2 else LAST
                            m = mm(ps[:, 7, LAST * hh:LAST * hh + LAST],
                                   vals[0:n, kb, P * (4 * g + hh):P * (4 * g + hh) + P],
                                   probs2T[0:n, g, kb, 32 * hh:32 * hh + LAST], start=(kb == 0), stop=(kb == 2))
                    m.then_inc(pe_a2, 1)
                if h % 2:
                    pe.wait_ge(gab_exp, h + 1)
                    pe.sem_inc(slot_free[h // 2], 1)
            project(0, 1, 1)
            pe.wait_ge(a2_merged, 3)
            rows = ROWS[2]
            for k in range(KD):
                for n in range(2):
                    m = mm(ps[32 * n:32 * n + rows, 2, :], mT[:, k, 2 * P:T], w_out[n][:, k, :],
                           start=(k == 0), stop=(k == KD - 1))
            m.then_inc(pe_wo, 1)

            def turn_h2(t, j, banks):
                n = ROWS[t]
                pe.wait_ge(h2_ready, 1 + j)
                for k in range(KD):
                    m = nc.tensor.transpose(ps[:, banks[k // 4], P * (k % 4):P * (k % 4) + n],
                                            h2[0:n, t, P * k:P * k + P], ident[0:n, 0:n])
                    if k % 4 == 3:
                        m.then_inc(pe_h2T, 1)

            def logits(t, j):
                pe.wait_ge(h2T_act, j + 1)
                pe.wait_ge(h2T_dve, j + 1)
                for k in range(KD):
                    m = mm(ps[0:ROWS[t], 7, NE * t:NE * t + NE], hT[:, k, P * t:P * t + ROWS[t]], w_rt[:, k, :],
                           start=(k == 0), stop=(k == KD - 1))
                m.then_inc(pe_logit, 1)

            pe.wait_ge(short_out, 1)
            mm(ps[0:rows, 3, :], ident[32:32 + rows, 32:32 + rows], y_short[32:32 + rows, :], start=True, stop=True
               ).then_inc(pe_wo, 1)
            project(1, 0, 4)
            turn_h2(0, 0, (0, 1))
            turn_h2(2, 1, (2, 3))
            pe.wait_ge(x_mid, 5)
            pe.sem_inc(slot_free[4], 1)
            project(1, 1, 5)
            pe.wait_ge(in_router, 32)
            logits(0, 0)
            logits(2, 1)
            pe.wait_ge(x_mid, 6)
            pe.sem_inc(slot_free[5], 1)
            turn_h2(1, 2, (4, 5))
            logits(1, 2)
            pe.wait_ge(h2T_dve, 3)
            pe.wait_ge(sel_ready, 1)
            for t in range(NT):
                for s in range(t + 1):
                    mm(ps[:, 5, NE * t:NE * t + NE], const["before"] if s == t else ones, sel[:, s, :],
                       start=(s == 0), stop=(s == t))
            for s in range(NT):
                m = mm(ps[0:1, 5, NE * NT:NE * NT + NE], ones[:, 0:1], sel[:, s, :], start=(s == 0), stop=(s == NT - 1))
            m.then_inc(pe_rank, 1)

            pe.sem_inc(pe_comb, 1)

            def gather(count):
                pe.wait_ge(pick_ready, count)
                for k in range(KD):
                    for t in range(NT):
                        n = ROWS[t]
                        m = mm(ps[:, 6 + k // 4, P * (k % 4):P * (k % 4) + P], h2[0:n, t, P * k:P * k + P],
                               pick[0:n, t, :, :].rearrange("p u s -> p (u s)"), start=(t == 0), stop=(t == NT - 1))
                m.then_inc(pe_gather, 1)

            def pair(n, extra, ahead, first=False):
                if extra:
                    pe.wait_ge(y_added, 3 * n + 1)
                    gather(n + 1)
                pe.wait_ge(xg_ready, n + 1)
                pe.wait_ge(pickg_ready, n + 1)
                for t in range(NT):
                    m = nc.tensor.transpose(ps[:, 7, P * t:P * t + P], pickg[:, t, :, :].rearrange("p u s -> p (u s)"),
                                            ident)
                m.then_inc(pe_pick, 1)
                pe.wait_ge(y_added, 3 * n + 2)
                for c in range(4):
                    s0 = 2 * (c % 3)
                    w = []
                    for e in range(2):
                        source = slot[s0 + e]
                        if c in (1, 2):
                            pe.wait_ge(in_chunk[s0 + e], 32 * n + (16 if s0 + e > 2 or first else 0))
                        elif first and c == 3:
                            pe.wait_ge(in_wo[e], 32)
                            source = spare[e]
                        elif first:
                            pe.wait_ge(in_chunk[e], 16)
                        else:
                            pe.wait_ge(in_chunk[e], 32 * n + 16 * (c // 3))
                        w.append(source.rearrange("p (k b n) -> p k b n", k=2, b=4))
                    order = ([(kk, b) for b in (0, 2, 1, 3) for kk in range(2)] if c == 3 else
                             [(kk, b) for kk in range(2) for b in range(4)])
                    for j, (kk, b) in enumerate(order):
                        for e in range(2):
                            m = mm(ps[SL * e:SL * e + SL, b, :], xg[:, 2 * c + kk, SL * e:SL * e + SL],
                                   w[e][:, kk, b, :], start=(c == 0 and kk == 0),
                                   stop=(c == 3 and kk == 1), skip_group_check=True)
                            if j == 7:
                                m.then_inc(slot_free[s0 + e], 1)
                        if c == 3 and j == 3:
                            m.then_inc(pe_gu, 1)
                    if c == 0:
                        pe.wait_ge(in_bias, 32 * n + 32)
                        for b in range(4):
                            row = b_gate if b < 2 else b_up
                            mm(ps[:, b, :], half[1], row[:, 512 * (b % 2):512 * (b % 2) + 512], start=False,
                               stop=False, skip_group_check=True)
                if ahead:
                    pe.wait_ge(pickT_ready, n + 1)
                    pe.wait_ge(y_added, 3 * n + 1)
                    gather(n + 2)
                pe.wait_ge(gate_ready, 2 * n + 2)
                pe.wait_ge(in_b_down, 16 * n + 16)
                for u in range(2):
                    mm(ps[:, u, :], half[2], b_down[:, 512 * u:512 * u + 512], start=True, stop=False,
                       skip_group_check=True)
                pe.wait_ge(y_added, 3 * n + 3)
                for u in range(2):
                    pe.wait_ge(hid_ready, 2 * n + u + 1)
                    for j in range(4):
                        m = nc.tensor.transpose(ps[:, 4 + u, P * j:P * j + P],
                                                hid[:, 512 * u + P * j:512 * u + P * j + P], ident)
                    m.then_inc(pe_hidT, 1)
                for c in range(2):
                    s0 = 2 + 2 * c
                    pe.wait_ge(hidT_act if c == 0 else hidT_dve, n + 1)
                    w = []
                    for e in range(2):
                        source = slot[s0 + e]
                        if s0 + e > 2:
                            pe.wait_ge(in_chunk[s0 + e], 32 * n + 32)
                        elif first:
                            pe.wait_ge(in_p, 32)
                            source = spare[2]
                        else:
                            pe.wait_ge(in_chunk[2], 32 * n + 16)
                        w.append(source.rearrange("p (k u n) -> p k u n", k=4, u=2))
                    order = ([(kk, u) for u in range(2) for kk in range(4)] if c == 1 else
                             [(kk, u) for kk in range(4) for u in range(2)])
                    for j, (kk, u) in enumerate(order):
                        for e in range(2):
                            m = mm(ps[SL * e:SL * e + SL, u, :], hidT[:, 4 * c + kk, SL * e:SL * e + SL],
                                   w[e][:, kk, u, :], start=False, stop=(c == 1 and kk == 3),
                                   skip_group_check=True)
                            if j == 7:
                                m.then_inc(slot_free[s0 + e], 1)
                        if c == 1 and j == 3:
                            m.then_inc(pe_down, 1)
                pe.wait_ge(pickT_ready, n + 1)
                pe.wait_ge(ye_ready, 2 * n + 1)
                pe.wait_ge(hid_ready, 2 * n + 2)
                for t in range(2):
                    mm(ps[:, 2 + 2 * t, :], pickT[:, t, :], ye[:, 0:512], start=True, stop=True)
                pe.wait_ge(ye_ready, 2 * n + 2)
                pe.wait_ge(xg_ready, n + (2 if ahead else 1))
                for u in range(2):
                    m = mm(ps[32 * u:32 * u + 32, 6, :], pickT[:, 2, 0:32], ye[:, 512 * u:512 * u + 512],
                           start=True, stop=True)
                m.then_inc(pe_comb, 1)
                for t in range(2):
                    m = mm(ps[:, 3 + 2 * t, :], pickT[:, t, :], ye[:, 512:D], start=True, stop=True)
                    m.then_inc(pe_comb, 1)

            gather(1)
            pair(0, False, True, first=True)
            with pe.Fori(1, NP - 1) as p:
                pair(p, False, True)
            pair(NP - 1, False, False)
            pe.wait_ge(most_ready, 1)
            count = pe.value_load(most_i[0:1, 0:1], min_val=0, max_val=T)
            with pe.If(count > SL):
                with pe.Fori(0, PASSES - 1) as j:
                    with pe.Fori(0, NP) as p:
                        pair(j * NP + p + NP, True, False)
            pe.wait_ge(y_final, 1)
            for u in range(2):
                m = mm(ps[0:32, u, :], ident[0:64, 32 * u:32 * u + 32], y_last, start=True, stop=True)
            m.then_inc(pe_wo, 1)

        @block.scalar
        def _(act):
            def copy(out, in_):
                return act.activation(out, in_, ACT.Copy)

            for r0, name, n in ((0, "norm1_g", KD), (KD, "pool_scale", KD), (2 * KD, "q_norm_g", CT),
                                (2 * KD + CT, "kv_norm_g", CT)):
                act.dma_start(vrow[r0:r0 + n, :], a[name].rearrange("l (k p) -> (l k) p", p=P)).then_inc(in_vec, 16)
            act.dma_start(pt, a["page_table"].rearrange("(a b) s -> a (b s)", a=1).to_broadcast([P, NB * PAGES])
                          ).then_inc(in_pt, 16)
            act.wait_ge(in_x, 80)
            act.wait_ge(x_zero, 1)
            for t in (0, 2):
                act.activation(xn[0:ROWS[t], t, :], x[0:ROWS[t], t, :], ACT.Square,
                               accum_out=small[0:ROWS[t], t:t + 1]).then_inc(sumsq, 1)
            act.wait_ge(meansq, 1)
            act.activation(small[:, 8:8 + NT], small[:, 4:4 + NT], ACT.Sqrt).then_inc(root, 1)
            act.wait_ge(pe_vec, 1)
            copy(vecT, ps[:, 7, 0:VECS]).then_inc(vec_ready, 1)
            act.wait_ge(vec_ready, 1)
            for k in range(0, KD, 2):
                act.wait_ge(pe_hT, k + 1)
                act.activation(hT[:, k, :], ps[:, k % 4, 0:T], ACT.Copy, scale=vecT[:, k:k + 1]).then_inc(hT_act, 1)
            for j in range(4):
                act.wait_ge(z_copied, j + 1)
                act.activation(zsq[:, j, :], zT[:, j, :], ACT.Square).then_inc(zsq_ready, 1)
            for k in range(CT):
                act.wait_ge(pe_ukT, k + 1)
                copy(w_ukT[:, k, :], ps[:, 3 + k, :]).then_inc(ukT_ready, 1)
            for j in range(2):
                act.wait_ge(meansq, 2 + j)
                act.activation(r_bc[:, j, :], r_bc[:, j, :], ACT.Sqrt).then_inc(root, 1)
            act.wait_ge(pe_hist, 1)
            copy(s_ext[:, :, :, 0:HIST], ps[:, 5, :].rearrange("p (g n) -> p g n", g=G)[:, :, 0:NB * HIST]
                 .rearrange("p g (b t) -> p g b t", b=NB)).then_inc(hist_ready, 1)
            act.wait_ge(pe_kr, 1)
            copy(krT, ps[:, 0, 0:T]).then_inc(kr_ready, 1)
            act.wait_ge(kr_ready, 1)
            for u in range(2):
                copy(kT[NO:P, u, :], krT[NO:P, 0:LP]).then_inc(kT_rope, 1)
            for g in range(G):
                act.wait_ge(pe_p, g + 1)
                copy(p_ext[:, g, 16:16 + LP], ps[:, 6 + g % 2, 0:LP]).then_inc(p_prompt, 1)
            for j in range(6):
                act.wait_ge(pe_v, j + 1)
                rows = P if j < 4 else LAST
                copy(vals[0:rows, j // 2, 512 * (j % 2):512 * (j % 2) + 512], ps[0:rows, 1 + j % 4, :]
                     ).then_inc(v_ready, 1)

            act.wait_ge(prow_ready, 1)
            act.dma_start(o["pool_p"][0, 0, :, :], p_rows).then_inc(out_small, 16)
            act.dma_start(o["pool_s"][0, :, HIST - 1, :], s_rows).then_inc(out_small, 16)
            act.wait_ge(cout_ready, 3)
            for dst, col, n in (("ckv", 0, C), ("krope", C, R)):
                act.dma_start(o[dst + "_p"][0, 0, 0:P, :], c_out[:, 0, col:col + n]).then_inc(out_small, 16)
                act.dma_start(o[dst + "_p"][0, 0, P:2 * P, :], c_out[:, 1, col:col + n]).then_inc(out_small, 16)
                act.dma_start(o[dst + "_p"][0, 0, 2 * P:LP, :], c_out[0:LAST, 2, col:col + n]).then_inc(out_small, 16)
                act.dma_start(o[dst + "_s"][0, :, 0, :], c_out[LAST:LAST + NB, 2, col:col + n]).then_inc(out_small, 16)

            def exponents(b):
                act.wait_ge(s_max, 2 * b + 2)
                act.activation(probs_s, ps[:, 6, :], ACT.Exp, bias=small[:, 12:13], scale=SCALE,
                               accum_out=small[:, 14:15]).then_inc(e_ready, 1)

            def take_probs(b):
                act.wait_ge(pe_pt, b + 1)
                copy(probsT_s, ps[:, 7, :]).then_inc(pt_ready, 1)

            def take_out(b, one):
                act.wait_ge(pv_done, b + 1)
                copy(o_part[:, one, :].rearrange("p b c -> p (b c)"), ps[:, 5, 0:C]).then_inc(o_ready, 1)

            def batch(b, count):
                if count != 0:
                    act.wait_ge(s_done, b)
                    exponents(b - 1)
                for s in range(4):
                    act.wait_ge(pe_kt, 5 * b + (1, 2, 4, 5)[s])
                    copy(keysT[:, 0, 512 * s:512 * s + 512], ps[:, 3 * (s % 2), :]).then_inc(kt_act, 1)
                    if count != 0:
                        if s == 1:
                            take_probs(b - 1)
                        if s == 2:
                            take_out(b - 1, slice(0, 1) if count == 1 else bass.ds(b - 1, 1))

            batch(0, 0)
            batch(1, 1)
            with act.Fori(0, (NB - 2) // NBUF) as i:
                for j in range(NBUF):
                    batch(3 * i + 2 + j, None)
            exponents(NB - 1)
            take_probs(NB - 1)
            take_out(NB - 1, slice(NB - 1, NB))
            for h in range(H):
                if h == 0:
                    act.wait_ge(pe_k, 1)
                    copy(kT[0:NO, 0, :], ps[0:NO, 0, 0:LP]).then_inc(k_ready, 1)
                act.wait_ge(s_masked, h + 1)
                for j, (lo, hi) in enumerate(((0, P), (P, 3 * P))):
                    e = probs[:, h % 2, lo:hi]
                    act.activation(e, e, ACT.Exp, bias=small[:, 20 + j:21 + j], scale=SCALE,
                                   accum_out=small[:, 24 + j:25 + j]).then_inc(p_exp, 1)
                if h % 4 == 3:
                    act.wait_ge(s2_masked, h // 4 + 1)
                    act.activation(probs_last, probs_last, ACT.Exp, bias=small[:, 28:29], scale=SCALE,
                                   accum_out=small[:, 30:31]).then_inc(p2_exp, 1)
                if h == 0:
                    act.wait_ge(merge_in, 2)
                    act.activation(m_w4, m_tmp, ACT.Exp, scale=SCALE).then_inc(merge_act, 1)
                    act.activation(m_wnew, m_diff, ACT.Exp, scale=SCALE).then_inc(merge_act, 1)
                elif h == 2:
                    act.wait_ge(pe_merge, 3)
                    copy(o_rows.rearrange("p g c -> p (g c)"), ps[:, 6, :]).then_inc(merge_read, 1)
                elif h == 4:
                    act.wait_ge(pe_merge, 5)
                    copy(o_rows[:, 0, :], ps[:, 6, 0:2 * P]).then_inc(merge_read, 1)
                act.wait_ge(pe_gab, h + 1)
                if h:
                    act.wait_ge(a_merged, h)
                act.activation(sig[:, :, :], ps[:, 4:6, 0:T], ACT.Exp, scale=-1.0).then_inc(gab_exp, 1)
                if h + 1 < H:
                    act.wait_ge(pe_k, h + 2)
                    copy(kT[0:NO, (h + 1) % 2, :], ps[0:NO, 0, 0:LP]).then_inc(k_ready, 1)
                act.wait_ge(pe_pT, h + 1)
                copy(probsT[:, h % 2, 0:3 * P], ps[:, 2, 0:3 * P]).then_inc(pT_ready, 1)
                if h % 4 == 3:
                    g = h // 4
                    act.wait_ge(pe_p2T, g + 1)
                    copy(probs2T[:, g, 0:2, :], ps[:, 2, 0:2 * P].rearrange("p (k q) -> p k q", k=2)
                         ).then_inc(p2T_ready, 1)
                    copy(probs2T[0:LAST, g, 2, :], ps[0:LAST, 2, 2 * P:3 * P]).then_inc(p2T_ready, 1)
            act.wait_ge(pe_k, H)
            act.dma_start(norm2_g, a["norm2_g"].to_broadcast([P, D])).then_inc(in_g2, 16)
            def take_h2T(t, j, bank):
                act.wait_ge(pe_h2T, 2 * j + 1)
                copy(hT[:, 0:4, P * t:P * t + ROWS[t]],
                     ps[:, bank, :].rearrange("p (k n) -> p k n", k=4)[:, :, 0:ROWS[t]]).then_inc(h2T_act, 1)

            act.wait_ge(pe_wo, 3)
            copy(y_short[32:64, :], ps[32:64, 2, :]).then_inc(short_out, 1)
            for j, (t, bank) in enumerate(((0, 0), (2, 2), (1, 4))):
                n = ROWS[t]
                if j == 2:
                    for i, (tt, bb) in enumerate(((0, 0), (2, 2))):
                        take_h2T(tt, i, bb)
                act.wait_ge(x_mid, (4, 4, 6)[j])
                act.activation(h2[0:n, t, :], x[0:n, t, :], ACT.Square, accum_out=small[0:n, t:t + 1]
                               ).then_inc(sumsq, 1)
                act.wait_ge(meansq, 4 + j)
                act.activation(small[0:n, 8 + t:9 + t], small[0:n, 4 + t:5 + t], ACT.Sqrt).then_inc(root, 1)
            take_h2T(1, 2, 4)
            act.wait_ge(top_ready, 1)
            act.activation(rt[:, 1, :, :], rt[:, 0, :, :], ACT.Exp).then_inc(e_top, 1)

            def take_gathered(count):
                act.wait_ge(pe_gather, count)
                copy(xg, ps[:, 6:8, :].rearrange("p b (k s) -> p (b k) s", k=4)).then_inc(xg_ready, 1)

            def pair(n, extra, ahead):
                if extra:
                    take_gathered(n + 1)
                act.wait_ge(pe_pick, n + 1)
                act.wait_ge(pe_comb, 3 * n + 1)
                copy(pickT, ps[:, 7, 0:NT * P].rearrange("p (t n) -> p t n", t=NT)).then_inc(pickT_ready, 1)
                for u in range(2):
                    half_row = slice(512 * u, 512 * u + 512)
                    act.wait_ge(gate_ready, 2 * n + u + 1)
                    act.activation(sgm[:, half_row], gate[:, half_row], ACT.Sigmoid, scale=ALPHA
                                   ).then_inc(sgm_ready, 1)
                act.wait_ge(pe_hidT, 2 * n + 1)
                copy(hidT[:, 0:4, :], ps[:, 4, :].rearrange("p (j n) -> p j n", j=4)).then_inc(hidT_act, 1)
                if ahead:
                    take_gathered(n + 2)
                for u in range(2):
                    if u == 0:
                        act.wait_ge(pe_down, n + 1)
                    else:
                        act.wait_ge(slot_free[5], 2 * n + 3)
                    copy(ye[:, 512 * u:512 * u + 512], ps[:, u, :]).then_inc(ye_ready, 1)

            act.wait_ge(rank_ready, 1)
            act.wait_ge(out_small, 176)
            take_gathered(1)
            with act.Fori(0, NP - 1) as p:
                pair(p, False, True)
            pair(NP - 1, False, False)
            act.wait_ge(most_ready, 1)
            count = act.value_load(most_i[0:1, 0:1], min_val=0, max_val=T)
            with act.If(count > SL):
                with act.Fori(0, PASSES - 1) as j:
                    with act.Fori(0, NP) as p:
                        pair(j * NP + p + NP, True, False)
            act.wait_ge(y_final, 1)
            act.activation(h2[:, 0, :], x[:, 0, :], ACT.Square, accum_out=small[:, 0:1]).then_inc(sumsq, 1)
            for t in range(NT):
                n = ROWS[t]
                if t == 2:
                    act.wait_ge(y_final, 2)
                    act.activation(h2[0:n, 2, :], x[0:n, 2, :], ACT.Square, accum_out=small[0:n, 2:3]
                                   ).then_inc(sumsq, 1)
                act.wait_ge(meansq, 7 + t)
                act.activation(small[0:n, 8 + t:9 + t], small[0:n, 4 + t:5 + t], ACT.Sqrt).then_inc(root, 1)

        @block.vector
        def _(dve):
            steps = [0]

            def link(ins):
                steps[0] += 1
                ins.then_inc(dve_step, 1)
                dve.wait_ge(dve_step, steps[0])

            link(dve.memset(small, 1.0))
            dve.memset(x[:, 2, :], 0.0).then_inc(x_zero, 1)
            dve.wait_ge(in_x, 80)
            dve.tensor_tensor_reduce(xn[:, 1, :], x[:, 1, :], x[:, 1, :], 1.0, 0.0, ALU.mult, ALU.add,
                                     small[:, 1:2]).then_inc(sumsq, 1)
            dve.wait_ge(sumsq, 3)
            dve.tensor_scalar(small[:, 4:4 + NT], small[:, 0:NT], 1.0 / D, EPS, ALU.mult, ALU.add
                              ).then_inc(meansq, 1)
            dve.wait_ge(root, 1)
            link(dve.reciprocal(small[:, 16:16 + NT], small[:, 8:8 + NT]))
            for t in range(NT):
                n = ROWS[t]
                dve.tensor_scalar(xn[0:n, t, :], x[0:n, t, :], small[0:n, 16 + t:17 + t], None, ALU.mult
                                  ).then_inc(xn_ready, 1)
            dve.wait_ge(in_pt, 16)
            dve.wait_ge(in_const, 16)
            for g in range(4):
                q = slice(32 * g, 32 * g + 32)
                dve.tensor_scalar(idx[q, :], pt[q, g::4], 32.0, const["mod32"][q, :], ALU.mult, ALU.add
                                  ).then_inc(idx_ready, 1)
            dve.wait_ge(vec_ready, 1)
            for k in range(1, KD, 2):
                dve.wait_ge(pe_hT, k + 1)
                dve.tensor_scalar(hT[:, k, :], ps[:, k % 4, 0:T], vecT[:, k:k + 1], None, ALU.mult).then_inc(hT_dve, 1)
            for j in range(4):
                dve.wait_ge(pe_z, j + 1)
                dve.tensor_copy(zT[:, j, :], ps[:, 4 + j, 0:T]).then_inc(z_copied, 1)
            dve.wait_ge(pe_z, 5)
            dve.tensor_tensor(kr_cs[0:2 * R, :], ps[0:2 * R, 0, 0:T], const["rope0"][0:2 * R, :], ALU.mult
                              ).then_inc(kr_rot, 1)
            for j in range(2):
                dve.wait_ge(pe_stat, j + 1)
                dve.tensor_scalar(r_bc[:, j, :], ps[:, 1 + j, 0:T], 1.0 / C, EPS, ALU.mult, ALU.add
                                  ).then_inc(meansq, 1)
            for j in range(2):
                dve.wait_ge(root, 2 + j)
                dve.reciprocal(r_bc[:, j, :], r_bc[:, j, :]).then_inc(r_ready, 1)
            dve.wait_ge(r_ready, 2)
            dve.wait_ge(z_copied, 4)
            link(dve.tensor_tensor(rope_q, const["rope"], r_bc[:, 0, :], ALU.mult))
            for k in range(CT):
                col = 2 * KD + CT + k
                dve.scalar_tensor_tensor(out=cT[:, k, :], in0=zT[:, 2 + k, :], scalar=vecT[:, col:col + 1],
                                         in1=r_bc[:, 1, :], op0=ALU.mult, op1=ALU.mult).then_inc(c_ready, 1)
            for g in range(G):
                dve.wait_ge(p_prompt, g + 1)
                dve.tensor_copy(s_ext[:, g, :, HIST], ps[:, 6 + g % 2, LP:T]).then_inc(p_sample, 1)
            for h in range(H):
                dve.wait_ge(pe_q, h + 1)
                dve.tensor_tensor(qT[:, h, 0:T], ps[:, 1 + h % 4, 0:T], rope_q, ALU.mult).then_inc(q_ready, 1)
            dve.wait_ge(pe_prow, 1)
            link(dve.tensor_copy(p_rows[0:HIST, :], ps[0:HIST, 5, :]))
            dve.tensor_copy(s_rows[0:NB, :], ps[0:NB, 6, :]).then_inc(prow_ready, 1)
            dve.wait_ge(hist_ready, 1)
            dve.wait_ge(p_sample, G)
            for g in range(G):
                w = 2 << g
                link(dve.tensor_reduce(small[:, 32:32 + NB], s_ext[:, g, :, 16 - w:16], AX.X, ALU.add))
                m = dve.scalar_tensor_tensor(out=pooled[:, g, LP:T], in0=small[:, 32:32 + NB], scalar=1.0 / w,
                                             in1=s_ext[:, g, :, HIST], op0=ALU.mult, op1=ALU.subtract)
                if g < G - 1:
                    link(m)
            m.then_inc(p_sample, 1)
            dve.wait_ge(pe_ql, 2)
            dve.wait_ge(zeros_ready, 4)
            for k in range(CT):
                dve.tensor_copy(qL[:, k, :, 0:H], ps[:, 7, k * 64:k * 64 + 64].rearrange("p (h b) -> p b h", h=H)
                                ).then_inc(ql_ready, 1)
            dve.tensor_copy(qR[:, :, 0:H], ps[:, 0, 0:64].rearrange("p (h b) -> p b h", h=H)).then_inc(ql_ready, 1)
            for t in range(NT):
                dve.wait_ge(pe_cout, t + 1)
                dve.tensor_copy(c_out[0:ROWS[t], t, :], ps[0:ROWS[t], 5 + t, 0:C + R]).then_inc(cout_ready, 1)
            dve.wait_ge(ql_ready, 3)

            def maxima(b, one):
                dve.wait_ge(s_done, b + 1)
                dve.tensor_reduce(stats[:, 0, one], ps[:, 6, :], AX.X, ALU.max).then_inc(s_max, 1)
                dve.wait_ge(s_max, 2 * b + 1)
                dve.tensor_scalar(small[:, 12:13], stats[:, 0, one], -SCALE, None, ALU.mult).then_inc(s_max, 1)

            def sums(b, one):
                dve.wait_ge(e_ready, b + 1)
                dve.tensor_copy(stats[:, 1, one], small[:, 14:15]).then_inc(sum_kept, 1)

            def batch(b, u, count):
                one = slice(b, b + 1) if count is not None else bass.ds(b, 1)
                before = slice(0, 1) if count == 1 else bass.ds(b - 1, 1)
                if count != 0:
                    maxima(b - 1, before)
                dve.tensor_copy(qLb[:, u, :, :], qL[:, :, one, :].rearrange("p k b h -> p k (b h)")
                                ).then_inc(q_batch, 1)
                dve.tensor_tensor(qRb[:, u, :, :], qR[:, one, :].to_broadcast([P, 4, 32]),
                                  const["block"].unsqueeze(2).to_broadcast([P, 4, 32]), ALU.mult
                                  ).then_inc(q_batch, 1)
                for s in range(4):
                    dve.wait_ge(pe_kt, 5 * b + (1, 2, 4, 5)[s])
                    dve.tensor_copy(keysT[:, 1, 512 * s:512 * s + 512], ps[:, 3 * (s % 2) + 1, :]).then_inc(kt_dve, 1)
                    if s == 1:
                        dve.wait_ge(pe_kt, 5 * b + 3)
                        dve.tensor_copy(kropeT, ps[:, 2, :]).then_inc(kt_dve, 1)
                        if count != 0:
                            sums(b - 1, before)

            batch(0, 0, 0)
            batch(1, 1, 1)
            with dve.Fori(0, (NB - 2) // NBUF) as i:
                for j in range(NBUF):
                    batch(3 * i + 2 + j, (2 + j) % NBUF, None)
            maxima(NB - 1, slice(NB - 1, NB))
            sums(NB - 1, slice(NB - 1, NB))
            dve.wait_ge(sum_kept, NB)
            dve.wait_ge(pv_done, 6)
            for k in range(CT):
                link(dve.tensor_tensor(qk_new[:, 64 * k:64 * k + 64].rearrange("p (b h) -> p b h", b=NB),
                                       qL[:, k, :, 0:H], cT[:, k, LP:T].unsqueeze(2).to_broadcast([P, NB, H]),
                                       ALU.mult))
            link(dve.memset(m_weights, 0.0))
            link(dve.memset(o_lat, 0.0))
            dve.tensor_tensor(qk_new[0:R, 128:192].rearrange("p (b h) -> p b h", b=NB), qR[0:R, :, 0:H],
                              krT[0:R, LP:T].unsqueeze(2).to_broadcast([R, NB, H]), ALU.mult).then_inc(merge_in, 1)

            def by_slot(row):
                return row.rearrange("p (s h) -> p s h", s=4)[:, :, 0:H]

            def merge_stage(h):
                if h in (0, 1, 3, 5):
                    dve.wait_ge(pe_merge, h + 1)
                if h == 0:
                    link(dve.tensor_tensor(m_tmp[:, 0:64], ps[0:NB, 6, 0:64], const["diag"][0:NB, :], ALU.mult))
                    link(dve.tensor_reduce(m_snew, m_tmp[:, 0:64].rearrange("p (b h) -> p h b", b=NB), AX.X,
                                           ALU.add))
                    mx = by_slot(ps[0:NB, 6, 64:64 + P])
                    link(dve.tensor_reduce(m_top, mx.rearrange("p s h -> p h s"), AX.X, ALU.max))
                    link(dve.tensor_tensor(m_top, m_top, m_snew, ALU.max))
                    link(dve.memset(m_tmp, 0.0))
                    link(dve.tensor_tensor(by_slot(m_tmp), mx, m_top.unsqueeze(1).to_broadcast([NB, 4, H]),
                                           ALU.subtract))
                    dve.tensor_tensor(m_diff, m_snew, m_top, ALU.subtract).then_inc(merge_in, 1)
                elif h == 1:
                    dve.tensor_copy(m_wcol, ps[:, 6, 0:NB]).then_inc(merge_step, 1)
                    dve.wait_ge(merge_step, 1)
                    dve.tensor_tensor(m_weights[:, :, 0:H], const["headsel"].unsqueeze(1).to_broadcast([P, NB, H]),
                                      m_wcol.unsqueeze(2).to_broadcast([P, NB, H]), ALU.mult).then_inc(merge_in, 1)
                    dve.tensor_tensor(qk_new[:, 0:128].rearrange("p (k b h) -> p k b h", k=CT, b=NB),
                                      cT[:, :, LP:T].unsqueeze(3).to_broadcast([P, CT, NB, H]),
                                      ps[:, 6, 8:72].rearrange("p (b h) -> p b h", b=NB).unsqueeze(1)
                                      .to_broadcast([P, CT, NB, H]), ALU.mult).then_inc(merge_read, 1)
                elif h == 3:
                    dve.wait_ge(merge_read, 3)
                    for k in range(CT):
                        m = dve.tensor_tensor(
                            o_lat[:, k, :, 0:NB].rearrange("p h (g j) -> p g j h", g=2),
                            ps[:, 6, :].rearrange("p (g k j h) -> p g k j h", g=2, k=CT, j=4)[:, :, k, :, 0:H],
                            qk_new[:, 64 * k:64 * k + 64].rearrange("p (g j h) -> p g j h", g=2, j=4), ALU.add)
                        m.then_inc(merge_in, 1)
                    dve.wait_ge(merge_in, 6)
                    dve.memset(small[:, 41:42], 0.0).then_inc(merge_read, 1)
                elif h == 5:
                    dve.tensor_copy(aS, ps[:, 6, 0:2 * P].rearrange("p (h b) -> p h b", h=H)[:, :, 0:NB]
                                    ).then_inc(merge_read, 1)

            def merge_weights():
                dve.wait_ge(merge_act, 2)
                dve.tensor_tensor(m_tmp, m_w4, ps[0:NB, 6, 64 + P:64 + 2 * P], ALU.mult).then_inc(merge_read, 1)
                dve.wait_ge(merge_read, 1)
                link(dve.tensor_reduce(m_den, by_slot(m_tmp).rearrange("p s h -> p h s"), AX.X, ALU.add))
                link(dve.tensor_tensor(m_den, m_den, m_wnew, ALU.add))
                link(dve.reciprocal(m_den, m_den))
                link(dve.memset(m_wrow, 0.0))
                link(dve.tensor_tensor(by_slot(m_wrow), by_slot(m_w4), m_den.unsqueeze(1).to_broadcast([NB, 4, H]),
                                       ALU.mult))
                link(dve.tensor_tensor(m_wnew, m_wnew, m_den, ALU.mult))
                dve.tensor_tensor(m_diag.rearrange("p (b h) -> p b h", b=NB),
                                  const["diag"][0:NB, :].rearrange("p (b h) -> p b h", b=NB),
                                  m_wnew.unsqueeze(1).to_broadcast([NB, NB, H]), ALU.mult).then_inc(merge_in, 1)

            dve.wait_ge(out_small, 176)

            for h in range(H):
                E = probs[:, h % 2, :]
                dve.wait_ge(pe_s, 2 * h + 1)
                if h >= 2:
                    dve.wait_ge(pe_pT, h - 1)
                m1 = const["mask1"]
                link(dve.tensor_tensor_reduce(E[:, 0:P], ps[:, 1, 0:P], m1[:, P:2 * P], 1.0, NEG, ALU.add, ALU.max,
                                              small[:, 18:19]))
                link(dve.tensor_tensor_reduce(E[:, P:3 * P], ps[:, 1, P:3 * P], m1, 1.0, NEG, ALU.add, ALU.max,
                                              small[:, 19:20]))
                if h:
                    dve.wait_ge(p_exp, 2 * h)
                dve.tensor_scalar(small[:, 20:22], small[:, 18:20], -SCALE, None, ALU.mult).then_inc(s_masked, 1)
                if h < 6:
                    merge_stage(h)
                dve.wait_ge(p_exp, 2 * h + 2)
                link(dve.reciprocal(small[:, 26:28], small[:, 24:26]))
                link(dve.tensor_scalar(E[:, 0:P], E[:, 0:P], small[:, 26:27], None, ALU.mult))
                dve.tensor_scalar(E[:, P:3 * P], E[:, P:3 * P], small[:, 27:28], None, ALU.mult).then_inc(p_norm, 1)
                if h % 4 == 3:
                    g = h // 4
                    dve.wait_ge(pe_s, 2 * h + 2)
                    link(dve.tensor_tensor_reduce(probs_last, ps[:, 7, 0:LP], const["mask2"], 1.0, NEG, ALU.add,
                                                  ALU.max, small[:, 29:30]))
                    dve.tensor_scalar(small[:, 28:29], small[:, 29:30], -SCALE, None, ALU.mult).then_inc(s2_masked, 1)
                    dve.wait_ge(p2_exp, g + 1)
                    link(dve.reciprocal(small[:, 31:32], small[:, 30:31]))
                    dve.tensor_scalar(probs_last, probs_last, small[:, 31:32], None, ALU.mult).then_inc(p2_norm, 1)
                if h == 0:
                    merge_weights()
                dve.wait_ge(gab_exp, h + 1)
                link(dve.tensor_scalar(sig[:, :, :], sig[:, :, :], 1.0, None, ALU.add))
                link(dve.reciprocal(sig[:, :, :], sig[:, :, :]))
                dve.wait_ge(pe_y, h + 1)
                dve.scalar_tensor_tensor(out=mT[:, h, :], in0=ps[:, 6, 0:T], scalar=vecT[:, KD + h:KD + h + 1],
                                         in1=sig[:, 1, :], op0=ALU.mult, op1=ALU.mult).then_inc(y_merged, 1)
                dve.wait_ge(y_merged, h + 1)
                link(dve.tensor_copy(sga_last[:, h, :], sig[:, 0, 2 * P:T]))
                dve.wait_ge(pe_a, h + 1)
                link(dve.tensor_tensor(sig[:, 0, 0:2 * P], ps[:, 3, 0:2 * P], sig[:, 0, 0:2 * P], ALU.mult))
                dve.tensor_tensor(mT[:, h, 0:2 * P], mT[:, h, 0:2 * P], sig[:, 0, 0:2 * P], ALU.add
                                  ).then_inc(a_merged, 1)
                if h % 4 == 3:
                    g = h // 4
                    last = small2.rearrange("p (h t) -> p h t", h=4)
                    dve.wait_ge(pe_a2, g + 1)
                    link(dve.tensor_tensor(last, ps[:, 7, 0:4 * LAST].rearrange("p (h t) -> p h t", h=4),
                                           sga_last[:, 4 * g:4 * g + 4, 0:LAST], ALU.mult))
                    dve.tensor_tensor(mT[:, 4 * g:4 * g + 4, 2 * P:LP], mT[:, 4 * g:4 * g + 4, 2 * P:LP], last,
                                      ALU.add).then_inc(a2_merged, 1)
                if h == H - 1:
                    dve.wait_ge(a2_merged, 2)
                    one = small2.rearrange("p (h b) -> p h b", h=H)
                    link(dve.tensor_tensor(one, aS, sga_last[:, :, LAST:LAST + NB], ALU.mult))
                    dve.tensor_tensor(mT[:, :, LP:T], mT[:, :, LP:T], one, ALU.add).then_inc(a2_merged, 1)
            dve.wait_ge(out_small, 176)
            link(dve.memset(lg, 0.0))
            link(dve.memset(y_last, 0.0))

            def add_half(t, n, bank, count):
                dve.wait_ge(pe_wo, count)
                xr = x[0:ROWS[t], t, 512 * n:512 * n + 512]
                dve.tensor_tensor(xr, xr, ps[0:ROWS[t], bank, :], ALU.add).then_inc(x_mid, 1)

            def scale_rows(t, j):
                n = ROWS[t]
                dve.wait_ge(sumsq, 4 + j)
                dve.tensor_scalar(small[0:n, 4 + t:5 + t], small[0:n, t:t + 1], 1.0 / D, EPS, ALU.mult, ALU.add
                                  ).then_inc(meansq, 1)
                dve.wait_ge(root, 4 + j)
                link(dve.reciprocal(small[0:n, 16 + t:17 + t], small[0:n, 8 + t:9 + t]))
                dve.scalar_tensor_tensor(out=h2[0:n, t, :], in0=x[0:n, t, :], scalar=small[0:n, 16 + t:17 + t],
                                         in1=norm2_g[0:n, :], op0=ALU.mult, op1=ALU.mult).then_inc(h2_ready, 1)

            def take_h2T(t, j, bank):
                dve.wait_ge(pe_h2T, 2 * j + 2)
                dve.tensor_copy(hT[:, 4:8, P * t:P * t + ROWS[t]],
                                ps[:, bank, :].rearrange("p (k n) -> p k n", k=4)[:, :, 0:ROWS[t]]
                                ).then_inc(h2T_dve, 1)

            add_half(0, 0, 0, 1)
            add_half(0, 1, 1, 2)
            dve.wait_ge(short_out, 1)
            add_half(2, 0, 2, 3)
            add_half(2, 1, 3, 4)
            dve.wait_ge(in_g2, 16)
            dve.wait_ge(x_mid, 4)
            scale_rows(0, 0)
            scale_rows(2, 1)
            add_half(1, 0, 4, 5)
            take_h2T(0, 0, 1)
            take_h2T(2, 1, 3)
            add_half(1, 1, 5, 6)
            dve.wait_ge(x_mid, 6)
            scale_rows(1, 2)
            take_h2T(1, 2, 5)
            dve.wait_ge(pe_logit, NT)
            dve.wait_ge(in_router, 32)
            for t in range(NT):
                n = ROWS[t]
                link(dve.tensor_tensor(lg[0:n, t, :], ps[0:n, 7, NE * t:NE * t + NE], b_rt[0:n, :], ALU.add))
            for t in range(NT):
                link(dve.max(top8[:, t, :], lg[:, t, :]))
            best = top8[:, :, 0:1].to_broadcast([P, NT, NE])
            fourth = top8[:, :, 3:4].to_broadcast([P, NT, NE])
            dve.tensor_tensor(rt[:, 0, :, :], lg, best, ALU.subtract).then_inc(top_ready, 1)
            link(dve.tensor_tensor(rt[:, 2, :, :], lg, fourth, ALU.is_gt))
            link(dve.tensor_tensor(rt[:, 3, :, :], lg, fourth, ALU.is_equal))
            left = small[:, 36:36 + NT]
            link(dve.tensor_reduce(left, rt[:, 2, :, :], AX.X, ALU.add))
            link(dve.tensor_scalar(left, left, -1.0, 4.0, ALU.mult, ALU.add))
            for t in range(NT):
                link(dve.tensor_tensor_scan(sel[:, t, :], rt[:, 3, t, :], rt[:, 3, t, :], 0.0, ALU.add, ALU.max))
            link(dve.tensor_tensor(sel, sel, left.unsqueeze(2).to_broadcast([P, NT, NE]), ALU.is_le))
            link(dve.tensor_tensor(sel, sel, rt[:, 3, :, :], ALU.mult))
            link(dve.tensor_tensor(sel, sel, rt[:, 2, :, :], ALU.add))
            dve.tensor_tensor(sel, sel, const["valid"].unsqueeze(2).to_broadcast([P, NT, NE]), ALU.mult
                              ).then_inc(sel_ready, 1)
            dve.wait_ge(sel_ready, 1)
            dve.wait_ge(e_top, 1)
            link(dve.tensor_tensor(rt[:, 2, :, :], rt[:, 1, :, :], sel, ALU.mult))
            link(dve.tensor_reduce(left, rt[:, 2, :, :], AX.X, ALU.add))
            link(dve.tensor_scalar(left, left, 1.0e-30, None, ALU.max))
            link(dve.reciprocal(left, left))
            link(dve.tensor_tensor(gates, rt[:, 2, :, :], left.unsqueeze(2).to_broadcast([P, NT, NE]),
                                   ALU.mult))
            dve.wait_ge(pe_rank, 1)
            pr = ps[:, 5, 0:NT * NE].rearrange("p (t e) -> p t e", t=NT)
            dve.scalar_tensor_tensor(out=rank, in0=pr, scalar=1.0, in1=sel, op0=ALU.add, op1=ALU.mult
                                     ).then_inc(rank_ready, 1)
            dve.wait_ge(rank_ready, 1)

            def choose(experts, count, first):
                iota = const["iota"][:, first].unsqueeze(1).unsqueeze(1).to_broadcast([P, NT, 2, SL])
                dve.tensor_tensor(pick, iota, rank[:, :, experts].unsqueeze(3).to_broadcast([P, NT, 2, SL]),
                                  ALU.is_equal).then_inc(pick_ready, 1)
                dve.wait_ge(pick_ready, count)
                dve.tensor_tensor(pickg, pick, gates[:, :, experts].unsqueeze(3).to_broadcast([P, NT, 2, SL]),
                                  ALU.mult).then_inc(pickg_ready, 1)

            def pair(p, n, extra, first, ahead):
                if ahead:
                    dve.wait_ge(pe_gather, n + 1)
                    dve.wait_ge(pe_pick, n + 1)
                    choose(bass.ds(2 * p + 2, 2), n + 2, first)
                if extra:
                    choose(bass.ds(2 * p, 2), n + 1, first)
                for u in range(2):
                    at_u = slice(512 * u, 512 * u + 512)
                    if u == 0:
                        dve.wait_ge(pe_gu, n + 1)
                    else:
                        dve.wait_ge(slot_free[1], 2 * n + 3)
                    dve.tensor_scalar(gate[:, at_u], ps[:, u, :], LIMIT, None, ALU.min).then_inc(gate_ready, 1)
                    dve.tensor_scalar(up[:, at_u], ps[:, 2 + u, :], LIMIT, -LIMIT, ALU.min, ALU.max
                                      ).then_inc(up_ready, 1)
                    dve.wait_ge(gate_ready, 2 * n + u + 1)
                    dve.wait_ge(up_ready, 4 * n + 2 * u + 1)
                    dve.scalar_tensor_tensor(out=up[:, at_u], in0=up[:, at_u], scalar=1.0, in1=gate[:, at_u],
                                             op0=ALU.add, op1=ALU.mult).then_inc(up_ready, 1)
                    dve.wait_ge(up_ready, 4 * n + 2 * u + 2)
                    dve.wait_ge(sgm_ready, 2 * n + u + 1)
                    dve.tensor_tensor(hid[:, at_u], up[:, at_u], sgm[:, at_u], ALU.mult).then_inc(hid_ready, 1)
                dve.wait_ge(pe_hidT, 2 * n + 2)
                dve.tensor_copy(hidT[:, 4:8, :], ps[:, 5, :].rearrange("p (j n) -> p j n", j=4)
                                ).then_inc(hidT_dve, 1)
                dve.wait_ge(y_added, 3 * n + 3)
                dve.wait_ge(pe_comb, 3 * n + 2)
                dve.tensor_tensor(y_last, y_last, ps[0:64, 6, :], ALU.add).then_inc(y_added, 1)
                for t in range(2):
                    dve.wait_ge(pe_comb, 3 * n + t + 3)
                    dve.tensor_tensor(x[:, t, :], x[:, t, :],
                                      ps[:, 2 + 2 * t:4 + 2 * t, :].rearrange("p b n -> p (b n)"),
                                      ALU.add).then_inc(y_added, 1)

            dve.sem_inc(y_added, 3)
            choose(slice(0, 2), 1, slice(0, SL))
            link(dve.tensor_reduce(most[0:1, 0:1], ps[0:1, 5, NT * NE:NT * NE + NE], AX.X, ALU.max))
            dve.tensor_copy(most_i[0:1, 0:1], most[0:1, 0:1]).then_inc(most_ready, 1)
            with dve.Fori(0, NP - 1) as p:
                pair(p, p, False, slice(0, SL), True)
            pair(NP - 1, NP - 1, False, slice(0, SL), False)
            dve.wait_ge(y_added, 3 * NP + 3)
            dve.wait_ge(most_ready, 1)
            count = dve.value_load(most_i[0:1, 0:1], min_val=0, max_val=T)
            with dve.If(count > SL):
                with dve.Fori(0, PASSES - 1) as j:
                    with dve.Fori(0, NP) as p:
                        pair(p, j * NP + p + NP, True, bass.ds((j + 1) * SL, SL), False)
                dve.wait_ge(y_added, 3 * NP * PASSES + 3)
            dve.memset(small[:, 40:41], 0.0).then_inc(y_final, 1)
            link(dve.tensor_tensor_reduce(h2[:, 1, :], x[:, 1, :], x[:, 1, :], 1.0, 0.0, ALU.mult, ALU.add,
                                          small[:, 1:2]))

            def mean(t):
                n = ROWS[t]
                if t != 1:
                    dve.wait_ge(sumsq, 7 if t == 0 else 8)
                dve.tensor_scalar(small[0:n, 4 + t:5 + t], small[0:n, t:t + 1], 1.0 / D, EPS, ALU.mult, ALU.add
                                  ).then_inc(meansq, 1)

            def normed(t):
                n = ROWS[t]
                dve.wait_ge(root, 7 + t)
                link(dve.reciprocal(small[0:n, 16 + t:17 + t], small[0:n, 8 + t:9 + t]))
                dve.scalar_tensor_tensor(out=h2[0:n, t, :], in0=x[0:n, t, :], scalar=small[0:n, 16 + t:17 + t],
                                         in1=final_g[0:n, :], op0=ALU.mult, op1=ALU.mult).then_inc(y_final, 1)

            mean(0)
            mean(1)
            dve.wait_ge(pe_wo, 7)
            last = x[0:ROWS[2], 2, :]
            dve.tensor_tensor(last, last, ps[0:ROWS[2], 0:2, :].rearrange("p b n -> p (b n)"), ALU.add
                              ).then_inc(y_final, 1)
            dve.wait_ge(in_final, 16)
            normed(0)
            mean(2)
            normed(1)
            normed(2)


INS = ("x_prompt", "x_sample", "cache_ckv", "cache_krope", "state_pool", "page_table", "meta_tokens", "norm1_g",
       "w_in", "q_norm_g", "w_uq", "kv_norm_g", "w_uk", "w_uv", "w_pool", "pool_scale", "w_out", "norm2_g",
       "w_router", "b_router", "w_gate_up", "b_gate_up", "w_down", "b_down", "final_norm_g")
OUTS = (("y_p", (1, SEQ, D)), ("y_s", (NB, 1, D)), ("ckv_p", (1, 1, LP, C)), ("krope_p", (1, 1, LP, R)),
        ("pool_p", (1, 1, HIST, PW)), ("ckv_s", (1, NB, 1, C)), ("krope_s", (1, NB, 1, R)),
        ("pool_s", (1, NB, HIST, PW)))


def constants():
    import numpy as np
    c = np.zeros((P, NCONST), np.float32)

    def put(name, value):
        start, n = CONST[name]
        c[:, start:start + n] = value

    row = np.arange(P)[:, None]
    pos = np.concatenate([np.arange(LP), np.full(NB, PAST)]).astype(np.float32)
    inv = (np.float32(10000.0) ** (-np.arange(R // 2, dtype=np.float32) / np.float32(R // 2))).astype(np.float32)
    angle = pos[None, :] * inv[:, None]
    cos, sin = np.cos(angle), np.sin(angle)
    put("ident", np.eye(P))
    put("rope", np.concatenate([np.ones((NO, T)), cos, cos, sin, sin]))
    put("rope0", np.concatenate([cos, cos, sin, sin, np.zeros((NO, T))]))
    put("fold", (row % R == np.arange(P) % R) & (row < 2 * R))
    put("fold_hi", (row % R == np.arange(P) % R) & (row >= NO))
    put("half", (row % 32 < 2) & (np.arange(P) // SL == row % 32))
    put("before", row < np.arange(P))
    put("iota", np.arange(PASSES * SL) + 1)
    put("mask1", np.where(np.arange(2 * P) <= P + row, 0.0, NEG))
    put("mask2", np.where(np.arange(LP) <= 2 * P + row % R, 0.0, NEG))
    put("headsel", row % R == np.arange(H))
    put("diag", np.arange(NB * H) // H == row)
    put("invcnt", 1.0 / np.minimum(np.repeat(2 << np.arange(G), 16), np.tile(np.arange(16), G) + 1))
    put("valid", np.arange(NT) * P + row < T)
    put("mod32", row % R)
    put("block", row // R == np.arange(4))
    return c


def kernel(**inputs):
    import numpy as np
    import concourse.bacc as bacc
    from concourse.bass_utils import run_bass_kernel_spmd

    nc = bacc.Bacc("TRN2", target_bir_lowering=False, num_devices=1)
    arrays, a = {}, {}
    for name in INS:
        v = np.ascontiguousarray(inputs[name])
        arrays[f"in_{name}"] = v
        a[name] = nc.dram_tensor(f"in_{name}", v.shape, mybir.dt.from_np(v.dtype), kind="ExternalInput").ap()
    arrays["in_consts"] = constants()
    a["consts"] = nc.dram_tensor("in_consts", (P, NCONST), F32, kind="ExternalInput").ap()
    o = {name: nc.dram_tensor(f"out_{name}", shape, F32, kind="ExternalOutput").ap() for name, shape in OUTS}
    build(nc, a, o)
    r = run_bass_kernel_spmd(nc, [arrays], core_ids=[0]).results[0]
    return tuple(r[f"out_{name}"] for name, _ in OUTS)
```
